# Optimizing a Trainium2 kernel written in Bass

```python
import math
import jax, jax.numpy as jnp
from jax import lax
import numpy as np

D_MODEL = 1024
BATCH = 1
SEQ = 1024
DEPTH = 1

HEAD_DIM = 64
RWKV_DIM = D_MODEL // 2
RWKV_HEADS = RWKV_DIM // HEAD_DIM
ATT_DIM = D_MODEL - RWKV_DIM
ATT_HEADS = ATT_DIM // HEAD_DIM
KV_HEADS = 2
KV_DIM = KV_HEADS * HEAD_DIM
MIX_DIM = RWKV_DIM + ATT_DIM
DECAY_LORA = 64
ICLR_LORA = 64
GATE_LORA = 128
SHIFT_DIM = 3 * RWKV_DIM + DECAY_LORA + ICLR_LORA + GATE_LORA
PROJ_DIM = SHIFT_DIM + ATT_DIM + 2 * KV_DIM
WINDOW = 128
BLOCK = 128
D_FF = 2816
CONV_WIDTH = 3
NORM_EPS = 1e-6
LNX_EPS = 64e-5
L2_EPS = 1e-12
MASK_VALUE = -1e30

kernel_name = "hymba_rwkv7_swa_alibi_convffn_encoder"

def rms_norm(x, g):
    xf = x.astype(jnp.float32)
    y = xf * lax.rsqrt(jnp.mean(xf * xf, axis=-1, keepdims=True) + NORM_EPS)
    return (y * g.astype(jnp.float32)).astype(x.dtype)

def split_cols(p, sizes):
    offsets = [int(o) for o in np.cumsum(sizes)[:-1]]
    return jnp.split(p, offsets, axis=-1)

def token_shift(p, mu_prev, mu_next):
    zero = jnp.zeros_like(p[:, :1])
    prev = jnp.concatenate([zero, p[:, :-1]], axis=1)
    nxt = jnp.concatenate([p[:, 1:], zero], axis=1)
    return p + (prev - p) * mu_prev + (nxt - p) * mu_next

def alibi_slopes(n_heads):
    return jnp.asarray(2.0 ** (-8.0 * np.arange(1, n_heads + 1, dtype=np.float32) / n_heads), jnp.float32)

def rwkv7_bidirectional(r, k, v, wd, ad, gd, decay_w0, decay_w2, iclr_a0, iclr_a2,
                        gate_g2, k_k, k_a, r_k, lnx_g, lnx_b):
    B, T, C = r.shape
    H, N = RWKV_HEADS, HEAD_DIM
    f32 = jnp.float32
    w_log = -jax.nn.softplus(-(decay_w0[:, None, None, :]
                               + jnp.einsum('btr,zrc->zbtc', jnp.tanh(wd), decay_w2))) - 0.5
    decay = jnp.exp(-jnp.exp(w_log.astype(f32))).reshape(2, B, T, H, N)
    a = jax.nn.sigmoid(iclr_a0 + ad @ iclr_a2)
    kk = (k * k_k).reshape(B, T, H, N).astype(f32)
    kk = kk / jnp.maximum(jnp.sqrt(jnp.sum(kk * kk, axis=-1, keepdims=True)), L2_EPS)
    k = k * (1.0 + (a - 1.0) * k_a)
    rh, kh, vh, ah = (t.reshape(B, T, H, N) for t in (r, k, v, a))

    def both_dirs(t):
        t = t.astype(f32)
        return jnp.stack([t, t[:, ::-1]], axis=0).transpose(2, 0, 1, 3, 4)

    dec = jnp.stack([decay[0], decay[1][:, ::-1]], axis=0).transpose(2, 0, 1, 3, 4)
    xs = (both_dirs(rh), dec, both_dirs(kh), both_dirs(vh),
          both_dirs(-kk), both_dirs(kk * ah.astype(f32)))

    def step(S, inp):
        rt, wt, kt, vt, at, bt = inp
        Sa = jnp.einsum('zbhij,zbhj->zbhi', S, at)
        S = S * wt[..., None, :] + Sa[..., :, None] * bt[..., None, :] + vt[..., :, None] * kt[..., None, :]
        return S, jnp.einsum('zbhij,zbhj->zbhi', S, rt)

    S0 = jnp.zeros((2, B, H, N, N), f32)
    _, ys = lax.scan(step, S0, xs)
    y = (ys[:, 0] + ys[::-1, 1]).transpose(1, 0, 2, 3)
    mu = jnp.mean(y, axis=-1, keepdims=True)
    var = jnp.mean(jnp.square(y - mu), axis=-1, keepdims=True)
    y = ((y - mu) * lax.rsqrt(var + LNX_EPS)).reshape(B, T, C)
    y = (y * lnx_g.astype(f32) + lnx_b.astype(f32)).astype(r.dtype)
    bonus = jnp.sum(rh * kh * r_k, axis=-1, keepdims=True) * vh
    g = jax.nn.sigmoid(gd) @ gate_g2
    return (y + bonus.reshape(B, T, C)) * g

def windowed_gqa_alibi(q, k, v, sink):
    B, T, H, D = q.shape
    Hkv = k.shape[2]
    G = H // Hkv
    nb = T // BLOCK
    f32 = jnp.float32
    qb = q.reshape(B, nb, BLOCK, Hkv, G, D)

    def band(t):
        tp = jnp.pad(t, ((0, 0), (WINDOW, WINDOW), (0, 0), (0, 0)))
        return jnp.concatenate([tp[:, o:o + T].reshape(B, nb, BLOCK, Hkv, D)
                                for o in (0, BLOCK, 2 * BLOCK)], axis=2)

    kb, vb = band(k), band(v)
    s = jnp.einsum('bnqhgd,bnkhd->bnhgqk', qb, kb).astype(f32) * (D ** -0.5)
    q_off = jnp.arange(BLOCK)
    k_off = jnp.arange(3 * BLOCK) - BLOCK
    dist = jnp.abs(k_off[None, :] - q_off[:, None])
    key_pos = jnp.arange(nb)[:, None] * BLOCK + k_off[None, :]
    valid = (dist <= WINDOW)[None] & ((key_pos >= 0) & (key_pos < T))[:, None, :]
    slopes = alibi_slopes(H).reshape(Hkv, G)
    s = s - slopes[:, :, None, None] * dist.astype(f32)
    s = jnp.where(valid[None, :, None, None], s, MASK_VALUE)
    sink_col = jnp.broadcast_to(sink.astype(f32).reshape(Hkv, G)[:, :, None, None], s.shape[:-1] + (1,))
    p = jax.nn.softmax(jnp.concatenate([s, sink_col], axis=-1), axis=-1)[..., :-1]
    o = jnp.einsum('bnhgqk,bnkhd->bnqhgd', p.astype(v.dtype), vb)
    return o.reshape(B, T, H * D)

def depthwise_conv_centred(h, w, b):
    C = h.shape[-1]
    y = lax.conv_general_dilated(h, w[:, None, :].astype(h.dtype), window_strides=(1,),
                                 padding=((CONV_WIDTH // 2, CONV_WIDTH // 2),),
                                 dimension_numbers=('NWC', 'WIO', 'NWC'),
                                 feature_group_count=C)
    return y + b

def setup_inputs(seed: int = 0) -> dict:
    key = jax.random.key(seed)
    ks = jax.random.split(key, 24)
    L, D, F = DEPTH, D_MODEL, D_FF
    nrm = lambda k, shape, s: jax.random.normal(k, shape, jnp.float32) * s
    return {
        "x": nrm(ks[0], (BATCH, SEQ, D), 1.0),
        "ln1_g": 1.0 + nrm(ks[1], (L, D), 0.02),
        "w_in": nrm(ks[2], (L, D, PROJ_DIM), D ** -0.5),
        "shift_mu_prev": jax.random.uniform(ks[3], (L, SHIFT_DIM), jnp.float32, 0.0, 0.5),
        "shift_mu_next": jax.random.uniform(ks[4], (L, SHIFT_DIM), jnp.float32, 0.0, 0.5),
        "decay_w0": jax.random.uniform(ks[5], (L, 2, RWKV_DIM), jnp.float32, -6.0, -1.0),
        "decay_w2": nrm(ks[6], (L, 2, DECAY_LORA, RWKV_DIM), 0.5 * DECAY_LORA ** -0.5),
        "iclr_a0": nrm(ks[7], (L, RWKV_DIM), 0.1),
        "iclr_a2": nrm(ks[8], (L, ICLR_LORA, RWKV_DIM), 0.5 * ICLR_LORA ** -0.5),
        "gate_g2": nrm(ks[9], (L, GATE_LORA, RWKV_DIM), GATE_LORA ** -0.5),
        "k_k": 0.85 + nrm(ks[10], (L, RWKV_DIM), 0.05),
        "k_a": 1.0 + nrm(ks[11], (L, RWKV_DIM), 0.05),
        "r_k": nrm(ks[12], (L, RWKV_HEADS, HEAD_DIM), 0.1),
        "lnx_g": 1.0 + nrm(ks[13], (L, RWKV_DIM), 0.02),
        "lnx_b": nrm(ks[14], (L, RWKV_DIM), 0.02),
        "attn_sink": nrm(ks[15], (L, ATT_HEADS), 1.0),
        "w_out": nrm(ks[16], (L, MIX_DIM, D), MIX_DIM ** -0.5),
        "ln2_g": 1.0 + nrm(ks[17], (L, D), 0.02),
        "ffn_w_gate": nrm(ks[18], (L, D, F), D ** -0.5),
        "ffn_w_up": nrm(ks[19], (L, D, F), D ** -0.5),
        "ffn_conv_w": nrm(ks[20], (L, CONV_WIDTH, F), CONV_WIDTH ** -0.5),
        "ffn_conv_b": nrm(ks[21], (L, F), 0.02),
        "ffn_w_down": nrm(ks[22], (L, F, D), F ** -0.5),
        "lnf_g": 1.0 + nrm(ks[23], (D,), 0.02),
    }

def reference(x, ln1_g, w_in, shift_mu_prev, shift_mu_next, decay_w0, decay_w2, iclr_a0,
              iclr_a2, gate_g2, k_k, k_a, r_k, lnx_g, lnx_b, attn_sink, w_out, ln2_g,
              ffn_w_gate, ffn_w_up, ffn_conv_w, ffn_conv_b, ffn_w_down, lnf_g):
    B, T, _ = x.shape
    for l in range(DEPTH):
        h = rms_norm(x, ln1_g[l])
        p = h @ w_in[l]
        p_rwkv = token_shift(p[..., :SHIFT_DIM], shift_mu_prev[l], shift_mu_next[l])
        r, k, v, wd, ad, gd = split_cols(p_rwkv, [RWKV_DIM, RWKV_DIM, RWKV_DIM,
                                                  DECAY_LORA, ICLR_LORA, GATE_LORA])
        q, ka, va = split_cols(p[..., SHIFT_DIM:], [ATT_DIM, KV_DIM, KV_DIM])
        o_rwkv = rwkv7_bidirectional(r, k, v, wd, ad, gd, decay_w0[l], decay_w2[l],
                                     iclr_a0[l], iclr_a2[l], gate_g2[l], k_k[l], k_a[l],
                                     r_k[l], lnx_g[l], lnx_b[l])
        o_att = windowed_gqa_alibi(q.reshape(B, T, ATT_HEADS, HEAD_DIM),
                                   ka.reshape(B, T, KV_HEADS, HEAD_DIM),
                                   va.reshape(B, T, KV_HEADS, HEAD_DIM), attn_sink[l])
        x = x + jnp.concatenate([o_rwkv, o_att], axis=-1) @ w_out[l]
        h = rms_norm(x, ln2_g[l])
        gate = depthwise_conv_centred(h @ ffn_w_gate[l], ffn_conv_w[l], ffn_conv_b[l])
        x = x + (jax.nn.gelu(gate, approximate=False) * (h @ ffn_w_up[l])) @ ffn_w_down[l]
    return rms_norm(x, lnf_g)


_drawn_inputs = setup_inputs


def setup_inputs(seed=0):
    import zlib

    import numpy as np

    out = dict(_drawn_inputs(seed))
    spreads = {}
    factors = {'ln1_g': 3.418,
     'decay_w2': 6.188,
     'iclr_a0': 3.711,
     'lnx_g': 20.733,
     'lnx_b': 22.071,
     'attn_sink': 42.792,
     'ln2_g': 3.813,
     'ffn_conv_b': 5.299,
     'lnf_g': 8.435}
    for name, (base, spread) in spreads.items():
        noise = np.random.default_rng([zlib.crc32(name.encode()), seed]).standard_normal(out[name].shape)
        drawn = base * np.exp(spread * noise) if base else spread * noise
        out[name] = __import__('jax').numpy.asarray(drawn.astype(out[name].dtype))
    for name, factor in factors.items():
        out[name] = (out[name] * factor).astype(out[name].dtype)
    return out
```

```python
import math
from contextlib import ExitStack

import numpy as np

import concourse.bass as bass
from concourse import mybir

F32 = mybir.dt.float32
ALU = mybir.AluOpType
ACT = mybir.ActivationFunctionType
AX = mybir.AxisListType

P = 128
T = 1024
D = 1024
HD = 64
KD = D // P
RW = 512
NPAIR = RW // P
NT = T // P
C = 32
NC = T // C
CP = C + 1
TP = NC * CP
F = 2816
KF = F // P
AH = 8
GH = 4
BAND = 3 * P
DECAY = math.exp(-0.5)
NORM_EPS = 1e-6
LNX_EPS = 64e-5
L2_EPS = 1e-12
FREE = 1
HALF = 512

COLS = {}
_n = 0
for _name, _w in (("mu_prev", 14), ("mu_next", 14), ("w0", 8), ("a0", 4), ("k_k", 4), ("k_a", 4), ("r_k", 4),
                  ("lnx_g", 4), ("lnx_b", 4), ("ln1", 8), ("ln2", 8), ("lnf", 8),
                  ("cw0", 22), ("cw1", 22), ("cw2", 22), ("cb", 22)):
    COLS[_name] = _n
    _n += _w
NPAR = _n


def hymba_block(nc, a):
    with ExitStack() as ctx:
        def sb(name, shape):
            return ctx.enter_context(nc.sbuf_tensor(name, shape, F32))

        def sem(name):
            return ctx.enter_context(nc.semaphore(name))

        def dram(name, shape):
            return nc.dram_tensor(name, shape, F32, kind="Internal").ap()

        AR_d = dram("AR_d", (2, NPAIR, P, NC * 2 * C))
        G_d = dram("G_d", (2, NPAIR, P, NC * 2 * C))
        BK_d = dram("BK_d", (2, NPAIR, P, NC * HD))
        TI_d = dram("TI_d", (2, NPAIR, 2, C, NC * C))
        v_d = dram("v_d", (T, RW))
        y_d = dram("y_d", (2, T, RW))
        q_d = dram("q_d", (4, P, T))
        kk_d = dram("kk_d", (2, P, T + 2 * P))
        va_d = dram("va_d", (T + 2 * P, P))

        par = sb("par", [P, NPAR])
        c0 = sb("c0", [P, 14])
        oka = sb("oka", [P, NPAIR])
        ident = sb("ident", [P, P])
        pairones = sb("pairones", [P, P])
        ones = sb("ones", [P, P])
        gmask = sb("gmask", [P, 2, 2 * C])
        eps = sb("eps", [P, 2])
        sink = sb("sink", [P, AH])
        slope = sb("slope", [P, AH])
        PC = sb("PC", [P, 2, NPAIR, NC])
        xT = sb("xT", [P, KD, T])
        hT = sb("hT", [P, KD, T])
        oT = hT
        bonusT = sb("bonusT", [P, NPAIR, T])
        sgT = sb("sgT", [P, T])
        WORK = 30300
        work = sb("work", [P, WORK])

        class Carve:
            def __init__(self, at=0):
                self.at = at

            def __call__(self, *shape):
                n = int(np.prod(shape))
                v = work[:, self.at:self.at + n]
                self.at += n
                assert self.at <= WORK, self.at
                if len(shape) == 1:
                    return v
                names = "abcd"[:len(shape)]
                return v.rearrange(f"p ({' '.join(names)}) -> p {' '.join(names)}",
                                   **{x: s for x, s in zip(names[1:], shape[1:])})

        banks = ctx.enter_context(nc.psum_tensor("banks", [P, 8, HALF], F32))
        flat = banks[:, :, :].rearrange("p b n -> p (b n)")
        ps = [flat[:, 2 * s * HALF:2 * (s + 1) * HALF] for s in range(4)]

        def col(name, m, n=1):
            return par[:, bass.ds(m + COLS[name], n)]

        acc, rs = bonusT[:, 0, :], bonusT[:, 1, :]
        sqb = [bonusT[:, 2, :], bonusT[:, 3, :]]

        w = Carve()
        W3 = [w(KD, P) for _ in range(3)]
        lora = w(T)
        lw = w(2 * P)
        rT, kT, vT = w(T), w(T), w(T)
        kkT, bT, aT, tpT, sqT = w(T), w(T), w(T), w(T), w(T)
        L = [w(TP) for _ in range(2)]
        E = [w(TP) for _ in range(2)]
        Ei = [w(TP) for _ in range(2)]
        reset = w(2, TP)
        AR, BK = w(NC, 2, C), w(NC, 2, C)
        G, BKt = w(NC, 2 * C), w(NC // 2, P)
        vts = w(NT, P)
        assert w.at <= WORK

        w = Carve(3 * KD * P)
        M = [w(2, C, C) for _ in range(2)]
        TI = [w(2, C, C) for _ in range(2)]
        prod = w(2, C, C)
        qst = [w(T) for _ in range(2)]
        zero = w(P)
        vast = w(NT, P)

        w = Carve()
        ARs = [w(2, NPAIR, 2 * 2 * C) for _ in range(2)]
        Gs = [w(2, NPAIR, 2 * 2 * C) for _ in range(2)]
        BKs = [w(2, NPAIR, 2 * HD) for _ in range(2)]
        TIs = [w(2, NPAIR, 2 * C) for _ in range(2)]
        UV = [w(2, 2, NPAIR, HD) for _ in range(2)]
        S = w(2, NPAIR, HD)
        St = w(2, NPAIR, HD)
        Xs = w(2, NPAIR * HD)
        Ys = [w(2, NPAIR * HD) for _ in range(2)]
        qs = [w(4, P) for _ in range(2)]
        ks = [w(2, BAND) for _ in range(2)]
        vs = [w(3, P) for _ in range(2)]
        nd = [w(BAND) for _ in range(2)]
        Lg = w(GH, BAND)
        Pr = w(GH, BAND)
        PT = w(3, 2, 2, P)
        mx, nm, es, rsum, rinv = w(GH), w(GH), w(GH), w(GH), w(GH)

        w = Carve()
        yin = [w(2, RW) for _ in range(2)]
        ysum, ycen, ysq = w(RW), w(RW), w(RW)
        stat = w(4, AH)
        yn = w(NT, RW)
        gw = w(RW)
        ot1 = w(T)

        w = Carve()
        W2 = [w(KD, P) for _ in range(2)]

        w = Carve()
        actT = w(KF, T)
        Wgu = [sb_ for sb_ in (w(2, KD, P), bonusT[:, 0:2, :].rearrange("p a b -> p (a b)").rearrange(
            "p (g k n) -> p g k n", g=2, k=KD))]
        ga = [w(T), bonusT[:, 2, :]]
        hflat = hT[:, :, :].rearrange("p a b -> p (a b)")
        Wd = [hflat[:, s * KF * P:(s + 1) * KF * P].rearrange("p (k n) -> p k n", k=KF) for s in range(2)]

        names = """consts_loaded x_loaded consts_made
            p_mm p_scaled p_shift1 p_shifted lora_tanh gate_sig lw_full
            dz0_mm dz1_mm ic_mm sig0 sig1 a_ready kk_ready kk_sq ss_mm nrm_ready nrm_max nrm_rec nk_ready b_ready
            ka_fac kp_ready bon_in bon_mm bon_out vt_mm vts_ready v_stored
            L0_ready L1_ready E0_ready E1_ready
            ab_ready k_prod gram_mm G_half G_ready bkt_mm bkt_half bkt_ready AR_stored G_stored BK_stored PC_saved
            pad_zero
            qkv_mm qkv_evicted q_stored q_stored2 z_stored c0_part vat_mm vat_evicted zero_made
            M_loaded TI_init sol_prod sol_row TI_stored
            X0_mm X1_mm X0_out X1_out U0_mm U1_mm U00 U01 U10 U11 Y0_mm Y1_mm S0_mm S1_mm Y0_out Y1_out
            S0_add S1_add S0_new S1_new
            sc_mm sc_out mx_red mx_sink nm_ready p_exp s_exp sum_all inv_ready p_norm pt_mm pt_out o_mm o_out
            y_summed y_mean y_cent y_sq y_var y_sd y_inv y_normed yt_mm gt_mm y_aff y_bon y_gated gw_loaded
            out_stored""".split()
        s = {n: sem(n) for n in names}
        w_full = [sem(f"w_full{i}") for i in range(3)]
        scan_full = [sem(f"scan_full{i}") for i in range(2)]
        att_full = [sem(f"att_full{i}") for i in range(2)]
        y_full = [sem(f"y_full{i}") for i in range(2)]
        pe_passed = sem("pe_passed")
        yin_used = [sem(f"yin_used{i}") for i in range(2)]
        ys_stored = [sem(f"ys_stored{i}") for i in range(2)]
        sz = [{k: s[v] for k, v in dict(X_mm=f"X{z}_mm", X_out=f"X{z}_out", U_mm=f"U{z}_mm", U_e0=f"U{z}0",
                                        U_e1=f"U{z}1", Y_mm=f"Y{z}_mm", S_mm=f"S{z}_mm", Y_out=f"Y{z}_out",
                                        S_add=f"S{z}_add", S_new=f"S{z}_new").items()} for z in range(2)]

        ns = {k: sem(f"norm_{k}") for k in ("squared", "summed", "ms_mm", "root", "rstd", "scaled")}

        def slot_sems(tag, keys):
            return {k: [sem(f"{tag}_{k}{i}") for i in range(2)] for k in keys}

        so = slot_sems("lin", ("full", "mm", "added"))
        sg = slot_sems("gu", ("full", "done"))
        sg.update({k: sem(f"gu_{k}") for k in ("g_mm", "u_mm", "scaled", "c1", "c2", "gelu")})

        NCONST = 8
        start_at_one = [s[n] for n in """p_mm ic_mm bkt_ready G_ready pt_out o_out gram_mm v_stored BK_stored
            AR_stored G_stored pt_mm o_mm bkt_mm p_exp s_exp y_normed""".split()]
        start_at_one += ys_stored + so["added"] + sg["done"] + [sz[z][n] for z in range(2) for n in ("Y_out", "S_add")]
        block = ctx.enter_context(nc.Block())

        def chunked(x, z, excl):
            v = x.rearrange("p (c t) -> p c t", t=CP)
            first = (0 if excl else 1) if z == 0 else (1 if excl else 0)
            return v[:, :, first:first + C]

        @block.sync
        def _(sp):
            for x in start_at_one:
                sp.sem_inc(x, FREE)
            for dst, src in ((par[:, :], a["par"]), (ident[:, :], a["ident"]), (pairones[:, :], a["pairones"]),
                             (gmask[:, :, :], a["gmask"]), (reset, a["reset"]), (sink[:, :], a["sink"]),
                             (slope[:, :], a["slope"]), (ones[:, :], a["ones"])):
                sp.dma_start(dst, src).then_inc(s["consts_loaded"], 16)
            for k in range(0, KD, 2):
                sp.dma_start(xT[:, k, :], a["xT"][:, k, :]).then_inc(s["x_loaded"], 16)
            for i in range(2):
                sp.dma_start(W3[i], a["w_in"][i]).then_inc(w_full[i], 16)
            sp.dma_start(W3[2], a["w_in"][4]).then_inc(w_full[2], 16)
            for i in range(2):
                sp.wait_ge(s["p_mm"], i + 1 + FREE)
                sp.dma_start(W3[i], a["w_in"][2 + i]).then_inc(w_full[i], 16)
            with sp.Fori(0, NPAIR) as j:
                pair = bass.ds(j, 1)
                sp.wait_ge(s["ic_mm"], j + FREE)
                sp.dma_start(lw, a["lora_w"][pair].rearrange("o p n -> (o p) n")).then_inc(s["lw_full"], 16)
                for i in range(3):
                    sp.wait_ge(s["p_mm"], 3 * j + 3 + i + FREE)
                    sp.dma_start(W3[i], a["w_in"][bass.ds(3 * j + (5 + i), 1)].rearrange("o p k n -> (o p) k n"))\
                      .then_inc(w_full[i], 16)
                sp.wait_ge(s["vts_ready"], j + 1)
                sp.dma_start(v_d.rearrange("(b p) n -> p b n", p=P)[:, :, bass.ds(j * P, P)], vts)\
                  .then_inc(s["v_stored"], 16)
                for z in range(2):
                    sp.wait_ge(s["ab_ready"], 2 * j + z + 1)
                    sp.dma_start(AR_d[z][pair].rearrange("o p n -> (o p) n"), AR.rearrange("p c a t -> p (c a t)"))\
                      .then_inc(s["AR_stored"], 16)
                    sp.wait_ge(s["G_ready"], 2 * j + z + 1 + FREE)
                    sp.dma_start(G_d[z][pair].rearrange("o p n -> (o p) n"), G.rearrange("p c t -> p (c t)"))\
                      .then_inc(s["G_stored"], 16)
                    sp.wait_ge(s["bkt_ready"], 2 * j + z + 1 + FREE)
                    for odd in range(2):
                        for e in range(2):
                            dst = BK_d[z][pair, 64 * e:64 * e + 64].rearrange("o p (c q n) -> (o p) c q n", q=2, n=HD)
                            sp.dma_start(dst[:, :, odd, :], BKt[64 * odd:64 * odd + 64, :, HD * e:HD * e + HD])\
                              .then_inc(s["BK_stored"], 16)
            for i in range(3, 6):
                sp.wait_ge(s["qkv_mm"], i - 2)
                sp.dma_start(W3[i % 3], a["w_in"][14 + i]).then_inc(w_full[i % 3], 16)
            sp.wait_ge(s["G_stored"], 16 * 2 * NPAIR + FREE)
            sp.wait_ge(s["BK_stored"], 16 * 8 * NPAIR + FREE)
            sp.wait_ge(s["AR_stored"], 16 * 2 * NPAIR + FREE)
            sp.wait_ge(s["v_stored"], 16 * NPAIR + FREE)
            for z in range(2):
                for j in range(NPAIR):
                    for e in range(2):
                        src = G_d[z, j, 64 * e:64 * e + C].rearrange("s (c x) -> c s x", x=2 * C)[:, :, 0:C]
                        sp.dma_start(M[z][C * j:C * (j + 1), e, :, :], src).then_inc(s["M_loaded"], 16)
            sp.wait_ge(s["TI_stored"], 16 * 4 * NPAIR)
            sp.wait_ge(s["q_stored"], 16 * 10)
            sp.wait_ge(s["q_stored2"], 32)
            sp.wait_ge(s["z_stored"], 16 * 6)
            v_rows = v_d.rearrange("(c t) (j e i) -> c e t j i", t=C, j=NPAIR, e=2)

            def load_scan(i, slot):
                for z in range(2):
                    c = (4 * i + 2 * slot) if z == 0 else (i * -4 + (NC - 2 - 2 * slot))
                    for dst, src, n in ((ARs, AR_d, 2 * C), (Gs, G_d, 2 * C), (BKs, BK_d, HD)):
                        sp.dma_start(dst[slot][:, z], src[z].rearrange("j p n -> p j n")[:, :, bass.ds(c * n, 2 * n)])\
                          .then_inc(scan_full[slot], 16)
                    for e in range(2):
                        sp.dma_start(TIs[slot][64 * e:64 * e + C, z],
                                     TI_d[z, :, e].rearrange("j s n -> s j n")[:, :, bass.ds(c * C, 2 * C)])\
                          .then_inc(scan_full[slot], 16)
                        for cc in range(2):
                            sp.dma_start(UV[slot][64 * e + C:64 * e + 2 * C, z, cc],
                                         v_rows[bass.ds(c + cc, 1), e].rearrange("o t j i -> (o t) j i"))\
                              .then_inc(scan_full[slot], 16)

            def load_att(i, slot):
                n = (2 * i + slot) * P
                sp.dma_start(qs[slot], q_d.rearrange("j p t -> p j t")[:, :, bass.ds(n, P)]).then_inc(att_full[slot], 16)
                sp.dma_start(ks[slot], kk_d.rearrange("g p t -> p g t")[:, :, bass.ds(n, BAND)])\
                  .then_inc(att_full[slot], 16)
                sp.dma_start(vs[slot], va_d.rearrange("(b p) n -> p b n", p=P)[:, bass.ds(2 * i + slot, 3), :])\
                  .then_inc(att_full[slot], 16)
                sp.dma_start(nd[slot], a["negdist"][bass.ds(2 * i + slot, 1)].rearrange("o p n -> (o p) n"))\
                  .then_inc(att_full[slot], 16)

            for slot in range(2):
                load_scan(0, slot)
                load_att(0, slot)
            y_rows = y_d.rearrange("z (c t) (j e i) -> z c e t j i", t=C, j=NPAIR, e=2)

            def store_y(i, q):
                for z in range(2):
                    c = 4 * i + q if z == 0 else i * -4 + (NC - 1 - q)
                    sp.wait_ge(sz[z]["Y_out"], 4 * i + q + 1 + FREE)
                    for e in range(2):
                        sp.dma_start(y_rows[z, bass.ds(c, 1), e].rearrange("o t j i -> (o t) j i"),
                                     Ys[q % 2][64 * e + C:64 * e + 2 * C, z].rearrange("p (j i) -> p j i", j=NPAIR))\
                          .then_inc(ys_stored[q % 2], 16)

            with sp.Fori(0, NC // 4 - 1) as i:
                for slot in range(2):
                    store_y(i, 2 * slot)
                    store_y(i, 2 * slot + 1)
                    for z in range(2):
                        sp.wait_ge(sz[z]["Y_mm"], 4 * i + 2 * slot + 2)
                        sp.wait_ge(sz[z]["S_mm"], 4 * i + 2 * slot + 2)
                    load_scan(i + 1, slot)
            for q in range(4):
                store_y(NC // 4 - 1, q)
            with sp.Fori(0, NT // 2 - 1) as i:
                for slot in range(2):
                    sp.wait_ge(s["o_mm"], 4 * i + 2 * slot + 2 + FREE)
                    load_att(i + 1, slot)
            for b in range(2):
                sp.wait_ge(ys_stored[b], 64 * NC // 2 + FREE)
            sp.wait_ge(s["o_out"], 2 * NT + FREE)
            sp.dma_start(gw, a["gate_w"]).then_inc(s["gw_loaded"], 16)
            for slot in range(2):
                sp.dma_start(yin[slot], y_d[:, slot * P:(slot + 1) * P].rearrange("z p n -> p z n"))\
                  .then_inc(y_full[slot], 16)
            with sp.Fori(0, NT // 2 - 1) as i:
                for slot in range(2):
                    sp.wait_ge(yin_used[slot], i + 1)
                    sp.dma_start(yin[slot], y_d[:, bass.ds((2 * i + 2 + slot) * P, P)].rearrange("z p n -> p z n"))\
                      .then_inc(y_full[slot], 16)
            sp.wait_ge(s["y_gated"], NPAIR)
            for slot in range(2):
                sp.dma_start(W2[slot], a["w_out"][slot]).then_inc(so["full"][slot], 16)
            with sp.Fori(0, KD // 2 - 1) as i:
                for slot in range(2):
                    sp.wait_ge(so["mm"][slot], i + 1)
                    sp.dma_start(W2[slot], a["w_out"][bass.ds(2 * i + 2 + slot, 1)].rearrange("o p k n -> (o p) k n"))\
                      .then_inc(so["full"][slot], 16)
            for slot in range(2):
                sp.wait_ge(so["mm"][slot], KD // 2)
            sp.wait_ge(s["y_gated"], NPAIR)
            sp.wait_ge(ns["scaled"], 2 * KD)
            for slot in range(2):
                sp.dma_start(Wgu[slot], a["w_gu"][slot]).then_inc(sg["full"][slot], 16)
            with sp.Fori(0, KF // 2 - 1) as i:
                for slot in range(2):
                    sp.wait_ge(sg["u_mm"], 2 * i + slot + 1)
                    sp.dma_start(Wgu[slot], a["w_gu"][bass.ds(2 * i + 2 + slot, 1)]
                                 .rearrange("o p g k n -> (o p) g k n")).then_inc(sg["full"][slot], 16)
            sp.wait_ge(sg["u_mm"], KF)
            for slot in range(2):
                sp.dma_start(Wd[slot], a["w_down"][slot]).then_inc(so["full"][slot], 16)
            with sp.Fori(0, KD // 2 - 1) as i:
                for slot in range(2):
                    sp.wait_ge(so["mm"][slot], KD // 2 + i + 1)
                    sp.dma_start(Wd[slot], a["w_down"][bass.ds(2 * i + 2 + slot, 1)]
                                 .rearrange("o p k n -> (o p) k n")).then_inc(so["full"][slot], 16)
            for k in range(KD):
                sp.wait_ge(ns["scaled"], 2 * KD + k + 1)
                sp.dma_start(a["out"][:, k, :], hT[:, k, :]).then_inc(s["out_stored"], 16)
            sp.wait_ge(s["out_stored"], 16 * KD)

        @block.tensor
        def _(pe):
            def dense(out, wt, src, kn, done):
                for k in range(kn):
                    for h in range(2):
                        mm = pe.matmul(out[:, h * HALF:(h + 1) * HALF], wt[:, k, :],
                                       src[:, k, h * HALF:(h + 1) * HALF], start=(k == 0), stop=(k == kn - 1))
                mm.then_inc(done, 1)

            def whole(out, wt, src, done, rows=slice(0, P)):
                for h in range(2):
                    mm = pe.matmul(out[:, h * HALF:(h + 1) * HALF], wt, src[rows, h * HALF:(h + 1) * HALF],
                                   start=True, stop=True)
                mm.then_inc(done, 1)

            def settled():
                pe.sem_inc(pe_passed, 1)

            def norm(n, ac):
                pe.wait_ge(ns["summed"], (n + 1) * (KD - 1))
                whole(ps[0], ones[:, :], ac, ns["ms_mm"])

            pe.wait_ge(s["consts_loaded"], 16 * NCONST)
            norm(0, acc)
            pe.wait_ge(ns["root"], 1)
            pe.wait_ge(ns["scaled"], KD)
            for i in range(2):
                pe.wait_ge(w_full[i], 16)
                dense(ps[i], W3[i], hT, KD, s["p_mm"])
            pe.wait_ge(s["p_shifted"], 2)
            pe.wait_ge(s["lora_tanh"], 1)
            with pe.Fori(0, NPAIR) as j:
                pe.wait_ge(s["bkt_ready"], 2 * j + FREE)
                pe.wait_ge(s["G_ready"], 2 * j + FREE)
                for i in range(3):
                    pe.wait_ge(w_full[i], 16 * j + (32 if i < 2 else 16))
                    dense(ps[i], W3[i], hT, KD, s["p_mm"])
                pe.wait_ge(s["lw_full"], 16 * j + 16)
                whole(ps[3], lw[0:64, 0:P], lora, s["dz0_mm"], slice(0, 64))
                pe.wait_ge(s["p_shifted"], 3 * j + 3)
                whole(ps[0], lw[0:64, P:2 * P], lora, s["dz1_mm"], slice(0, 64))
                pe.wait_ge(s["p_shifted"], 3 * j + 4)
                whole(ps[1], lw[64:128, 0:P], lora, s["ic_mm"], slice(64, P))
                pe.wait_ge(s["p_shifted"], 3 * j + 5)
                for n in range(NT):
                    mm = pe.transpose(ps[2][:, n * P:(n + 1) * P], vT[:, n * P:(n + 1) * P], ident[:, :])
                mm.then_inc(s["vt_mm"], 1)
                pe.wait_ge(s["kk_sq"], j + 1)
                pe.wait_ge(s["sig0"], j + 1)
                whole(ps[3], pairones[:, :], sqT, s["ss_mm"])
                pe.wait_ge(s["bon_in"], j + 1)
                pe.wait_ge(s["sig1"], j + 1)
                whole(ps[0], pairones[:, :], tpT, s["bon_mm"])
                for z in range(2):
                    pe.wait_ge(s["ab_ready"], 2 * j + z + 1)
                    pe.wait_ge(s["k_prod"], 2 * j + z + 1)
                    if z == 0:
                        pe.wait_ge(s["a_ready"], j + 1)
                        pe.wait_ge(s["vts_ready"], j + 1)
                    else:
                        pe.wait_ge(s["G_ready"], 2 * j + 1 + FREE)
                    settled()
                    for c in range(NC):
                        for e in range(2):
                            h = slice(64 * e, 64 * e + 64)
                            out = ps[1 + c // 16][h, (c % 16) * 64:(c % 16) * 64 + 64]
                            mm = pe.matmul(out, BK[h, c].rearrange("p a b -> p (a b)"),
                                           AR[h, c].rearrange("p a b -> p (a b)"), start=True, stop=True)
                    mm.then_inc(s["gram_mm"], 1)
                    if z == 0:
                        pe.wait_ge(s["nrm_ready"], j + 1)
                        pe.wait_ge(s["bon_out"], j + 1)
                    else:
                        pe.wait_ge(s["bkt_ready"], 2 * j + 1 + FREE)
                    for c in range(NC // 2):
                        out = ps[(3, 0)[c // 8]][:, (c % 8) * P:(c % 8 + 1) * P]
                        mm = pe.transpose(out, BK[:, 2 * c:2 * c + 2].rearrange("p c a b -> p (c a b)"), ident[:, :])
                    mm.then_inc(s["bkt_mm"], 1)
            for i in range(6):
                if i == 0:
                    pe.wait_ge(s["bkt_ready"], 2 * NPAIR + FREE)
                    pe.wait_ge(s["G_ready"], 2 * NPAIR + FREE)
                if i >= 4:
                    pe.wait_ge(s["qkv_evicted"], i - 3)
                pe.wait_ge(w_full[i % 3], 16 * (NPAIR + 1 + i // 3 + (1 if i % 3 < 2 else 0)))
                dense(ps[i % 4], W3[i % 3], hT, KD, s["qkv_mm"])
            pe.wait_ge(s["qkv_evicted"], 6)
            for n in range(NT):
                mm = pe.transpose(ps[2][:, n * P:(n + 1) * P], qst[1][:, n * P:(n + 1) * P], ident[:, :])
            mm.then_inc(s["vat_mm"], 1)
            pe.wait_ge(s["vat_evicted"], 1)
            pe.wait_ge(s["sol_row"], 2 * (C - 1))
            XY = [banks[:, z, 0:NPAIR * HD] for z in range(2)]
            US = [banks[:, 2 + z, :] for z in range(2)]
            with pe.Fori(0, NC // 4) as i:
                for q in range(4):
                    slot, cc = q // 2, q % 2
                    n = 4 * i + q
                    if cc == 0:
                        pe.wait_ge(scan_full[slot], 16 * 18 * i + 16 * 18)
                    for z in range(2):
                        c2 = cc if z == 0 else 1 - cc
                        pe.wait_ge(sz[z]["Y_out"], n + FREE)
                        for part in range(2):
                            if part == 1:
                                pe.wait_ge(sz[z]["S_new"], n + 1)
                                settled()
                            for j in range(NPAIR):
                                for e in range(2):
                                    h = slice(64 * e, 64 * e + 64)
                                    hk = slice(64 * e + C, 64 * e + 2 * C)
                                    out = XY[z][h, j * HD:(j + 1) * HD]
                                    if part == 0:
                                        mm = pe.matmul(out, Gs[slot][hk, z, j, c2 * 64:c2 * 64 + 64],
                                                       UV[slot][hk, z, c2, j, :], start=(j == 0), stop=False,
                                                       skip_group_check=True)
                                    else:
                                        mm = pe.matmul(out, ARs[slot][h, z, j, c2 * 64:c2 * 64 + 64],
                                                       S[h, z, j, :], start=False, stop=(j == NPAIR - 1),
                                                       skip_group_check=True)
                        mm.then_inc(sz[z]["X_mm"], 1)
                    for z in range(2):
                        c2 = cc if z == 0 else 1 - cc
                        pe.wait_ge(sz[z]["X_out"], n + 1)
                        pe.wait_ge(sz[z]["S_add"], n + FREE)
                        settled()
                        for j in range(NPAIR):
                            for e in range(2):
                                hu = slice(64 * e, 64 * e + C)
                                mm = pe.matmul(US[z][hu, j * HD:(j + 1) * HD], TIs[slot][hu, z, j, c2 * C:c2 * C + C],
                                               Xs[hu, z, j * HD:(j + 1) * HD], start=True, stop=True)
                        mm.then_inc(sz[z]["U_mm"], 1)
                    for z in range(2):
                        c2 = cc if z == 0 else 1 - cc
                        pe.wait_ge(sz[z]["U_e0"], n + 1)
                        pe.wait_ge(sz[z]["U_e1"], n + 1)
                        settled()
                        for j in range(NPAIR):
                            for e in range(2):
                                h = slice(64 * e, 64 * e + 64)
                                mm = pe.matmul(US[z][h, 256 + j * HD:256 + (j + 1) * HD],
                                               BKs[slot][h, z, j, c2 * HD:c2 * HD + HD], UV[slot][h, z, c2, j, :],
                                               start=True, stop=True)
                        mm.then_inc(sz[z]["S_mm"], 1)
                        for j in range(NPAIR):
                            for e in range(2):
                                hu = slice(64 * e, 64 * e + C)
                                mm = pe.matmul(XY[z][64 * e + C:64 * e + 2 * C, j * HD:(j + 1) * HD],
                                               Gs[slot][hu, z, j, c2 * 64 + C:c2 * 64 + 2 * C],
                                               UV[slot][hu, z, c2, j, :], start=False, stop=True,
                                               skip_group_check=True)
                        mm.then_inc(sz[z]["Y_mm"], 1)
            with pe.Fori(0, NT // 2) as i:
                for slot in range(2):
                    pe.wait_ge(att_full[slot], 64 * i + 64)
                    for g in range(2):
                        blk = 4 * i + 2 * slot + g
                        for h in range(GH):
                            e, hh = h % 2, h // 2
                            if h < 2:
                                pe.wait_ge(s["pt_out"], 3 * blk + FREE)
                            else:
                                pe.wait_ge(s["sc_out"], 4 * blk + h - 1)
                            mm = pe.matmul(banks[:, 4 + h % 2, 0:BAND],
                                           qs[slot][64 * e:64 * e + 64, 2 * g + hh, :],
                                           ks[slot][64 * e:64 * e + 64, g, :], start=True, stop=True)
                            mm.then_inc(s["sc_mm"], 1)
                        pe.wait_ge(s["p_norm"], blk + 1)
                        for kb in range(3):
                            for h in range(GH):
                                e, hh = h % 2, h // 2
                                mm = pe.transpose(banks[:, 4 + kb, (2 * e + hh) * P:(2 * e + hh + 1) * P],
                                                  Pr[:, h, kb * P:(kb + 1) * P], ident[:, :])
                            mm.then_inc(s["pt_mm"], 1)
                        pe.wait_ge(s["pt_out"], 3 * blk + 3 + FREE)
                        pe.wait_ge(s["o_out"], blk + FREE)
                        for e in range(2):
                            for kb in range(3):
                                mm = pe.matmul(banks[64 * e:64 * e + 64, 7, 0:2 * P], vs[slot][:, kb, HD * g:HD * g + HD],
                                               PT[:, kb, e].rearrange("p a b -> p (a b)"), start=(kb == 0),
                                               stop=(kb == 2))
                        mm.then_inc(s["o_mm"], 1)
            pe.wait_ge(s["y_normed"], NT + FREE)
            pe.wait_ge(s["gw_loaded"], 16)
            pe.wait_ge(s["o_out"], 2 * NT + FREE)
            for z in range(2):
                pe.wait_ge(sz[z]["Y_out"], NC + FREE)
                pe.wait_ge(sz[z]["S_add"], NC + FREE)
            for j in range(NPAIR):
                if j >= 2:
                    pe.wait_ge(s["y_gated"], j - 1)
                a0, a1 = ps[2 * (j % 2)], ps[2 * (j % 2) + 1]
                for n in range(NT):
                    mm = pe.transpose(a0[:, n * P:(n + 1) * P], yn[:, n, j * P:(j + 1) * P], ident[:, :])
                mm.then_inc(s["yt_mm"], 1)
                whole(a1, gw[:, j * P:(j + 1) * P], sgT, s["gt_mm"])
            pe.wait_ge(s["y_gated"], NPAIR)
            with pe.Fori(0, KD // 2) as i:
                for slot in range(2):
                    pe.wait_ge(so["full"][slot], 16 * i + 16)
                    pe.wait_ge(so["added"][slot], i + FREE)
                    dense(ps[slot], W2[slot], oT, KD, so["mm"][slot])
            for slot in range(2):
                pe.wait_ge(so["added"][slot], KD // 2 + FREE)
            norm(1, acc)
            pe.wait_ge(ns["root"], 2)
            pe.wait_ge(ns["scaled"], 2 * KD)
            with pe.Fori(0, KF // 2) as i:
                for slot in range(2):
                    pe.wait_ge(sg["full"][slot], 16 * i + 16)
                    pe.wait_ge(sg["done"][slot], i + FREE)
                    dense(ps[2 * slot], Wgu[slot][:, 0], hT, KD, sg["g_mm"])
                    dense(ps[2 * slot + 1], Wgu[slot][:, 1], hT, KD, sg["u_mm"])
            for slot in range(2):
                pe.wait_ge(sg["done"][slot], KF // 2 + FREE)
            with pe.Fori(0, KD // 2) as i:
                for slot in range(2):
                    pe.wait_ge(so["full"][slot], 16 * (KD // 2) + 16 * i + 16)
                    pe.wait_ge(so["added"][slot], KD // 2 + i + FREE)
                    dense(ps[slot], Wd[slot], actT, KF, so["mm"][slot])
            for slot in range(2):
                pe.wait_ge(so["added"][slot], KD + FREE)
            norm(2, hT[:, 7, :])

        @block.scalar
        def _(act):
            for k in range(1, KD, 2):
                act.dma_start(xT[:, k, :], a["xT"][:, k, :]).then_inc(s["x_loaded"], 16)

            def norm(n, ac, sq, root):
                for k in range(KD):
                    if k >= 3:
                        act.wait_ge(ns["summed"], n * (KD - 1) + k - 2)
                    act.activation(ac if k == 0 else sq[k % 2], xT[:, k, :], ACT.Square).then_inc(ns["squared"], 1)
                act.wait_ge(ns["ms_mm"], n + 1)
                act.activation(root, ps[0], ACT.Sqrt, bias=eps[:, 0:1], scale=1.0 / D).then_inc(ns["root"], 1)

            act.wait_ge(s["x_loaded"], 16 * KD)
            act.wait_ge(s["consts_made"], 4)
            norm(0, acc, sqb, rs)
            for i, dst in enumerate((lora, sgT[:, :])):
                act.wait_ge(s["p_mm"], i + 1 + FREE)
                act.activation(dst, ps[i], ACT.Copy, scale=c0[:, 12 + i:13 + i]).then_inc(s["p_scaled"], 1)
            act.wait_ge(s["p_shifted"], 1)
            act.activation(lora[0:64, :], lora[0:64, :], ACT.Tanh).then_inc(s["lora_tanh"], 1)
            act.wait_ge(s["p_shifted"], 2)
            act.activation(sgT[:, :], sgT[:, :], ACT.Sigmoid).then_inc(s["gate_sig"], 1)
            with act.Fori(0, NPAIR) as j:
                act.wait_ge(s["gram_mm"], 2 * j + FREE)
                act.wait_ge(s["G_ready"], 2 * j + FREE)
                for i, dst in enumerate((rT, kT, vT)):
                    act.wait_ge(s["p_mm"], 3 * j + 3 + i + FREE)
                    act.activation(dst, ps[i], ACT.Copy, scale=c0[:, bass.ds(j + 4 * i, 1)])\
                       .then_inc(s["p_scaled"], 1)
                act.wait_ge(s["pad_zero"], 2)
                for z, slot in ((0, 3), (1, 0)):
                    act.wait_ge(s[f"dz{z}_mm"], j + 1)
                    act.activation(chunked(L[z], z, False), ps[slot].rearrange("p (c t) -> p c t", t=C), ACT.Sigmoid,
                                   bias=col("w0", j + 4 * z)).then_inc(s[f"sig{z}"], 1)
                act.wait_ge(s["ic_mm"], j + 1 + FREE)
                act.activation(aT, ps[1], ACT.Sigmoid, bias=col("a0", j)).then_inc(s["a_ready"], 1)
                act.wait_ge(s["vt_mm"], j + 1)
                act.wait_ge(s["v_stored"], 16 * j + FREE)
                act.activation(vts.rearrange("p a b -> p (a b)"), ps[2], ACT.Copy).then_inc(s["vts_ready"], 1)
                act.wait_ge(s["kk_ready"], j + 1)
                act.activation(sqT, kkT, ACT.Square).then_inc(s["kk_sq"], 1)
                for z in range(2):
                    act.wait_ge(s[f"L{z}_ready"], j + 1)
                    act.activation(E[z], L[z], ACT.Exp, scale=-DECAY).then_inc(s[f"E{z}_ready"], 1)
                    act.activation(Ei[z], L[z], ACT.Exp, scale=DECAY).then_inc(s[f"E{z}_ready"], 1)
                act.wait_ge(s["ss_mm"], j + 1)
                act.activation(sqT, ps[3], ACT.Sqrt).then_inc(s["nrm_ready"], 1)
                for z in range(2):
                    act.wait_ge(s["bkt_mm"], 2 * j + z + 1 + FREE)
                    act.wait_ge(s["BK_stored"], 128 * j + 64 * z + FREE)
                    act.activation(BKt[:, 0:8].rearrange("p a b -> p (a b)"), ps[3], ACT.Copy).then_inc(s["bkt_half"], 1)
                    act.activation(BKt[:, 8:16].rearrange("p a b -> p (a b)"), ps[0], ACT.Copy)\
                       .then_inc(s["bkt_ready"], 1)
            act.wait_ge(s["BK_stored"], 16 * 8 * NPAIR + FREE)
            act.wait_ge(s["AR_stored"], 16 * 2 * NPAIR + FREE)
            act.wait_ge(s["G_stored"], 16 * 2 * NPAIR + FREE)
            act.wait_ge(s["v_stored"], 16 * NPAIR + FREE)
            for i in range(6):
                act.wait_ge(s["qkv_mm"], i + 1)
                if i >= 2:
                    act.wait_ge(s[("q_stored", "q_stored2")[i % 2]], 16 * (i // 2))
                act.activation(qst[i % 2], ps[i % 4], ACT.Copy, scale=(HD ** -0.5 if i < 4 else 1.0))\
                   .then_inc(s["qkv_evicted"], 1)
                act.wait_ge(s["qkv_evicted"], i + 1)
                if i < 4:
                    act.dma_start(q_d[i], qst[i % 2]).then_inc(s[("q_stored", "q_stored2")[i % 2]], 16)
                elif i == 4:
                    for g in range(2):
                        for e in range(2):
                            act.dma_start(kk_d[g, 64 * e:64 * e + 64, P:P + T], qst[0][64 * g:64 * g + 64, :])\
                               .then_inc(s["q_stored"], 16)
            act.wait_ge(s["vat_mm"], 1)
            act.activation(vast.rearrange("p a b -> p (a b)"), ps[2], ACT.Copy).then_inc(s["vat_evicted"], 1)
            act.wait_ge(s["vat_evicted"], 1)
            for n in range(4):
                act.dma_start(va_d[(1 + 2 * n) * P:(3 + 2 * n) * P].rearrange("(b p) n -> p b n", p=P),
                              vast[:, 2 * n:2 * n + 2]).then_inc(s["q_stored"], 16)
            act.wait_ge(s["q_stored"], 16 * 10)
            act.wait_ge(s["q_stored2"], 32)
            act.wait_ge(s["TI_stored"], 16 * 4 * NPAIR)
            with act.Fori(0, NC // 4) as i:
                for q in range(4):
                    slot, cc = q // 2, q % 2
                    n = 4 * i + q
                    act.wait_ge(sz[1]["X_mm"], n + 1)
                    act.activation(Xs[:, 1], banks[:, 1, 0:256], ACT.Copy).then_inc(sz[1]["X_out"], 1)
                    for z in range(2):
                        c2 = cc if z == 0 else 1 - cc
                        act.wait_ge(sz[z]["U_mm"], n + 1)
                        act.activation(UV[slot][64:64 + C, z, c2].rearrange("p a b -> p (a b)"),
                                       banks[64:64 + C, 2 + z, 0:256], ACT.Copy).then_inc(sz[z]["U_e1"], 1)
                    for z in range(2):
                        act.wait_ge(sz[z]["Y_mm"], n + 1)
                        if z == 0:
                            act.wait_ge(ys_stored[q % 2], 64 * (2 * i + q // 2) + FREE)
                        act.activation(Ys[q % 2][:, z], banks[:, z, 0:256], ACT.Copy).then_inc(sz[z]["Y_out"], 1)
            with act.Fori(0, NT // 2) as i:
                for slot in range(2):
                    for g in range(2):
                        blk = 4 * i + 2 * slot + g
                        act.wait_ge(s["nm_ready"], blk + 1)
                        act.wait_ge(s["pt_mm"], 3 * blk + FREE)
                        for h in range(GH):
                            act.activation(Pr[:, h, :], Lg[:, h, :], ACT.Exp, bias=nm[:, h:h + 1],
                                           accum_out=rsum[:, h:h + 1]).then_inc(s["p_exp"], 1)
                        act.wait_ge(s["mx_sink"], 2 * blk + 2)
                        act.activation(es, mx, ACT.Exp).then_inc(s["s_exp"], 1)
                        act.wait_ge(s["o_mm"], blk + FREE)
                        for kb in range(3):
                            act.wait_ge(s["pt_mm"], 3 * blk + kb + 1 + FREE)
                            act.activation(PT[:, kb].rearrange("p a b c -> p (a b c)"), banks[:, 4 + kb, :], ACT.Copy)\
                               .then_inc(s["pt_out"], 1)
                        act.wait_ge(s["o_mm"], blk + 1 + FREE)
                        act.activation(oT[:, NPAIR + 2 * g:NPAIR + 2 * g + 2, bass.ds((2 * i + slot) * P, P)],
                                       banks[:, 7, 0:2 * P].rearrange("p (a b) -> p a b", a=2), ACT.Copy)\
                           .then_inc(s["o_out"], 1)
            with act.Fori(0, NT) as t:
                act.wait_ge(s["y_cent"], t + 1)
                act.activation(ysq, ycen, ACT.Square).then_inc(s["y_sq"], 1)
                act.wait_ge(s["y_var"], t + 1)
                act.activation(stat[:, 2], stat[:, 1], ACT.Sqrt, bias=eps[:, 1:2], scale=1.0 / HD).then_inc(s["y_sd"], 1)
            for slot in range(2):
                act.wait_ge(so["added"][slot], KD // 2 + FREE)
            norm(1, acc, sqb, rs)
            act.wait_ge(ns["scaled"], 2 * KD)
            with act.Fori(0, KF // 2) as i:
                for slot in range(2):
                    act.wait_ge(sg["g_mm"], 2 * i + slot + 1)
                    act.wait_ge(sg["done"][slot], i + FREE)
                    act.activation(ga[slot], ps[2 * slot], ACT.Identity, bias=col("cb", 2 * i + slot),
                                   scale=col("cw1", 2 * i + slot)).then_inc(sg["scaled"], 1)
                    act.wait_ge(sg["c2"], 2 * i + slot + 1)
                    act.activation(ga[slot], ga[slot], ACT.Gelu).then_inc(sg["gelu"], 1)
            for slot in range(2):
                act.wait_ge(so["added"][slot], KD + FREE)
            norm(2, hT[:, 7, :], (hT[:, 5, :], hT[:, 6, :]), work[:, 0:T])

        @block.gpsimd
        def _(pool):
            for z in range(2):
                v = L[z].rearrange("p (c t) -> p c t", t=CP)
                pool.wait_ge(ns["scaled"], KD)
                pool.memset(v[:, :, 0:1] if z == 0 else v[:, :, C:C + 1], 0.0).then_inc(s["pad_zero"], 1)

            with pool.Fori(0, NPAIR) as j:
                for z in range(2):
                    pool.wait_ge(s["kp_ready"], j + 1)
                    pool.wait_ge(s[f"E{z}_ready"], 2 * j + 2)
                    pool.wait_ge(s["bkt_mm"], 2 * j + z + FREE)
                    pool.tensor_tensor(BK[:, :, 1, :], kT.rearrange("p (c t) -> p c t", t=C), chunked(Ei[z], z, False),
                                       ALU.mult).then_inc(s["k_prod"], 1)
            pool.wait_ge(s["BK_stored"], 16 * 8 * NPAIR + FREE)
            pool.wait_ge(s["v_stored"], 16 * NPAIR + FREE)
            pool.wait_ge(s["G_stored"], 16 * 2 * NPAIR + FREE)
            pool.memset(zero, 0.0).then_inc(s["zero_made"], 1)
            pool.wait_ge(s["zero_made"], 1)
            for at in (0, P + T):
                for g in range(2):
                    pool.dma_start(kk_d[g, :, at:at + P], zero).then_inc(s["z_stored"], 16)
                pool.dma_start(va_d[at:at + P, :], zero).then_inc(s["z_stored"], 16)
            for z in range(2):
                pool.wait_ge(s["sol_row"], (z + 1) * (C - 1))
                for j in range(NPAIR):
                    for e in range(2):
                        pool.dma_start(TI_d[z, j, e].rearrange("s (c t) -> c s t", t=C), TI[z][C * j:C * (j + 1), e])\
                            .then_inc(s["TI_stored"], 16)

        @block.vector
        def _(dve):
            tt, ts, stt = dve.tensor_tensor, dve.tensor_scalar, dve.scalar_tensor_tensor

            def norm(n, ac, sq, root, gain):
                for k in range(1, KD):
                    dve.wait_ge(ns["squared"], n * KD + k + 1)
                    if k >= 2:
                        dve.wait_ge(ns["summed"], n * (KD - 1) + k - 1)
                    tt(ac, ac, sq[k % 2], ALU.add).then_inc(ns["summed"], 1)
                dve.wait_ge(ns["root"], n + 1)
                dve.reciprocal(root, root).then_inc(ns["rstd"], 1)
                dve.wait_ge(ns["rstd"], n + 1)
                for k in range(KD):
                    stt(hT[:, k, :], xT[:, k, :], col(gain, k), root, ALU.mult, ALU.mult).then_inc(ns["scaled"], 1)

            dve.memset(eps[:, 0:1], NORM_EPS).then_inc(s["consts_made"], 1)
            dve.memset(eps[:, 1:2], LNX_EPS).then_inc(s["consts_made"], 1)
            dve.wait_ge(s["consts_loaded"], 16 * NCONST)
            mp, mn = par[:, COLS["mu_prev"]:COLS["mu_prev"] + 14], par[:, COLS["mu_next"]:COLS["mu_next"] + 14]
            ts(c0[:, :], mp, -1.0, 1.0, ALU.mult, ALU.add).then_inc(s["c0_part"], 1)
            dve.wait_ge(s["c0_part"], 1)
            tt(c0[:, :], c0[:, :], mn, ALU.subtract).then_inc(s["consts_made"], 1)
            ka = par[:, COLS["k_a"]:COLS["k_a"] + NPAIR]
            ts(oka[:, :], ka, -1.0, 1.0, ALU.mult, ALU.add).then_inc(s["consts_made"], 1)
            norm(0, acc, sqb, rs, "ln1")

            for i, dst in enumerate((lora, sgT[:, :])):
                dve.wait_ge(s["p_scaled"], i + 1)
                stt(dst[:, 1:T], ps[i][:, 0:T - 1], col("mu_prev", 12 + i), dst[:, 1:T], ALU.mult, ALU.add)\
                    .then_inc(s["p_shift1"], 1)
                dve.wait_ge(s["p_shift1"], i + 1)
                stt(dst[:, 0:T - 1], ps[i][:, 1:T], col("mu_next", 12 + i), dst[:, 0:T - 1], ALU.mult, ALU.add)\
                    .then_inc(s["p_shifted"], 1)

            with dve.Fori(0, NPAIR) as j:
                for i, dst in enumerate((rT, kT, vT)):
                    dve.wait_ge(s["p_scaled"], 3 * j + 3 + i)
                    stt(dst[:, 1:T], ps[i][:, 0:T - 1], col("mu_prev", j + 4 * i), dst[:, 1:T], ALU.mult, ALU.add)\
                        .then_inc(s["p_shift1"], 1)
                    dve.wait_ge(s["p_shift1"], 3 * j + 3 + i)
                    stt(dst[:, 0:T - 1], ps[i][:, 1:T], col("mu_next", j + 4 * i), dst[:, 0:T - 1], ALU.mult, ALU.add)\
                        .then_inc(s["p_shifted"], 1)
                dve.wait_ge(s["p_shifted"], 3 * j + 4)
                ts(kkT, kT, col("k_k", j), None, ALU.mult).then_inc(s["kk_ready"], 1)
                for z in range(2):
                    dve.wait_ge(s[f"sig{z}"], j + 1)
                    order = slice(None) if z == 0 else slice(None, None, -1)
                    dve.tensor_tensor_scan(L[z][:, order], reset[:, z, order], L[z][:, order], 0.0, ALU.mult, ALU.add)\
                        .then_inc(s[f"L{z}_ready"], 1)
                dve.wait_ge(s["a_ready"], j + 1)
                dve.wait_ge(s["kk_ready"], j + 1)
                ts(tpT, aT, col("k_a", j), oka[:, bass.ds(j, 1)], ALU.mult, ALU.add).then_inc(s["ka_fac"], 1)
                dve.wait_ge(s["ka_fac"], j + 1)
                tt(kT, kT, tpT, ALU.mult).then_inc(s["kp_ready"], 1)
                dve.wait_ge(s["kp_ready"], j + 1)
                dve.wait_ge(s["p_shifted"], 3 * j + 3)
                stt(tpT, rT, col("r_k", j), kT, ALU.mult, ALU.mult).then_inc(s["bon_in"], 1)
                dve.wait_ge(s["nrm_ready"], j + 1)
                ts(sqT, sqT, L2_EPS, None, ALU.max).then_inc(s["nrm_max"], 1)
                dve.wait_ge(s["nrm_max"], j + 1)
                dve.reciprocal(sqT, sqT).then_inc(s["nrm_rec"], 1)
                dve.wait_ge(s["nrm_rec"], j + 1)
                stt(kkT, kkT, -1.0, sqT, ALU.mult, ALU.mult).then_inc(s["nk_ready"], 1)
                dve.wait_ge(s["nk_ready"], j + 1)
                stt(bT, kkT, -1.0, aT, ALU.mult, ALU.mult).then_inc(s["b_ready"], 1)
                dve.wait_ge(s["p_shifted"], 3 * j + 5)
                dve.wait_ge(s["bon_mm"], j + 1)
                tt(bonusT[:, bass.ds(j, 1), :].rearrange("p o t -> p (o t)"), ps[0], vT, ALU.mult)\
                    .then_inc(s["bon_out"], 1)
                dve.wait_ge(s["b_ready"], j + 1)
                for z in range(2):
                    dve.wait_ge(s[f"E{z}_ready"], 2 * j + 2)
                    last = E[z].rearrange("p (c t) -> p c t", t=CP)[:, :, (C if z == 0 else 0)]
                    dve.tensor_copy(PC[:, z, bass.ds(j, 1), :].rearrange("p o c -> p (o c)"), last)
                    if z == 0:
                        dve.wait_ge(s["AR_stored"], 32 * j + FREE)
                    else:
                        dve.wait_ge(s["AR_stored"], 32 * j + 16 + FREE)
                    dve.wait_ge(s["bkt_mm"], 2 * j + z + FREE)
                    by_chunk = lambda x: x.rearrange("p (c t) -> p c t", t=C)
                    tt(AR[:, :, 0, :], by_chunk(kkT), chunked(E[z], z, True), ALU.mult)
                    tt(AR[:, :, 1, :], by_chunk(rT), chunked(E[z], z, False), ALU.mult)
                    tt(BK[:, :, 0, :], by_chunk(bT), chunked(Ei[z], z, False), ALU.mult).then_inc(s["ab_ready"], 1)
                    dve.wait_ge(s["gram_mm"], 2 * j + z + 1 + FREE)
                    dve.wait_ge(s["G_stored"], 32 * j + 16 * z + FREE)
                    for b in range(2):
                        tt(G[:, 16 * b:16 * b + 16, :], ps[1 + b].rearrange("p (c t) -> p c t", t=2 * C),
                           gmask[:, z, :].unsqueeze(1).broadcast_to([P, 16, 2 * C]), ALU.mult)\
                            .then_inc(s["G_half"] if b == 0 else s["G_ready"], 1)

            dve.wait_ge(s["BK_stored"], 16 * 8 * NPAIR + FREE)
            dve.wait_ge(s["AR_stored"], 16 * 2 * NPAIR + FREE)
            dve.wait_ge(s["G_stored"], 16 * 2 * NPAIR + FREE)
            dve.wait_ge(s["v_stored"], 16 * NPAIR + FREE)
            for z in range(2):
                dve.memset(TI[z], 0.0).then_inc(s["TI_init"], 1)
            dve.wait_ge(s["TI_init"], 2)
            for z in range(2):
                diag = TI[z].rearrange("p e s t -> p e (s t)")[:, :, 0:C * C:C + 1]
                dve.memset(diag, 1.0).then_inc(s["TI_init"], 1)
            dve.wait_ge(s["TI_init"], 4)
            dve.wait_ge(s["M_loaded"], 16 * 16)
            step = 0
            for z in range(2):
                for n in range(1, C):
                    row = C - 1 - n if z == 0 else n
                    lo = row + 1 if z == 0 else 0
                    m = M[z][:, :, row, lo:lo + n].unsqueeze(2).broadcast_to([P, 2, n, n])
                    known = TI[z][:, :, lo:lo + n, lo:lo + n].rearrange("p e s t -> p e t s")
                    out = prod[:, :, 0:n, 0:n]
                    if step:
                        dve.wait_ge(s["sol_row"], step)
                    tt(out, m, known, ALU.mult).then_inc(s["sol_prod"], 1)
                    step += 1
                    dve.wait_ge(s["sol_prod"], step)
                    dve.tensor_reduce(TI[z][:, :, row, lo:lo + n], out, AX.X, ALU.add).then_inc(s["sol_row"], 1)

            dve.wait_ge(s["TI_stored"], 16 * 4 * NPAIR)
            dve.wait_ge(s["vat_evicted"], 1)
            dve.wait_ge(s["q_stored"], 16 * 10)
            dve.wait_ge(s["z_stored"], 16 * 6)
            dve.wait_ge(s["q_stored2"], 32)
            for z in range(2):
                dve.memset(S[:, z], 0.0).then_inc(sz[z]["S_new"], 1)
            with dve.Fori(0, NC // 4) as i:
                for q in range(4):
                    slot, cc = q // 2, q % 2
                    n = 4 * i + q
                    dve.wait_ge(sz[0]["X_mm"], n + 1)
                    dve.tensor_copy(Xs[:, 0], banks[:, 0, 0:256]).then_inc(sz[0]["X_out"], 1)
                    for z in range(2):
                        c2 = cc if z == 0 else 1 - cc
                        dve.wait_ge(sz[z]["U_mm"], n + 1)
                        dve.tensor_copy(UV[slot][0:C, z, c2].rearrange("p a b -> p (a b)"),
                                        banks[0:C, 2 + z, 0:256]).then_inc(sz[z]["U_e0"], 1)
                    for z in range(2):
                        c = n if z == 0 else (i * -4 + (NC - 1 - q))
                        dve.wait_ge(sz[z]["S_mm"], n + 1)
                        tt(St[:, z], S[:, z], banks[:, 2 + z, 256:512].rearrange("p (j i) -> p j i", j=NPAIR), ALU.add)\
                            .then_inc(sz[z]["S_add"], 1)
                        dve.wait_ge(sz[z]["S_add"], n + 1 + FREE)
                        tt(S[:, z], St[:, z], PC[:, z, :, bass.ds(c, 1)].broadcast_to([P, NPAIR, HD]), ALU.mult)\
                            .then_inc(sz[z]["S_new"], 1)

            with dve.Fori(0, NT // 2) as i:
                for slot in range(2):
                    dve.wait_ge(att_full[slot], 64 * i + 64)
                    for g in range(2):
                        blk = 4 * i + 2 * slot + g
                        dve.wait_ge(s["p_exp"], 4 * blk + FREE)
                        for h in range(GH):
                            dve.wait_ge(s["sc_mm"], 4 * blk + h + 1)
                            stt(Lg[:, h, :], nd[slot], slope[:, GH * g + h:GH * g + h + 1], banks[:, 4 + h % 2, 0:BAND],
                                ALU.mult, ALU.add).then_inc(s["sc_out"], 1)
                        dve.wait_ge(s["sc_out"], 4 * blk + 4)
                        dve.tensor_reduce(nm, Lg, AX.X, ALU.max).then_inc(s["mx_red"], 1)
                        dve.wait_ge(s["mx_red"], blk + 1)
                        dve.wait_ge(s["s_exp"], blk + FREE)
                        tt(mx, nm, sink[:, GH * g:GH * g + GH], ALU.max).then_inc(s["mx_sink"], 1)
                        dve.wait_ge(s["mx_sink"], 2 * blk + 1)
                        ts(nm, mx, -1.0, None, ALU.mult).then_inc(s["nm_ready"], 1)
                        dve.wait_ge(s["nm_ready"], blk + 1)
                        tt(mx, sink[:, GH * g:GH * g + GH], mx, ALU.subtract).then_inc(s["mx_sink"], 1)
                        dve.wait_ge(s["p_exp"], 4 * blk + 4 + FREE)
                        dve.wait_ge(s["s_exp"], blk + 1 + FREE)
                        tt(rsum, rsum, es, ALU.add).then_inc(s["sum_all"], 1)
                        dve.wait_ge(s["sum_all"], blk + 1)
                        dve.reciprocal(rinv, rsum).then_inc(s["inv_ready"], 1)
                        dve.wait_ge(s["inv_ready"], blk + 1)
                        tt(Pr, Pr, rinv.unsqueeze(2).broadcast_to([P, GH, BAND]), ALU.mult).then_inc(s["p_norm"], 1)

            dve.wait_ge(s["o_out"], 2 * NT + FREE)
            heads = lambda x: x.rearrange("p (h n) -> p h n", n=HD)
            spread = lambda x: x.unsqueeze(2).broadcast_to([P, AH, HD])
            with dve.Fori(0, NT // 2) as i:
                for slot in range(2):
                    t = 2 * i + slot
                    dve.wait_ge(y_full[slot], 16 * i + 16)
                    tt(ysum, yin[slot][:, 0], yin[slot][:, 1], ALU.add).then_inc(yin_used[slot], 1)
                    dve.wait_ge(yin_used[slot], i + 1)
                    dve.tensor_reduce(stat[:, 0], heads(ysum), AX.X, ALU.add).then_inc(s["y_summed"], 1)
                    dve.wait_ge(s["y_summed"], t + 1)
                    ts(stat[:, 0], stat[:, 0], 1.0 / HD, None, ALU.mult).then_inc(s["y_mean"], 1)
                    dve.wait_ge(s["y_mean"], t + 1)
                    dve.wait_ge(s["y_normed"], t + FREE)
                    tt(heads(ycen), heads(ysum), spread(stat[:, 0]), ALU.subtract).then_inc(s["y_cent"], 1)
                    dve.wait_ge(s["y_sq"], t + 1)
                    dve.tensor_reduce(stat[:, 1], heads(ysq), AX.X, ALU.add).then_inc(s["y_var"], 1)
                    dve.wait_ge(s["y_sd"], t + 1)
                    dve.reciprocal(stat[:, 3], stat[:, 2]).then_inc(s["y_inv"], 1)
                    dve.wait_ge(s["y_inv"], t + 1)
                    tt(heads(yn[:, bass.ds(t, 1), :].rearrange("p o n -> p (o n)")), heads(ycen), spread(stat[:, 3]),
                       ALU.mult).then_inc(s["y_normed"], 1)
            for j in range(NPAIR):
                dve.wait_ge(s["yt_mm"], j + 1)
                ts(ot1, ps[2 * (j % 2)], col("lnx_g", j), col("lnx_b", j), ALU.mult, ALU.add).then_inc(s["y_aff"], 1)
                dve.wait_ge(s["y_aff"], j + 1)
                tt(ot1, ot1, bonusT[:, j, :], ALU.add).then_inc(s["y_bon"], 1)
                dve.wait_ge(s["y_bon"], j + 1)
                dve.wait_ge(s["gt_mm"], j + 1)
                tt(oT[:, j, :], ot1, ps[2 * (j % 2) + 1], ALU.mult).then_inc(s["y_gated"], 1)
                dve.wait_ge(s["y_gated"], j + 1)

            with dve.Fori(0, KD // 2) as i:
                for slot in range(2):
                    x = xT[:, bass.ds(2 * i + slot, 1), :].rearrange("p o t -> p (o t)")
                    dve.wait_ge(so["mm"][slot], i + 1)
                    tt(x, x, ps[slot], ALU.add).then_inc(so["added"][slot], 1)
            norm(1, acc, sqb, rs, "ln2")
            with dve.Fori(0, KF // 2) as i:
                for slot in range(2):
                    g = ga[slot]
                    dve.wait_ge(sg["scaled"], 2 * i + slot + 1)
                    stt(g[:, 1:T], ps[2 * slot][:, 0:T - 1], col("cw0", 2 * i + slot), g[:, 1:T], ALU.mult, ALU.add)\
                        .then_inc(sg["c1"], 1)
                    dve.wait_ge(sg["c1"], 2 * i + slot + 1)
                    stt(g[:, 0:T - 1], ps[2 * slot][:, 1:T], col("cw2", 2 * i + slot), g[:, 0:T - 1], ALU.mult,
                        ALU.add).then_inc(sg["c2"], 1)
                    dve.wait_ge(sg["u_mm"], 2 * i + slot + 1)
                    dve.wait_ge(sg["gelu"], 2 * i + slot + 1)
                    tt(actT[:, bass.ds(2 * i + slot, 1), :].rearrange("p o t -> p (o t)"), g, ps[2 * slot + 1],
                       ALU.mult).then_inc(sg["done"][slot], 1)
            with dve.Fori(0, KD // 2) as i:
                for slot in range(2):
                    x = xT[:, bass.ds(2 * i + slot, 1), :].rearrange("p o t -> p (o t)")
                    dve.wait_ge(so["mm"][slot], KD // 2 + i + 1)
                    tt(x, x, ps[slot], ALU.add).then_inc(so["added"][slot], 1)
            norm(2, hT[:, 7, :], (hT[:, 5, :], hT[:, 6, :]), work[:, 0:T], "lnf")


INPUTS = {"par": (P, NPAR), "ident": (P, P), "pairones": (P, P), "ones": (P, P), "gmask": (P, 2, 2 * C),
          "reset": (P, 2, TP), "sink": (P, AH), "slope": (P, AH), "negdist": (NT, P, BAND), "xT": (P, KD, T),
          "w_in": (20, P, KD, P), "lora_w": (NPAIR, P, 2 * P), "gate_w": (P, RW), "w_out": (KD, P, KD, P),
          "w_gu": (KF, P, 2, KD, P), "w_down": (KD, P, KF, P)}


def shape_constants():
    f = np.float32
    t = np.arange(C)
    gm = np.zeros((2, 2, C, 2, 2, C), f)
    sv, tv = t[:, None], t[None, :]
    for z, (strict, loose) in enumerate(((sv < tv, sv <= tv), (sv > tv, sv >= tv))):
        gm[:, :, :, z, 0] = strict
        gm[:, :, :, z, 1] = loose
    reset = np.ones((P, 2, NC, CP), f)
    reset[:, 0, :, 0] = 0
    reset[:, 1, :, C] = 0
    q, k = np.arange(P)[:, None], np.arange(BAND)[None, :] - P
    dist = np.abs(k - q)
    nd = np.empty((NT, P, BAND), f)
    for n in range(NT):
        ok = (dist <= P) & (n * P + k >= 0) & (n * P + k < T)
        nd[n] = np.where(ok, -dist, -1e33)
    slopes = (2.0 ** (-8.0 * np.arange(1, AH + 1) / AH)).astype(f)
    return {"ident": np.eye(P, dtype=f), "pairones": np.kron(np.eye(2), np.ones((HD, HD))).astype(f),
            "ones": np.ones((P, P), f), "gmask": gm.reshape(P, 2, 2 * C), "reset": reset.reshape(P, 2, TP),
            "slope": np.tile(slopes, (P, 1)), "negdist": nd}


def tiles(w):
    k, m = w.shape
    return np.ascontiguousarray(w.reshape(k // P, P, m // P, P).transpose(2, 1, 0, 3))


def kernel(**inputs):
    import concourse.bacc as bacc
    from concourse.bass_utils import run_bass_kernel_spmd

    v = {k: np.asarray(x) for k, x in inputs.items()}
    arrays = shape_constants()
    named = {"mu_prev": v["shift_mu_prev"], "mu_next": v["shift_mu_next"], "w0": v["decay_w0"], "a0": v["iclr_a0"],
             "k_k": v["k_k"], "k_a": v["k_a"], "r_k": v["r_k"], "lnx_g": v["lnx_g"], "lnx_b": v["lnx_b"],
             "ln1": v["ln1_g"], "ln2": v["ln2_g"], "lnf": v["lnf_g"], "cw0": v["ffn_conv_w"][0, 0],
             "cw1": v["ffn_conv_w"][0, 1], "cw2": v["ffn_conv_w"][0, 2], "cb": v["ffn_conv_b"]}
    arrays["par"] = np.ascontiguousarray(np.concatenate([named[n].reshape(-1, P) for n in COLS]).T)
    arrays["sink"] = np.ascontiguousarray(np.broadcast_to(v["attn_sink"][0], (P, AH)))
    arrays["xT"] = np.ascontiguousarray(v["x"][0].reshape(T, KD, P).transpose(2, 1, 0))
    w_in = tiles(v["w_in"][0])
    order = [12, 13] + [4 * i + j for j in range(NPAIR) for i in range(3)] + list(range(14, 20))
    arrays["w_in"] = np.ascontiguousarray(w_in[order])
    lora = np.zeros((NPAIR, P, 2 * P), np.float32)
    w2 = v["decay_w2"][0].reshape(2, HD, NPAIR, P)
    lora[:, 0:HD, 0:P], lora[:, 0:HD, P:] = w2[0].transpose(1, 0, 2), w2[1].transpose(1, 0, 2)
    lora[:, HD:, 0:P] = v["iclr_a2"][0].reshape(HD, NPAIR, P).transpose(1, 0, 2)
    arrays["lora_w"] = lora
    arrays["gate_w"] = np.ascontiguousarray(v["gate_g2"][0])
    arrays["w_out"] = tiles(v["w_out"][0])
    arrays["w_gu"] = np.ascontiguousarray(np.stack([tiles(v["ffn_w_gate"][0]), tiles(v["ffn_w_up"][0])], axis=2))
    arrays["w_down"] = tiles(v["ffn_w_down"][0])

    nc = bacc.Bacc("TRN2", target_bir_lowering=False, num_devices=1)
    args = {n: nc.dram_tensor(f"in_{n}", shape, F32, kind="ExternalInput").ap() for n, shape in INPUTS.items()}
    args["out"] = nc.dram_tensor("out_y", (P, KD, T), F32, kind="ExternalOutput").ap()
    hymba_block(nc, args)
    r = run_bass_kernel_spmd(nc, [{f"in_{n}": arrays[n] for n in INPUTS}], core_ids=[0])
    y = r.results[0]["out_y"]
    return np.ascontiguousarray(np.asarray(y).transpose(2, 1, 0).reshape(1, T, D))
```

```python
import math
from contextlib import ExitStack

import numpy as np

import concourse.bass as bass
from concourse import mybir

F32 = mybir.dt.float32
F32R = mybir.dt.float32r
ALU = mybir.AluOpType
ACT = mybir.ActivationFunctionType
AX = mybir.AxisListType

P = 128
T = 1024
D = 1024
HD = 64
KD = D // P
RW = 512
NPAIR = RW // P
NT = T // P
C = 32
NC = T // C
CP = C + 1
TP = NC * CP
F = 2816
KF = F // P
AH = 8
GH = 4
BAND = 3 * P
DECAY = math.exp(-0.5)
NORM_EPS = 1e-6
LNX_EPS = 64e-5
L2_EPS = 1e-12
FREE = 1
GROUPS = ((0, 8), (8, 8), (16, 6))
GK = 8
HALF = 512

COLS = {}
_n = 0
for _name, _w in (("mu_prev", 14), ("mu_next", 14), ("w0", 8), ("a0", 4), ("k_k", 4), ("k_a", 4), ("r_k", 4),
                  ("lnx_g", 4), ("lnx_b", 4), ("ln1", 8), ("ln2", 8), ("lnf", 8),
                  ("cw0", 22), ("cw1", 22), ("cw2", 22), ("cb", 22)):
    COLS[_name] = _n
    _n += _w
NPAR = _n


def hymba_block(nc, a):
    with ExitStack() as ctx:
        def sb(name, shape):
            return ctx.enter_context(nc.sbuf_tensor(name, shape, F32))

        def sem(name):
            return ctx.enter_context(nc.semaphore(name))

        def dram(name, shape):
            return nc.dram_tensor(name, shape, F32, kind="Internal").ap()

        AR_d = dram("AR_d", (2, NPAIR, P, NC * 2 * C))
        G_d = dram("G_d", (2, NPAIR, P, NC * 2 * C))
        BK_d = dram("BK_d", (2, NPAIR, P, NC * HD))
        TI_d = dram("TI_d", (2, NPAIR, 2, C, NC * C))
        v_d = dram("v_d", (T, RW))
        y_d = dram("y_d", (2, T, RW))
        q_d = dram("q_d", (4, P, T))
        kk_d = dram("kk_d", (2, P, T + 2 * P))
        va_d = dram("va_d", (T + 2 * P, P))

        par = sb("par", [P, NPAR])
        c0_eps = sb("c0_eps", [P, 16])
        c0 = c0_eps[:, 0:14]
        eps = c0_eps[:, 14:16]
        oka = sb("oka", [P, NPAIR])
        ident = sb("ident", [P, P])
        pairones = sb("pairones", [P, P])
        ones = sb("ones", [P, P])
        gmask = sb("gmask", [P, 2, 2 * C])
        sink = sb("sink", [P, AH])
        slope = sb("slope", [P, AH])
        PC = sb("PC", [P, 2, NPAIR, NC])
        xT = sb("xT", [P, KD, T])
        WPART = KD * P
        H_AT = 2 * GK * T + 6 * WPART
        SG_AT = H_AT + 2 * KD * T
        WORK = SG_AT - KD * T
        region_at = (nc.sbuf_base + 31) // 32 * 32
        hT = sb("hT", [P, KD, T])
        oT = hT
        work = sb("work", [P, WORK])
        sgT = sb("sgT", [P, T])
        bonusT = sb("bonusT", [P, NPAIR, T])

        def part(name, at, shape):
            return nc.alloc_sbuf_tensor_at(name, shape, F32R, offset=region_at + 4 * at)

        g_hi, g_lo = part("g_hi", 0, [P, GK, T]), part("g_lo", GK * T, [P, GK, T])
        w_hi = [part(f"w_hi{i}", 2 * GK * T + i * WPART, [P, KD, P]) for i in range(2)]
        w_lo = [part(f"w_lo{i}", 2 * GK * T + (2 + i) * WPART, [P, KD, P]) for i in range(2)]
        RAW_AT = 2 * GK * T + 4 * WPART - KD * T
        w_raw = [work[:, RAW_AT + i * WPART:RAW_AT + (i + 1) * WPART].rearrange("p (k n) -> p k n", n=P)
                 for i in range(2)]
        h_hi, h_lo = part("h_hi", H_AT, [P, KD, T]), part("h_lo", H_AT + KD * T, [P, KD, T])
        ga = [sgT[:, :], bonusT[:, 0, :]]

        class Carve:
            def __init__(self, at=0):
                self.at = at

            def __call__(self, *shape):
                n = int(np.prod(shape))
                v = work[:, self.at:self.at + n]
                self.at += n
                assert self.at <= WORK, self.at
                if len(shape) == 1:
                    return v
                names = "abcd"[:len(shape)]
                return v.rearrange(f"p ({' '.join(names)}) -> p {' '.join(names)}",
                                   **{x: s for x, s in zip(names[1:], shape[1:])})

        banks = ctx.enter_context(nc.psum_tensor("banks", [P, 8, HALF], F32))
        flat = banks[:, :, :].rearrange("p b n -> p (b n)")
        ps = [flat[:, 2 * s * HALF:2 * (s + 1) * HALF] for s in range(4)]

        def col(name, m, n=1):
            return par[:, bass.ds(m + COLS[name], n)]

        acc, rs = bonusT[:, 0, :], bonusT[:, 1, :]
        sqb = [bonusT[:, 2, :], bonusT[:, 3, :]]

        w = Carve()
        W3 = [w(KD, P) for _ in range(3)]
        lora = w(T)
        lw = w(2 * P)
        rT, kT, vT = w(T), w(T), w(T)
        kkT, bT, aT, tpT, sqT = w(T), w(T), w(T), w(T), w(T)
        L = [w(TP) for _ in range(2)]
        E = [w(TP) for _ in range(2)]
        Ei = [w(TP) for _ in range(2)]
        reset = w(2, TP)
        AR, BK = w(NC, 2, C), w(NC, 2, C)
        G, BKt = w(NC, 2 * C), w(NC // 2, P)
        vts = w(NT, P)
        assert w.at <= WORK

        w = Carve(3 * KD * P)
        M = [w(2, C, C) for _ in range(2)]
        TI = [w(2, C, C) for _ in range(2)]
        prod = w(2, C, C)
        qst = [w(T) for _ in range(2)]
        zero = w(P)
        vast = w(NT, P)

        w = Carve()
        ARs = [w(2, NPAIR, 2 * 2 * C) for _ in range(2)]
        Gs = [w(2, NPAIR, 2 * 2 * C) for _ in range(2)]
        BKs = [w(2, NPAIR, 2 * HD) for _ in range(2)]
        TIs = [w(2, NPAIR, 2 * C) for _ in range(2)]
        UV = [w(2, 2, NPAIR, HD) for _ in range(2)]
        S = w(2, NPAIR, HD)
        St = w(2, NPAIR, HD)
        Xs = w(2, NPAIR * HD)
        Ys = [w(2, NPAIR * HD) for _ in range(2)]
        qs, ks, vs, nd = w(4, P), w(2, BAND), w(3, P), w(BAND)
        Lg = w(GH, BAND)
        Pr = w(GH, BAND)
        PT = w(3, 2, 2, P)
        mx, nm, es, rsum, rinv = w(GH), w(GH), w(GH), w(GH), w(GH)

        w = Carve()
        yin = [w(2, RW) for _ in range(2)]
        ysum, ycen, ysq = w(RW), w(RW), w(RW)
        stat = w(4, AH)
        yn = w(NT, RW)
        assert w.at <= 2 * GK * T - KD * T
        w = Carve(2 * GK * T + 2 * WPART - KD * T)
        gw = w(RW)
        ot1 = w(T)

        names = """consts_loaded x_loaded consts_made
            p_mm p_scaled p_shift1 p_shifted lora_tanh gate_sig lw_full
            dz0_mm dz1_mm ic_mm sig0 sig1 a_ready kk_ready kk_sq ss_mm nrm_ready nrm_max nrm_rec nk_ready b_ready
            ka_fac kp_ready bon_in bon_mm bon_out vt_mm vts_ready v_stored
            L0_ready L1_ready E0_ready E1_ready
            ab_ready k_prod gram_mm G_half G_ready bkt_mm bkt_half bkt_ready AR_stored G_stored BK_stored PC_saved
            pad_zero
            qkv_mm qkv_evicted q_stored q_stored2 z_stored c0_part vat_mm vat_evicted zero_made
            M_loaded TI_init sol_prod sol_row TI_stored
            X0_mm X1_mm X0_out X1_out U0_mm U1_mm U00 U01 U10 U11 Y0_mm Y1_mm S0_mm S1_mm Y0_out Y1_out
            S0_add S1_add S0_new S1_new
            sc_mm sc_out mx_red mx_sink nm_ready p_exp s_exp sum_all inv_ready p_norm pt_mm pt_out o_mm o_out
            y_summed y_mean y_cent y_sq y_var y_sd y_inv y_normed yt_mm gt_mm y_aff y_bon y_gated gw_loaded
            out_stored""".split()
        s = {n: sem(n) for n in names}
        w_full = [sem(f"w_full{i}") for i in range(3)]
        scan_full = [sem(f"scan_full{i}") for i in range(2)]
        qk_full, val_full = sem("qk_full"), sem("val_full")
        y_full = [sem(f"y_full{i}") for i in range(2)]
        pe_passed = sem("pe_passed")
        yin_used = [sem(f"yin_used{i}") for i in range(2)]
        ys_stored = [sem(f"ys_stored{i}") for i in range(2)]
        sz = [{k: s[v] for k, v in dict(X_mm=f"X{z}_mm", X_out=f"X{z}_out", U_mm=f"U{z}_mm", U_e0=f"U{z}0",
                                        U_e1=f"U{z}1", Y_mm=f"Y{z}_mm", S_mm=f"S{z}_mm", Y_out=f"Y{z}_out",
                                        S_add=f"S{z}_add", S_new=f"S{z}_new").items()} for z in range(2)]

        ns = {k: sem(f"norm_{k}") for k in ("squared", "summed", "ms_mm", "root", "rstd", "scaled")}

        def slot_sems(tag, keys):
            return {k: [sem(f"{tag}_{k}{i}") for i in range(2)] for k in keys}

        wt = slot_sems("wt", ("full", "hi", "lo", "used"))
        added = [sem(f"added{i}") for i in range(2)]
        gu_done = [sem(f"gu_done{i}") for i in range(2)]
        g_split = [sem(f"g_split{i}") for i in range(2)]
        fs = {k: sem(f"ffn_{k}") for k in ("scaled", "c1", "c2", "gelu", "g_hi")}
        sp_s = {k: sem(k) for k in ("o_hi", "att_hi", "o_lo", "att_lo", "h_hi", "h_lo")}

        NCONST = 8
        start_at_one = [s[n] for n in """p_mm ic_mm bkt_ready G_ready pt_out o_out gram_mm v_stored BK_stored
            AR_stored G_stored pt_mm o_mm bkt_mm p_exp s_exp y_normed""".split()]
        start_at_one += ys_stored + added + gu_done + wt["lo"] + wt["used"] + g_split + [sz[z][n] for z in range(2) for n in ("Y_out", "S_add")]
        block = ctx.enter_context(nc.Block())

        def first_unit(f0):
            return KD // 2 + f0 + (KD // 2) * [g[0] for g in GROUPS].index(f0)

        LAST_UNIT = first_unit(GROUPS[-1][0]) + GROUPS[-1][1] + KD // 2 - 1

        def chunked(x, z, excl):
            v = x.rearrange("p (c t) -> p c t", t=CP)
            first = (0 if excl else 1) if z == 0 else (1 if excl else 0)
            return v[:, :, first:first + C]

        @block.sync
        def _(sp):
            for x in start_at_one:
                sp.sem_inc(x, FREE)
            for dst, src in ((par[:, :], a["par"]), (ident[:, :], a["ident"]), (pairones[:, :], a["pairones"]),
                             (gmask[:, :, :], a["gmask"]), (reset, a["reset"]), (sink[:, :], a["sink"]),
                             (slope[:, :], a["slope"]), (ones[:, :], a["ones"])):
                sp.dma_start(dst, src).then_inc(s["consts_loaded"], 16)
            for k in range(0, KD, 2):
                sp.dma_start(xT[:, k, :], a["xT"][:, k, :]).then_inc(s["x_loaded"], 16)
            for i in range(2):
                sp.dma_start(W3[i], a["w_in"][i]).then_inc(w_full[i], 16)
            sp.dma_start(W3[2], a["w_in"][4]).then_inc(w_full[2], 16)
            for i in range(2):
                sp.wait_ge(s["p_mm"], i + 1 + FREE)
                sp.dma_start(W3[i], a["w_in"][2 + i]).then_inc(w_full[i], 16)
            with sp.Fori(0, NPAIR) as j:
                pair = bass.ds(j, 1)
                sp.wait_ge(s["ic_mm"], j + FREE)
                sp.dma_start(lw, a["lora_w"][pair].rearrange("o p n -> (o p) n")).then_inc(s["lw_full"], 16)
                for i in range(3):
                    sp.wait_ge(s["p_mm"], 3 * j + 3 + i + FREE)
                    sp.dma_start(W3[i], a["w_in"][bass.ds(3 * j + (5 + i), 1)].rearrange("o p k n -> (o p) k n"))\
                      .then_inc(w_full[i], 16)
                sp.wait_ge(s["vts_ready"], j + 1)
                sp.dma_start(v_d.rearrange("(b p) n -> p b n", p=P)[:, :, bass.ds(j * P, P)], vts)\
                  .then_inc(s["v_stored"], 16)
                for z in range(2):
                    sp.wait_ge(s["ab_ready"], 2 * j + z + 1)
                    sp.dma_start(AR_d[z][pair].rearrange("o p n -> (o p) n"), AR.rearrange("p c a t -> p (c a t)"))\
                      .then_inc(s["AR_stored"], 16)
                    sp.wait_ge(s["G_ready"], 2 * j + z + 1 + FREE)
                    sp.dma_start(G_d[z][pair].rearrange("o p n -> (o p) n"), G.rearrange("p c t -> p (c t)"))\
                      .then_inc(s["G_stored"], 16)
                    sp.wait_ge(s["bkt_ready"], 2 * j + z + 1 + FREE)
                    for odd in range(2):
                        for e in range(2):
                            dst = BK_d[z][pair, 64 * e:64 * e + 64].rearrange("o p (c q n) -> (o p) c q n", q=2, n=HD)
                            sp.dma_start(dst[:, :, odd, :], BKt[64 * odd:64 * odd + 64, :, HD * e:HD * e + HD])\
                              .then_inc(s["BK_stored"], 16)
            for i in range(3, 6):
                sp.wait_ge(s["qkv_mm"], i - 2)
                sp.dma_start(W3[i % 3], a["w_in"][14 + i]).then_inc(w_full[i % 3], 16)
            sp.wait_ge(s["G_stored"], 16 * 2 * NPAIR + FREE)
            sp.wait_ge(s["BK_stored"], 16 * 8 * NPAIR + FREE)
            sp.wait_ge(s["AR_stored"], 16 * 2 * NPAIR + FREE)
            sp.wait_ge(s["v_stored"], 16 * NPAIR + FREE)
            for z in range(2):
                for j in range(NPAIR):
                    for e in range(2):
                        src = G_d[z, j, 64 * e:64 * e + C].rearrange("s (c x) -> c s x", x=2 * C)[:, :, 0:C]
                        sp.dma_start(M[z][C * j:C * (j + 1), e, :, :], src).then_inc(s["M_loaded"], 16)
            sp.wait_ge(s["TI_stored"], 16 * 4 * NPAIR)
            sp.wait_ge(s["q_stored"], 16 * 10)
            sp.wait_ge(s["q_stored2"], 32)
            sp.wait_ge(s["z_stored"], 16 * 6)
            v_rows = v_d.rearrange("(c t) (j e i) -> c e t j i", t=C, j=NPAIR, e=2)

            def load_scan(i, slot):
                for z in range(2):
                    c = (4 * i + 2 * slot) if z == 0 else (i * -4 + (NC - 2 - 2 * slot))
                    for dst, src, n in ((ARs, AR_d, 2 * C), (Gs, G_d, 2 * C), (BKs, BK_d, HD)):
                        sp.dma_start(dst[slot][:, z], src[z].rearrange("j p n -> p j n")[:, :, bass.ds(c * n, 2 * n)])\
                          .then_inc(scan_full[slot], 16)
                    for e in range(2):
                        sp.dma_start(TIs[slot][64 * e:64 * e + C, z],
                                     TI_d[z, :, e].rearrange("j s n -> s j n")[:, :, bass.ds(c * C, 2 * C)])\
                          .then_inc(scan_full[slot], 16)
                        for cc in range(2):
                            sp.dma_start(UV[slot][64 * e + C:64 * e + 2 * C, z, cc],
                                         v_rows[bass.ds(c + cc, 1), e].rearrange("o t j i -> (o t) j i"))\
                              .then_inc(scan_full[slot], 16)

            def load_qk(n):
                for dst, src in ((qs, q_d.rearrange("j p t -> p j t")[:, :, bass.ds(n * P, P)]),
                                 (ks, kk_d.rearrange("g p t -> p g t")[:, :, bass.ds(n * P, BAND)]),
                                 (nd, a["negdist"][bass.ds(n, 1)].rearrange("o p n -> (o p) n"))):
                    sp.dma_start(dst, src).then_inc(qk_full, 16)

            def load_values(n):
                sp.dma_start(vs, va_d.rearrange("(b p) n -> p b n", p=P)[:, bass.ds(n, 3), :]).then_inc(val_full, 16)

            load_scan(0, 0)
            load_qk(0)
            load_values(0)
            load_scan(0, 1)
            y_rows = y_d.rearrange("z (c t) (j e i) -> z c e t j i", t=C, j=NPAIR, e=2)

            def store_y(i, q):
                for z in range(2):
                    c = 4 * i + q if z == 0 else i * -4 + (NC - 1 - q)
                    sp.wait_ge(sz[z]["Y_out"], 4 * i + q + 1 + FREE)
                    for e in range(2):
                        sp.dma_start(y_rows[z, bass.ds(c, 1), e].rearrange("o t j i -> (o t) j i"),
                                     Ys[q % 2][64 * e + C:64 * e + 2 * C, z].rearrange("p (j i) -> p j i", j=NPAIR))\
                          .then_inc(ys_stored[q % 2], 16)

            with sp.Fori(0, NC // 4 - 1) as i:
                for slot in range(2):
                    store_y(i, 2 * slot)
                    store_y(i, 2 * slot + 1)
                    for z in range(2):
                        sp.wait_ge(sz[z]["Y_mm"], 4 * i + 2 * slot + 2)
                        sp.wait_ge(sz[z]["S_mm"], 4 * i + 2 * slot + 2)
                    load_scan(i + 1, slot)
                    if slot == 1:
                        sp.wait_ge(s["sc_out"], 8 * i + 8)
                        load_qk(i + 1)
                        sp.wait_ge(s["o_mm"], 2 * i + 2 + FREE)
                        load_values(i + 1)
            for q in range(4):
                store_y(NC // 4 - 1, q)
            for b in range(2):
                sp.wait_ge(ys_stored[b], 64 * NC // 2 + FREE)
            sp.wait_ge(s["o_out"], 2 * NT + FREE)
            sp.dma_start(gw, a["gate_w"]).then_inc(s["gw_loaded"], 16)
            for slot in range(2):
                sp.dma_start(yin[slot], y_d[:, slot * P:(slot + 1) * P].rearrange("z p n -> p z n"))\
                  .then_inc(y_full[slot], 16)
            with sp.Fori(0, NT // 2 - 1) as i:
                for slot in range(2):
                    sp.wait_ge(yin_used[slot], i + 1)
                    sp.dma_start(yin[slot], y_d[:, bass.ds((2 * i + 2 + slot) * P, P)].rearrange("z p n -> p z n"))\
                      .then_inc(y_full[slot], 16)
            def load_weights(slot, n, src, kn=KD):
                sp.wait_ge(wt["lo"][slot], n + FREE)
                sp.dma_start(w_raw[slot][:, 0:kn], src).then_inc(wt["full"][slot], 16)

            with sp.Fori(0, KD // 2) as i:
                for slot in range(2):
                    load_weights(slot, i, a["w_out"][bass.ds(2 * i + slot, 1)].rearrange("o p k n -> (o p) k n"))
            for f0, fn in GROUPS:
                with sp.Fori(0, fn) as f:
                    for slot in range(2):
                        load_weights(slot, f + first_unit(f0), a["w_gu"][bass.ds(f + f0, 1), :, slot]
                                     .rearrange("o p k n -> (o p) k n"))
                with sp.Fori(0, KD // 2) as i:
                    for slot in range(2):
                        load_weights(slot, i + first_unit(f0) + fn, a["w_down"][bass.ds(2 * i + slot, 1), :, f0:f0 + fn]
                                     .rearrange("o p k n -> (o p) k n"), fn)
            for k in range(KD):
                sp.wait_ge(ns["scaled"], 2 * KD + k + 1)
                sp.dma_start(a["out"][:, k, :], hT[:, k, :]).then_inc(s["out_stored"], 16)
            sp.wait_ge(s["out_stored"], 16 * KD)

        @block.tensor
        def _(pe):
            def dense(out, wt, src, kn, done):
                for k in range(kn):
                    for h in range(2):
                        mm = pe.matmul(out[:, h * HALF:(h + 1) * HALF], wt[:, k, :],
                                       src[:, k, h * HALF:(h + 1) * HALF], start=(k == 0), stop=(k == kn - 1))
                mm.then_inc(done, 1)

            def split_dense(out, slot, hi, lo, kn, after=()):
                for k in range(kn):
                    for k_at, sem_, n in after:
                        if k == k_at:
                            pe.wait_ge(sem_, n)
                    for p_, (wp, xp) in enumerate(((w_hi, hi), (w_hi, lo), (w_lo, hi))):
                        for h in range(2):
                            mm = pe.matmul(out[:, h * HALF:(h + 1) * HALF], wp[slot][:, k, :],
                                           xp[:, k, h * HALF:(h + 1) * HALF], start=(k == 0 and p_ == 0),
                                           stop=(k == kn - 1 and p_ == 2))
                mm.then_inc(wt["used"][slot], 1)

            def whole(out, wt, src, done, rows=slice(0, P)):
                for h in range(2):
                    mm = pe.matmul(out[:, h * HALF:(h + 1) * HALF], wt, src[rows, h * HALF:(h + 1) * HALF],
                                   start=True, stop=True)
                mm.then_inc(done, 1)

            def settled():
                pe.sem_inc(pe_passed, 1)

            def norm(n, ac):
                pe.wait_ge(ns["summed"], (n + 1) * (KD - 1))
                whole(ps[0], ones[:, :], ac, ns["ms_mm"])

            pe.wait_ge(s["consts_loaded"], 16 * NCONST)
            norm(0, acc)
            pe.wait_ge(ns["root"], 1)
            pe.wait_ge(ns["scaled"], KD)
            for i in range(2):
                pe.wait_ge(w_full[i], 16)
                dense(ps[i], W3[i], hT, KD, s["p_mm"])
            pe.wait_ge(s["p_shifted"], 2)
            pe.wait_ge(s["lora_tanh"], 1)
            with pe.Fori(0, NPAIR) as j:
                pe.wait_ge(s["bkt_ready"], 2 * j + FREE)
                pe.wait_ge(s["G_ready"], 2 * j + FREE)
                for i in range(3):
                    pe.wait_ge(w_full[i], 16 * j + (32 if i < 2 else 16))
                    dense(ps[i], W3[i], hT, KD, s["p_mm"])
                pe.wait_ge(s["lw_full"], 16 * j + 16)
                whole(ps[3], lw[0:64, 0:P], lora, s["dz0_mm"], slice(0, 64))
                pe.wait_ge(s["p_shifted"], 3 * j + 3)
                whole(ps[0], lw[0:64, P:2 * P], lora, s["dz1_mm"], slice(0, 64))
                pe.wait_ge(s["p_shifted"], 3 * j + 4)
                whole(ps[1], lw[64:128, 0:P], lora, s["ic_mm"], slice(64, P))
                pe.wait_ge(s["p_shifted"], 3 * j + 5)
                for n in range(NT):
                    mm = pe.transpose(ps[2][:, n * P:(n + 1) * P], vT[:, n * P:(n + 1) * P], ident[:, :])
                mm.then_inc(s["vt_mm"], 1)
                pe.wait_ge(s["kk_sq"], j + 1)
                pe.wait_ge(s["sig0"], j + 1)
                whole(ps[3], pairones[:, :], sqT, s["ss_mm"])
                pe.wait_ge(s["bon_in"], j + 1)
                pe.wait_ge(s["sig1"], j + 1)
                whole(ps[0], pairones[:, :], tpT, s["bon_mm"])
                for z in range(2):
                    pe.wait_ge(s["ab_ready"], 2 * j + z + 1)
                    pe.wait_ge(s["k_prod"], 2 * j + z + 1)
                    if z == 0:
                        pe.wait_ge(s["a_ready"], j + 1)
                        pe.wait_ge(s["vts_ready"], j + 1)
                    else:
                        pe.wait_ge(s["G_ready"], 2 * j + 1 + FREE)
                    settled()
                    for c in range(NC):
                        for e in range(2):
                            h = slice(64 * e, 64 * e + 64)
                            out = ps[1 + c // 16][h, (c % 16) * 64:(c % 16) * 64 + 64]
                            mm = pe.matmul(out, BK[h, c].rearrange("p a b -> p (a b)"),
                                           AR[h, c].rearrange("p a b -> p (a b)"), start=True, stop=True)
                    mm.then_inc(s["gram_mm"], 1)
                    if z == 0:
                        pe.wait_ge(s["nrm_ready"], j + 1)
                        pe.wait_ge(s["bon_out"], j + 1)
                    else:
                        pe.wait_ge(s["bkt_ready"], 2 * j + 1 + FREE)
                    for c in range(NC // 2):
                        out = ps[(3, 0)[c // 8]][:, (c % 8) * P:(c % 8 + 1) * P]
                        mm = pe.transpose(out, BK[:, 2 * c:2 * c + 2].rearrange("p c a b -> p (c a b)"), ident[:, :])
                    mm.then_inc(s["bkt_mm"], 1)
            for i in range(6):
                if i == 0:
                    pe.wait_ge(s["bkt_ready"], 2 * NPAIR + FREE)
                    pe.wait_ge(s["G_ready"], 2 * NPAIR + FREE)
                if i >= 4:
                    pe.wait_ge(s["qkv_evicted"], i - 3)
                pe.wait_ge(w_full[i % 3], 16 * (NPAIR + 1 + i // 3 + (1 if i % 3 < 2 else 0)))
                dense(ps[i % 4], W3[i % 3], hT, KD, s["qkv_mm"])
            pe.wait_ge(s["qkv_evicted"], 6)
            for n in range(NT):
                mm = pe.transpose(ps[2][:, n * P:(n + 1) * P], qst[1][:, n * P:(n + 1) * P], ident[:, :])
            mm.then_inc(s["vat_mm"], 1)
            pe.wait_ge(s["vat_evicted"], 1)
            pe.wait_ge(s["sol_row"], 2 * (C - 1))
            XY = [banks[:, z, 0:NPAIR * HD] for z in range(2)]
            US = [banks[:, 2 + z, :] for z in range(2)]
            def scores(i, g, heads):
                blk = 2 * i + g
                for h in heads:
                    e, hh = h % 2, h // 2
                    if h < 2:
                        pe.wait_ge(s["pt_out"], 3 * blk + FREE)
                    else:
                        pe.wait_ge(s["sc_out"], 4 * blk + h - 1)
                    pe.matmul(banks[:, 4 + h % 2, 0:BAND], qs[64 * e:64 * e + 64, 2 * g + hh, :],
                              ks[64 * e:64 * e + 64, g, :], start=True, stop=True).then_inc(s["sc_mm"], 1)

            def probabilities(i, g):
                pe.wait_ge(s["p_norm"], 2 * i + g + 1)
                for kb in range(3):
                    for h in range(GH):
                        e, hh = h % 2, h // 2
                        mm = pe.transpose(banks[:, 4 + kb, (2 * e + hh) * P:(2 * e + hh + 1) * P],
                                          Pr[:, h, kb * P:(kb + 1) * P], ident[:, :])
                    mm.then_inc(s["pt_mm"], 1)

            def values(i, g):
                blk = 2 * i + g
                pe.wait_ge(val_full, 16 * i + 16)
                pe.wait_ge(s["pt_out"], 3 * blk + 3 + FREE)
                pe.wait_ge(s["o_out"], blk + FREE)
                for e in range(2):
                    for kb in range(3):
                        mm = pe.matmul(banks[64 * e:64 * e + 64, 7, 0:2 * P], vs[:, kb, HD * g:HD * g + HD],
                                       PT[:, kb, e].rearrange("p a b -> p (a b)"), start=(kb == 0), stop=(kb == 2))
                mm.then_inc(s["o_mm"], 1)

            with pe.Fori(0, NC // 4) as i:
                for q in range(4):
                    slot, cc, g = q // 2, q % 2, q // 2
                    n = 4 * i + q
                    if cc == 0:
                        pe.wait_ge(scan_full[slot], 16 * 18 * i + 16 * 18)
                    for z in range(2):
                        c2 = cc if z == 0 else 1 - cc
                        pe.wait_ge(sz[z]["Y_out"], n + FREE)
                        for part in range(2):
                            if part == 1:
                                pe.wait_ge(sz[z]["S_new"], n + 1)
                                settled()
                            for j in range(NPAIR):
                                for e in range(2):
                                    h = slice(64 * e, 64 * e + 64)
                                    hk = slice(64 * e + C, 64 * e + 2 * C)
                                    out = XY[z][h, j * HD:(j + 1) * HD]
                                    if part == 0:
                                        mm = pe.matmul(out, Gs[slot][hk, z, j, c2 * 64:c2 * 64 + 64],
                                                       UV[slot][hk, z, c2, j, :], start=(j == 0), stop=False,
                                                       skip_group_check=True)
                                    else:
                                        mm = pe.matmul(out, ARs[slot][h, z, j, c2 * 64:c2 * 64 + 64],
                                                       S[h, z, j, :], start=False, stop=(j == NPAIR - 1),
                                                       skip_group_check=True)
                        mm.then_inc(sz[z]["X_mm"], 1)
                    if cc == 0:
                        pe.wait_ge(qk_full, 48 * i + 48)
                        scores(i, g, (0, 1))
                    else:
                        probabilities(i, g)
                    for z in range(2):
                        c2 = cc if z == 0 else 1 - cc
                        pe.wait_ge(sz[z]["X_out"], n + 1)
                        pe.wait_ge(sz[z]["S_add"], n + FREE)
                        settled()
                        for j in range(NPAIR):
                            for e in range(2):
                                hu = slice(64 * e, 64 * e + C)
                                mm = pe.matmul(US[z][hu, j * HD:(j + 1) * HD], TIs[slot][hu, z, j, c2 * C:c2 * C + C],
                                               Xs[hu, z, j * HD:(j + 1) * HD], start=True, stop=True)
                        mm.then_inc(sz[z]["U_mm"], 1)
                    if cc == 0:
                        scores(i, g, (2, 3))
                    else:
                        values(i, g)
                    for z in range(2):
                        c2 = cc if z == 0 else 1 - cc
                        pe.wait_ge(sz[z]["U_e0"], n + 1)
                        pe.wait_ge(sz[z]["U_e1"], n + 1)
                        settled()
                        for j in range(NPAIR):
                            for e in range(2):
                                h = slice(64 * e, 64 * e + 64)
                                mm = pe.matmul(US[z][h, 256 + j * HD:256 + (j + 1) * HD],
                                               BKs[slot][h, z, j, c2 * HD:c2 * HD + HD], UV[slot][h, z, c2, j, :],
                                               start=True, stop=True)
                        mm.then_inc(sz[z]["S_mm"], 1)
                        for j in range(NPAIR):
                            for e in range(2):
                                hu = slice(64 * e, 64 * e + C)
                                mm = pe.matmul(XY[z][64 * e + C:64 * e + 2 * C, j * HD:(j + 1) * HD],
                                               Gs[slot][hu, z, j, c2 * 64 + C:c2 * 64 + 2 * C],
                                               UV[slot][hu, z, c2, j, :], start=False, stop=True,
                                               skip_group_check=True)
                        mm.then_inc(sz[z]["Y_mm"], 1)
            pe.wait_ge(s["y_normed"], NT + FREE)
            pe.wait_ge(s["gw_loaded"], 16)
            pe.wait_ge(s["o_out"], 2 * NT + FREE)
            for z in range(2):
                pe.wait_ge(sz[z]["Y_out"], NC + FREE)
                pe.wait_ge(sz[z]["S_add"], NC + FREE)
            for j in range(NPAIR):
                if j >= 2:
                    pe.wait_ge(s["y_gated"], j - 1)
                a0, a1 = ps[2 * (j % 2)], ps[2 * (j % 2) + 1]
                for n in range(NT):
                    mm = pe.transpose(a0[:, n * P:(n + 1) * P], yn[:, n, j * P:(j + 1) * P], ident[:, :])
                mm.then_inc(s["yt_mm"], 1)
                whole(a1, gw[:, j * P:(j + 1) * P], sgT, s["gt_mm"])
            pe.wait_ge(s["y_gated"], NPAIR)
            pe.wait_ge(sp_s["att_lo"], KD - NPAIR)
            with pe.Fori(0, KD // 2) as i:
                for slot in range(2):
                    pe.wait_ge(wt["lo"][slot], i + 1 + FREE)
                    pe.wait_ge(added[slot], i + FREE)
                    split_dense(ps[slot], slot, h_hi, h_lo, KD, [(k, sp_s["o_lo"], k + 1) for k in range(NPAIR)])
            for slot in range(2):
                pe.wait_ge(added[slot], KD // 2 + FREE)
            norm(1, acc)
            pe.wait_ge(ns["root"], 2)
            for gi, (f0, fn) in enumerate(GROUPS):
                for slot in range(2):
                    pe.wait_ge(added[slot], KD // 2 * (gi + 1) + FREE)
                with pe.Fori(0, fn // 2) as i:
                    for b in range(2):
                        n = 2 * i + (b + first_unit(f0))
                        pe.wait_ge(gu_done[b], i + f0 // 2 + FREE)
                        for slot in range(2):
                            pe.wait_ge(wt["lo"][slot], n + 1 + FREE)
                            split_dense(ps[2 * b + slot], slot, h_hi, h_lo, KD,
                                        [(k, sp_s["h_lo"], k + 1) for k in range(KD)] if slot == 0 else ())
                pe.wait_ge(gu_done[0], (f0 + fn) // 2 + FREE)
                with pe.Fori(0, KD // 2) as i:
                    for slot in range(2):
                        pe.wait_ge(wt["lo"][slot], i + (first_unit(f0) + fn) + 1 + FREE)
                        pe.wait_ge(added[slot], i + KD // 2 * (gi + 1) + FREE)
                        split_dense(ps[slot], slot, g_hi, g_lo, fn,
                                    ((0, g_split[0], (f0 + fn) // 2 + FREE), (fn - 1, g_split[1], (f0 + fn) // 2 + FREE)))
            for slot in range(2):
                pe.wait_ge(added[slot], KD // 2 * (len(GROUPS) + 1) + FREE)
            norm(2, hT[:, 7, :])

        @block.scalar
        def _(act):
            for k in range(1, KD, 2):
                act.dma_start(xT[:, k, :], a["xT"][:, k, :]).then_inc(s["x_loaded"], 16)

            def norm(n, ac, sq, root):
                for k in range(KD):
                    if k >= 3:
                        act.wait_ge(ns["summed"], n * (KD - 1) + k - 2)
                    act.activation(ac if k == 0 else sq[k % 2], xT[:, k, :], ACT.Square).then_inc(ns["squared"], 1)
                act.wait_ge(ns["ms_mm"], n + 1)
                act.activation(root, ps[0], ACT.Sqrt, bias=eps[:, 0:1], scale=1.0 / D).then_inc(ns["root"], 1)

            act.wait_ge(s["x_loaded"], 16 * KD)
            act.wait_ge(s["consts_made"], 4)
            norm(0, acc, sqb, rs)
            for i, dst in enumerate((lora, sgT[:, :])):
                act.wait_ge(s["p_mm"], i + 1 + FREE)
                act.activation(dst, ps[i], ACT.Copy, scale=c0[:, 12 + i:13 + i]).then_inc(s["p_scaled"], 1)
            act.wait_ge(s["p_shifted"], 1)
            act.activation(lora[0:64, :], lora[0:64, :], ACT.Tanh).then_inc(s["lora_tanh"], 1)
            act.wait_ge(s["p_shifted"], 2)
            act.activation(sgT[:, :], sgT[:, :], ACT.Sigmoid).then_inc(s["gate_sig"], 1)
            with act.Fori(0, NPAIR) as j:
                act.wait_ge(s["gram_mm"], 2 * j + FREE)
                act.wait_ge(s["G_ready"], 2 * j + FREE)
                for i, dst in enumerate((rT, kT, vT)):
                    act.wait_ge(s["p_mm"], 3 * j + 3 + i + FREE)
                    act.activation(dst, ps[i], ACT.Copy, scale=c0[:, bass.ds(j + 4 * i, 1)])\
                       .then_inc(s["p_scaled"], 1)
                act.wait_ge(s["pad_zero"], 2)
                for z, slot in ((0, 3), (1, 0)):
                    act.wait_ge(s[f"dz{z}_mm"], j + 1)
                    act.activation(chunked(L[z], z, False), ps[slot].rearrange("p (c t) -> p c t", t=C), ACT.Sigmoid,
                                   bias=col("w0", j + 4 * z)).then_inc(s[f"sig{z}"], 1)
                act.wait_ge(s["ic_mm"], j + 1 + FREE)
                act.activation(aT, ps[1], ACT.Sigmoid, bias=col("a0", j)).then_inc(s["a_ready"], 1)
                act.wait_ge(s["vt_mm"], j + 1)
                act.wait_ge(s["v_stored"], 16 * j + FREE)
                act.activation(vts.rearrange("p a b -> p (a b)"), ps[2], ACT.Copy).then_inc(s["vts_ready"], 1)
                act.wait_ge(s["kk_ready"], j + 1)
                act.activation(sqT, kkT, ACT.Square).then_inc(s["kk_sq"], 1)
                for z in range(2):
                    act.wait_ge(s[f"L{z}_ready"], j + 1)
                    act.activation(E[z], L[z], ACT.Exp, scale=-DECAY).then_inc(s[f"E{z}_ready"], 1)
                    act.activation(Ei[z], L[z], ACT.Exp, scale=DECAY).then_inc(s[f"E{z}_ready"], 1)
                act.wait_ge(s["ss_mm"], j + 1)
                act.activation(sqT, ps[3], ACT.Sqrt).then_inc(s["nrm_ready"], 1)
                for z in range(2):
                    act.wait_ge(s["bkt_mm"], 2 * j + z + 1 + FREE)
                    act.wait_ge(s["BK_stored"], 128 * j + 64 * z + FREE)
                    act.activation(BKt[:, 0:8].rearrange("p a b -> p (a b)"), ps[3], ACT.Copy).then_inc(s["bkt_half"], 1)
                    act.activation(BKt[:, 8:16].rearrange("p a b -> p (a b)"), ps[0], ACT.Copy)\
                       .then_inc(s["bkt_ready"], 1)
            act.wait_ge(s["BK_stored"], 16 * 8 * NPAIR + FREE)
            act.wait_ge(s["AR_stored"], 16 * 2 * NPAIR + FREE)
            act.wait_ge(s["G_stored"], 16 * 2 * NPAIR + FREE)
            act.wait_ge(s["v_stored"], 16 * NPAIR + FREE)
            for i in range(6):
                act.wait_ge(s["qkv_mm"], i + 1)
                if i >= 2:
                    act.wait_ge(s[("q_stored", "q_stored2")[i % 2]], 16 * (i // 2))
                act.activation(qst[i % 2], ps[i % 4], ACT.Copy, scale=(HD ** -0.5 if i < 4 else 1.0))\
                   .then_inc(s["qkv_evicted"], 1)
                act.wait_ge(s["qkv_evicted"], i + 1)
                if i < 4:
                    act.dma_start(q_d[i], qst[i % 2]).then_inc(s[("q_stored", "q_stored2")[i % 2]], 16)
                elif i == 4:
                    for g in range(2):
                        for e in range(2):
                            act.dma_start(kk_d[g, 64 * e:64 * e + 64, P:P + T], qst[0][64 * g:64 * g + 64, :])\
                               .then_inc(s["q_stored"], 16)
            act.wait_ge(s["vat_mm"], 1)
            act.activation(vast.rearrange("p a b -> p (a b)"), ps[2], ACT.Copy).then_inc(s["vat_evicted"], 1)
            act.wait_ge(s["vat_evicted"], 1)
            for n in range(4):
                act.dma_start(va_d[(1 + 2 * n) * P:(3 + 2 * n) * P].rearrange("(b p) n -> p b n", p=P),
                              vast[:, 2 * n:2 * n + 2]).then_inc(s["q_stored"], 16)
            act.wait_ge(s["q_stored"], 16 * 10)
            act.wait_ge(s["q_stored2"], 32)
            act.wait_ge(s["TI_stored"], 16 * 4 * NPAIR)
            with act.Fori(0, NC // 4) as i:
                for q in range(4):
                    slot, cc, g = q // 2, q % 2, q // 2
                    n = 4 * i + q
                    blk = 2 * i + g
                    act.wait_ge(sz[1]["X_mm"], n + 1)
                    act.activation(Xs[:, 1], banks[:, 1, 0:256], ACT.Copy).then_inc(sz[1]["X_out"], 1)
                    if cc == 1:
                        act.wait_ge(s["o_mm"], blk + FREE)
                        for kb in range(3):
                            act.wait_ge(s["pt_mm"], 3 * blk + kb + 1 + FREE)
                            act.activation(PT[:, kb].rearrange("p a b c -> p (a b c)"), banks[:, 4 + kb, :], ACT.Copy)\
                               .then_inc(s["pt_out"], 1)
                    for z in range(2):
                        c2 = cc if z == 0 else 1 - cc
                        act.wait_ge(sz[z]["U_mm"], n + 1)
                        act.activation(UV[slot][64:64 + C, z, c2].rearrange("p a b -> p (a b)"),
                                       banks[64:64 + C, 2 + z, 0:256], ACT.Copy).then_inc(sz[z]["U_e1"], 1)
                    if cc == 1:
                        act.wait_ge(s["o_mm"], blk + 1 + FREE)
                        act.activation(oT[:, NPAIR + 2 * g:NPAIR + 2 * g + 2, bass.ds(i * P, P)],
                                       banks[:, 7, 0:2 * P].rearrange("p (a b) -> p a b", a=2), ACT.Copy)\
                           .then_inc(s["o_out"], 1)
                    for z in range(2):
                        act.wait_ge(sz[z]["Y_mm"], n + 1)
                        if z == 0:
                            act.wait_ge(ys_stored[q % 2], 64 * (2 * i + q // 2) + FREE)
                        act.activation(Ys[q % 2][:, z], banks[:, z, 0:256], ACT.Copy).then_inc(sz[z]["Y_out"], 1)
                    if cc == 0:
                        act.wait_ge(s["nm_ready"], blk + 1)
                        act.wait_ge(s["pt_mm"], 3 * blk + FREE)
                        for h in range(GH):
                            act.activation(Pr[:, h, :], Lg[:, h, :], ACT.Exp, bias=nm[:, h:h + 1],
                                           accum_out=rsum[:, h:h + 1]).then_inc(s["p_exp"], 1)
                        act.wait_ge(s["mx_sink"], 2 * blk + 2)
                        act.activation(es, mx, ACT.Exp).then_inc(s["s_exp"], 1)
            with act.Fori(0, NT) as t:
                act.wait_ge(s["y_cent"], t + 1)
                act.activation(ysq, ycen, ACT.Square).then_inc(s["y_sq"], 1)
                act.wait_ge(s["y_var"], t + 1)
                act.activation(stat[:, 2], stat[:, 1], ACT.Sqrt, bias=eps[:, 1:2], scale=1.0 / HD).then_inc(s["y_sd"], 1)
            def weights_hi(slot, n):
                act.wait_ge(wt["full"][slot], 16 * n + 16)
                act.wait_ge(wt["used"][slot], n + FREE)
                act.activation(w_hi[slot][:, :, :], w_raw[slot], ACT.Copy).then_inc(wt["hi"][slot], 1)

            for k in range(NPAIR, KD):
                act.activation(h_hi[:, k, :], oT[:, k, :], ACT.Copy).then_inc(sp_s["att_hi"], 1)
            for slot in range(2):
                weights_hi(slot, 0)
            for j in range(NPAIR):
                act.wait_ge(s["y_gated"], j + 1)
                act.activation(h_hi[:, j, :], oT[:, j, :], ACT.Copy).then_inc(sp_s["o_hi"], 1)
            with act.Fori(0, KD // 2) as i:
                for slot in range(2):
                    weights_hi(slot, i + 1)
            for slot in range(2):
                act.wait_ge(added[slot], KD // 2 + FREE)
            norm(1, acc, sqb, rs)
            for k in range(KD):
                act.wait_ge(ns["scaled"], KD + k + 1)
                act.activation(h_hi[:, k, :], hT[:, k, :], ACT.Copy).then_inc(sp_s["h_hi"], 1)
            act.wait_ge(ns["scaled"], 2 * KD)
            for gi, (f0, fn) in enumerate(GROUPS):
                with act.Fori(0, fn // 2) as i:
                    for b in range(2):
                        f = 2 * i + (f0 + b)
                        n = 2 * i + (b + first_unit(f0))
                        act.wait_ge(wt["used"][0], n + 1 + FREE)
                        act.wait_ge(g_split[b], i + f0 // 2 + FREE)
                        act.activation(ga[b], ps[2 * b], ACT.Identity, bias=col("cb", f), scale=col("cw1", f))\
                           .then_inc(fs["scaled"], 1)
                        weights_hi(0, n + 1)
                        act.wait_ge(fs["c2"], f + 1)
                        act.activation(ga[b], ga[b], ACT.Gelu).then_inc(fs["gelu"], 1)
                        weights_hi(1, n + 1)
                        act.wait_ge(gu_done[b], i + (f0 // 2 + 1) + FREE)
                        act.activation(g_hi[:, bass.ds(2 * i + b, 1), :].rearrange("p o t -> p (o t)"), ga[b], ACT.Copy)\
                           .then_inc(fs["g_hi"], 1)
                with act.Fori(0, KD // 2 - (gi == len(GROUPS) - 1)) as i:
                    for slot in range(2):
                        weights_hi(slot, i + (first_unit(f0) + fn + 1))
            for slot in range(2):
                act.wait_ge(added[slot], KD // 2 * (len(GROUPS) + 1) + FREE)
            norm(2, hT[:, 7, :], (hT[:, 5, :], hT[:, 6, :]), work[:, 0:T])

        @block.gpsimd
        def _(pool):
            for z in range(2):
                v = L[z].rearrange("p (c t) -> p c t", t=CP)
                pool.wait_ge(ns["scaled"], KD)
                pool.memset(v[:, :, 0:1] if z == 0 else v[:, :, C:C + 1], 0.0).then_inc(s["pad_zero"], 1)

            with pool.Fori(0, NPAIR) as j:
                for z in range(2):
                    pool.wait_ge(s["kp_ready"], j + 1)
                    pool.wait_ge(s[f"E{z}_ready"], 2 * j + 2)
                    pool.wait_ge(s["bkt_mm"], 2 * j + z + FREE)
                    pool.tensor_tensor(BK[:, :, 1, :], kT.rearrange("p (c t) -> p c t", t=C), chunked(Ei[z], z, False),
                                       ALU.mult).then_inc(s["k_prod"], 1)
            pool.wait_ge(s["BK_stored"], 16 * 8 * NPAIR + FREE)
            pool.wait_ge(s["v_stored"], 16 * NPAIR + FREE)
            pool.wait_ge(s["G_stored"], 16 * 2 * NPAIR + FREE)
            pool.memset(zero, 0.0).then_inc(s["zero_made"], 1)
            pool.wait_ge(s["zero_made"], 1)
            for at in (0, P + T):
                for g in range(2):
                    pool.dma_start(kk_d[g, :, at:at + P], zero).then_inc(s["z_stored"], 16)
                pool.dma_start(va_d[at:at + P, :], zero).then_inc(s["z_stored"], 16)
            for z in range(2):
                pool.wait_ge(s["sol_row"], (z + 1) * (C - 1))
                for j in range(NPAIR):
                    for e in range(2):
                        pool.dma_start(TI_d[z, j, e].rearrange("s (c t) -> c s t", t=C), TI[z][C * j:C * (j + 1), e])\
                            .then_inc(s["TI_stored"], 16)

            for k in range(NPAIR, KD):
                pool.wait_ge(sp_s["att_hi"], k - NPAIR + 1)
                pool.tensor_tensor(h_lo[:, k, :], oT[:, k, :], h_hi[:, k, :].bitcast(F32), ALU.subtract)\
                    .then_inc(sp_s["att_lo"], 1)

        @block.vector
        def _(dve):
            tt, ts, stt = dve.tensor_tensor, dve.tensor_scalar, dve.scalar_tensor_tensor

            def low_part(out, x, hi, hi_ready, count, done):
                dve.wait_ge(hi_ready, count)
                tt(out, x, hi.bitcast(F32), ALU.subtract).then_inc(done, 1)

            def weights_lo(slot, n):
                low_part(w_lo[slot][:, :, :], w_raw[slot], w_hi[slot][:, :, :], wt["hi"][slot], n + 1, wt["lo"][slot])

            def norm(n, ac, sq, root, gain):
                for k in range(1, KD):
                    dve.wait_ge(ns["squared"], n * KD + k + 1)
                    if k >= 2:
                        dve.wait_ge(ns["summed"], n * (KD - 1) + k - 1)
                    tt(ac, ac, sq[k % 2], ALU.add).then_inc(ns["summed"], 1)
                dve.wait_ge(ns["root"], n + 1)
                dve.reciprocal(root, root).then_inc(ns["rstd"], 1)
                dve.wait_ge(ns["rstd"], n + 1)
                for k in range(KD):
                    stt(hT[:, k, :], xT[:, k, :], col(gain, k), root, ALU.mult, ALU.mult).then_inc(ns["scaled"], 1)
                    if n == 1 and k:
                        low_part(h_lo[:, k - 1, :], hT[:, k - 1, :], h_hi[:, k - 1, :], sp_s["h_hi"], k, sp_s["h_lo"])
                if n == 1:
                    low_part(h_lo[:, KD - 1, :], hT[:, KD - 1, :], h_hi[:, KD - 1, :], sp_s["h_hi"], KD, sp_s["h_lo"])

            dve.memset(eps[:, 0:1], NORM_EPS).then_inc(s["consts_made"], 1)
            dve.memset(eps[:, 1:2], LNX_EPS).then_inc(s["consts_made"], 1)
            dve.wait_ge(s["consts_loaded"], 16 * NCONST)
            mp, mn = par[:, COLS["mu_prev"]:COLS["mu_prev"] + 14], par[:, COLS["mu_next"]:COLS["mu_next"] + 14]
            ts(c0[:, :], mp, -1.0, 1.0, ALU.mult, ALU.add).then_inc(s["c0_part"], 1)
            dve.wait_ge(s["c0_part"], 1)
            tt(c0[:, :], c0[:, :], mn, ALU.subtract).then_inc(s["consts_made"], 1)
            ka = par[:, COLS["k_a"]:COLS["k_a"] + NPAIR]
            ts(oka[:, :], ka, -1.0, 1.0, ALU.mult, ALU.add).then_inc(s["consts_made"], 1)
            norm(0, acc, sqb, rs, "ln1")

            for i, dst in enumerate((lora, sgT[:, :])):
                dve.wait_ge(s["p_scaled"], i + 1)
                stt(dst[:, 1:T], ps[i][:, 0:T - 1], col("mu_prev", 12 + i), dst[:, 1:T], ALU.mult, ALU.add)\
                    .then_inc(s["p_shift1"], 1)
                dve.wait_ge(s["p_shift1"], i + 1)
                stt(dst[:, 0:T - 1], ps[i][:, 1:T], col("mu_next", 12 + i), dst[:, 0:T - 1], ALU.mult, ALU.add)\
                    .then_inc(s["p_shifted"], 1)

            with dve.Fori(0, NPAIR) as j:
                for i, dst in enumerate((rT, kT, vT)):
                    dve.wait_ge(s["p_scaled"], 3 * j + 3 + i)
                    stt(dst[:, 1:T], ps[i][:, 0:T - 1], col("mu_prev", j + 4 * i), dst[:, 1:T], ALU.mult, ALU.add)\
                        .then_inc(s["p_shift1"], 1)
                    dve.wait_ge(s["p_shift1"], 3 * j + 3 + i)
                    stt(dst[:, 0:T - 1], ps[i][:, 1:T], col("mu_next", j + 4 * i), dst[:, 0:T - 1], ALU.mult, ALU.add)\
                        .then_inc(s["p_shifted"], 1)
                dve.wait_ge(s["p_shifted"], 3 * j + 4)
                ts(kkT, kT, col("k_k", j), None, ALU.mult).then_inc(s["kk_ready"], 1)
                for z in range(2):
                    dve.wait_ge(s[f"sig{z}"], j + 1)
                    order = slice(None) if z == 0 else slice(None, None, -1)
                    dve.tensor_tensor_scan(L[z][:, order], reset[:, z, order], L[z][:, order], 0.0, ALU.mult, ALU.add)\
                        .then_inc(s[f"L{z}_ready"], 1)
                dve.wait_ge(s["a_ready"], j + 1)
                dve.wait_ge(s["kk_ready"], j + 1)
                ts(tpT, aT, col("k_a", j), oka[:, bass.ds(j, 1)], ALU.mult, ALU.add).then_inc(s["ka_fac"], 1)
                dve.wait_ge(s["ka_fac"], j + 1)
                tt(kT, kT, tpT, ALU.mult).then_inc(s["kp_ready"], 1)
                dve.wait_ge(s["kp_ready"], j + 1)
                dve.wait_ge(s["p_shifted"], 3 * j + 3)
                stt(tpT, rT, col("r_k", j), kT, ALU.mult, ALU.mult).then_inc(s["bon_in"], 1)
                dve.wait_ge(s["nrm_ready"], j + 1)
                ts(sqT, sqT, L2_EPS, None, ALU.max).then_inc(s["nrm_max"], 1)
                dve.wait_ge(s["nrm_max"], j + 1)
                dve.reciprocal(sqT, sqT).then_inc(s["nrm_rec"], 1)
                dve.wait_ge(s["nrm_rec"], j + 1)
                stt(kkT, kkT, -1.0, sqT, ALU.mult, ALU.mult).then_inc(s["nk_ready"], 1)
                dve.wait_ge(s["nk_ready"], j + 1)
                stt(bT, kkT, -1.0, aT, ALU.mult, ALU.mult).then_inc(s["b_ready"], 1)
                dve.wait_ge(s["p_shifted"], 3 * j + 5)
                dve.wait_ge(s["bon_mm"], j + 1)
                tt(bonusT[:, bass.ds(j, 1), :].rearrange("p o t -> p (o t)"), ps[0], vT, ALU.mult)\
                    .then_inc(s["bon_out"], 1)
                dve.wait_ge(s["b_ready"], j + 1)
                for z in range(2):
                    dve.wait_ge(s[f"E{z}_ready"], 2 * j + 2)
                    last = E[z].rearrange("p (c t) -> p c t", t=CP)[:, :, (C if z == 0 else 0)]
                    dve.tensor_copy(PC[:, z, bass.ds(j, 1), :].rearrange("p o c -> p (o c)"), last)
                    if z == 0:
                        dve.wait_ge(s["AR_stored"], 32 * j + FREE)
                    else:
                        dve.wait_ge(s["AR_stored"], 32 * j + 16 + FREE)
                    dve.wait_ge(s["bkt_mm"], 2 * j + z + FREE)
                    by_chunk = lambda x: x.rearrange("p (c t) -> p c t", t=C)
                    tt(AR[:, :, 0, :], by_chunk(kkT), chunked(E[z], z, True), ALU.mult)
                    tt(AR[:, :, 1, :], by_chunk(rT), chunked(E[z], z, False), ALU.mult)
                    tt(BK[:, :, 0, :], by_chunk(bT), chunked(Ei[z], z, False), ALU.mult).then_inc(s["ab_ready"], 1)
                    dve.wait_ge(s["gram_mm"], 2 * j + z + 1 + FREE)
                    dve.wait_ge(s["G_stored"], 32 * j + 16 * z + FREE)
                    for b in range(2):
                        tt(G[:, 16 * b:16 * b + 16, :], ps[1 + b].rearrange("p (c t) -> p c t", t=2 * C),
                           gmask[:, z, :].unsqueeze(1).broadcast_to([P, 16, 2 * C]), ALU.mult)\
                            .then_inc(s["G_half"] if b == 0 else s["G_ready"], 1)

            dve.wait_ge(s["BK_stored"], 16 * 8 * NPAIR + FREE)
            dve.wait_ge(s["AR_stored"], 16 * 2 * NPAIR + FREE)
            dve.wait_ge(s["G_stored"], 16 * 2 * NPAIR + FREE)
            dve.wait_ge(s["v_stored"], 16 * NPAIR + FREE)
            for z in range(2):
                dve.memset(TI[z], 0.0).then_inc(s["TI_init"], 1)
            dve.wait_ge(s["TI_init"], 2)
            for z in range(2):
                diag = TI[z].rearrange("p e s t -> p e (s t)")[:, :, 0:C * C:C + 1]
                dve.memset(diag, 1.0).then_inc(s["TI_init"], 1)
            dve.wait_ge(s["TI_init"], 4)
            dve.wait_ge(s["M_loaded"], 16 * 16)
            step = 0
            for z in range(2):
                for n in range(1, C):
                    row = C - 1 - n if z == 0 else n
                    lo = row + 1 if z == 0 else 0
                    m = M[z][:, :, row, lo:lo + n].unsqueeze(2).broadcast_to([P, 2, n, n])
                    known = TI[z][:, :, lo:lo + n, lo:lo + n].rearrange("p e s t -> p e t s")
                    out = prod[:, :, 0:n, 0:n]
                    if step:
                        dve.wait_ge(s["sol_row"], step)
                    tt(out, m, known, ALU.mult).then_inc(s["sol_prod"], 1)
                    step += 1
                    dve.wait_ge(s["sol_prod"], step)
                    dve.tensor_reduce(TI[z][:, :, row, lo:lo + n], out, AX.X, ALU.add).then_inc(s["sol_row"], 1)

            dve.wait_ge(s["TI_stored"], 16 * 4 * NPAIR)
            dve.wait_ge(s["vat_evicted"], 1)
            dve.wait_ge(s["q_stored"], 16 * 10)
            dve.wait_ge(s["z_stored"], 16 * 6)
            dve.wait_ge(s["q_stored2"], 32)
            for z in range(2):
                dve.memset(S[:, z], 0.0).then_inc(sz[z]["S_new"], 1)
            def logits(i, g, heads):
                blk = 2 * i + g
                for h in heads:
                    dve.wait_ge(s["sc_mm"], 4 * blk + h + 1)
                    stt(Lg[:, h, :], nd, slope[:, GH * g + h:GH * g + h + 1], banks[:, 4 + h % 2, 0:BAND],
                        ALU.mult, ALU.add).then_inc(s["sc_out"], 1)

            def maxima(i, g):
                blk = 2 * i + g
                dve.wait_ge(s["sc_out"], 4 * blk + 4)
                dve.tensor_reduce(nm, Lg, AX.X, ALU.max).then_inc(s["mx_red"], 1)
                dve.wait_ge(s["mx_red"], blk + 1)
                dve.wait_ge(s["s_exp"], blk + FREE)
                tt(mx, nm, sink[:, GH * g:GH * g + GH], ALU.max).then_inc(s["mx_sink"], 1)
                dve.wait_ge(s["mx_sink"], 2 * blk + 1)
                ts(nm, mx, -1.0, None, ALU.mult).then_inc(s["nm_ready"], 1)
                dve.wait_ge(s["nm_ready"], blk + 1)
                tt(mx, sink[:, GH * g:GH * g + GH], mx, ALU.subtract).then_inc(s["mx_sink"], 1)

            def normalise(i, g):
                blk = 2 * i + g
                dve.wait_ge(s["p_exp"], 4 * blk + 4 + FREE)
                dve.wait_ge(s["s_exp"], blk + 1 + FREE)
                tt(rsum, rsum, es, ALU.add).then_inc(s["sum_all"], 1)
                dve.wait_ge(s["sum_all"], blk + 1)
                dve.reciprocal(rinv, rsum).then_inc(s["inv_ready"], 1)
                dve.wait_ge(s["inv_ready"], blk + 1)
                tt(Pr, Pr, rinv.unsqueeze(2).broadcast_to([P, GH, BAND]), ALU.mult).then_inc(s["p_norm"], 1)

            with dve.Fori(0, NC // 4) as i:
                for q in range(4):
                    slot, cc, g = q // 2, q % 2, q // 2
                    n = 4 * i + q
                    dve.wait_ge(sz[0]["X_mm"], n + 1)
                    dve.tensor_copy(Xs[:, 0], banks[:, 0, 0:256]).then_inc(sz[0]["X_out"], 1)
                    if cc == 0:
                        dve.wait_ge(s["p_exp"], 8 * i + 4 * g + FREE)
                        logits(i, g, (0, 1))
                    else:
                        normalise(i, g)
                    for z in range(2):
                        c2 = cc if z == 0 else 1 - cc
                        dve.wait_ge(sz[z]["U_mm"], n + 1)
                        dve.tensor_copy(UV[slot][0:C, z, c2].rearrange("p a b -> p (a b)"),
                                        banks[0:C, 2 + z, 0:256]).then_inc(sz[z]["U_e0"], 1)
                    if cc == 0:
                        logits(i, g, (2, 3))
                        maxima(i, g)
                    for z in range(2):
                        c = n if z == 0 else (i * -4 + (NC - 1 - q))
                        dve.wait_ge(sz[z]["S_mm"], n + 1)
                        tt(St[:, z], S[:, z], banks[:, 2 + z, 256:512].rearrange("p (j i) -> p j i", j=NPAIR), ALU.add)\
                            .then_inc(sz[z]["S_add"], 1)
                        dve.wait_ge(sz[z]["S_add"], n + 1 + FREE)
                        tt(S[:, z], St[:, z], PC[:, z, :, bass.ds(c, 1)].broadcast_to([P, NPAIR, HD]), ALU.mult)\
                            .then_inc(sz[z]["S_new"], 1)

            dve.wait_ge(s["o_out"], 2 * NT + FREE)
            heads = lambda x: x.rearrange("p (h n) -> p h n", n=HD)
            spread = lambda x: x.unsqueeze(2).broadcast_to([P, AH, HD])
            with dve.Fori(0, NT // 2) as i:
                for slot in range(2):
                    t = 2 * i + slot
                    dve.wait_ge(y_full[slot], 16 * i + 16)
                    tt(ysum, yin[slot][:, 0], yin[slot][:, 1], ALU.add).then_inc(yin_used[slot], 1)
                    dve.wait_ge(yin_used[slot], i + 1)
                    dve.tensor_reduce(stat[:, 0], heads(ysum), AX.X, ALU.add).then_inc(s["y_summed"], 1)
                    dve.wait_ge(s["y_summed"], t + 1)
                    ts(stat[:, 0], stat[:, 0], 1.0 / HD, None, ALU.mult).then_inc(s["y_mean"], 1)
                    dve.wait_ge(s["y_mean"], t + 1)
                    dve.wait_ge(s["y_normed"], t + FREE)
                    tt(heads(ycen), heads(ysum), spread(stat[:, 0]), ALU.subtract).then_inc(s["y_cent"], 1)
                    dve.wait_ge(s["y_sq"], t + 1)
                    dve.tensor_reduce(stat[:, 1], heads(ysq), AX.X, ALU.add).then_inc(s["y_var"], 1)
                    dve.wait_ge(s["y_sd"], t + 1)
                    dve.reciprocal(stat[:, 3], stat[:, 2]).then_inc(s["y_inv"], 1)
                    dve.wait_ge(s["y_inv"], t + 1)
                    tt(heads(yn[:, bass.ds(t, 1), :].rearrange("p o n -> p (o n)")), heads(ycen), spread(stat[:, 3]),
                       ALU.mult).then_inc(s["y_normed"], 1)
            for j in range(NPAIR):
                dve.wait_ge(s["yt_mm"], j + 1)
                ts(ot1, ps[2 * (j % 2)], col("lnx_g", j), col("lnx_b", j), ALU.mult, ALU.add).then_inc(s["y_aff"], 1)
                dve.wait_ge(s["y_aff"], j + 1)
                tt(ot1, ot1, bonusT[:, j, :], ALU.add).then_inc(s["y_bon"], 1)
                dve.wait_ge(s["y_bon"], j + 1)
                dve.wait_ge(s["gt_mm"], j + 1)
                tt(oT[:, j, :], ot1, ps[2 * (j % 2) + 1], ALU.mult).then_inc(s["y_gated"], 1)
                dve.wait_ge(s["y_gated"], j + 1)
                if j:
                    low_part(h_lo[:, j - 1, :], oT[:, j - 1, :], h_hi[:, j - 1, :], sp_s["o_hi"], j, sp_s["o_lo"])
            low_part(h_lo[:, NPAIR - 1, :], oT[:, NPAIR - 1, :], h_hi[:, NPAIR - 1, :], sp_s["o_hi"], NPAIR, sp_s["o_lo"])

            def add_products(n0, last):
                def one(i, slot, split):
                    x = xT[:, bass.ds(2 * i + slot, 1), :].rearrange("p o t -> p (o t)")
                    dve.wait_ge(wt["used"][slot], i + (n0 + 1) + FREE)
                    if split:
                        weights_lo(slot, i + (n0 + 1))
                    tt(x, x, ps[slot], ALU.add).then_inc(added[slot], 1)

                with dve.Fori(0, KD // 2 - last) as i:
                    for slot in range(2):
                        one(i, slot, True)
                if last:
                    for slot in range(2):
                        one(KD // 2 - 1, slot, False)

            for slot in range(2):
                weights_lo(slot, 0)
            add_products(0, 0)
            norm(1, acc, sqb, rs, "ln2")
            for gi, (f0, fn) in enumerate(GROUPS):
                with dve.Fori(0, fn // 2) as i:
                    for b in range(2):
                        g = ga[b]
                        f = 2 * i + (f0 + b)
                        n = 2 * i + (b + first_unit(f0))
                        dve.wait_ge(fs["scaled"], f + 1)
                        stt(g[:, 1:T], ps[2 * b][:, 0:T - 1], col("cw0", f), g[:, 1:T], ALU.mult, ALU.add)\
                            .then_inc(fs["c1"], 1)
                        dve.wait_ge(fs["c1"], f + 1)
                        stt(g[:, 0:T - 1], ps[2 * b][:, 1:T], col("cw2", f), g[:, 0:T - 1], ALU.mult, ALU.add)\
                            .then_inc(fs["c2"], 1)
                        weights_lo(0, n + 1)
                        dve.wait_ge(wt["used"][1], n + 1 + FREE)
                        dve.wait_ge(fs["gelu"], f + 1)
                        tt(g, g, ps[2 * b + 1], ALU.mult).then_inc(gu_done[b], 1)
                        weights_lo(1, n + 1)
                        low_part(g_lo[:, bass.ds(2 * i + b, 1), :].rearrange("p o t -> p (o t)"), g,
                                 g_hi[:, bass.ds(2 * i + b, 1), :].rearrange("p o t -> p (o t)"), fs["g_hi"], f + 1,
                                 g_split[b])
                add_products(first_unit(f0) + fn, int(gi == len(GROUPS) - 1))
            norm(2, hT[:, 7, :], (hT[:, 5, :], hT[:, 6, :]), work[:, 0:T], "lnf")


INPUTS = {"par": (P, NPAR), "ident": (P, P), "pairones": (P, P), "ones": (P, P), "gmask": (P, 2, 2 * C),
          "reset": (P, 2, TP), "sink": (P, AH), "slope": (P, AH), "negdist": (NT, P, BAND), "xT": (P, KD, T),
          "w_in": (20, P, KD, P), "lora_w": (NPAIR, P, 2 * P), "gate_w": (P, RW), "w_out": (KD, P, KD, P),
          "w_gu": (KF, P, 2, KD, P), "w_down": (KD, P, KF, P)}


def shape_constants():
    f = np.float32
    t = np.arange(C)
    gm = np.zeros((2, 2, C, 2, 2, C), f)
    sv, tv = t[:, None], t[None, :]
    for z, (strict, loose) in enumerate(((sv < tv, sv <= tv), (sv > tv, sv >= tv))):
        gm[:, :, :, z, 0] = strict
        gm[:, :, :, z, 1] = loose
    reset = np.ones((P, 2, NC, CP), f)
    reset[:, 0, :, 0] = 0
    reset[:, 1, :, C] = 0
    q, k = np.arange(P)[:, None], np.arange(BAND)[None, :] - P
    dist = np.abs(k - q)
    nd = np.empty((NT, P, BAND), f)
    for n in range(NT):
        ok = (dist <= P) & (n * P + k >= 0) & (n * P + k < T)
        nd[n] = np.where(ok, -dist, -1e33)
    slopes = (2.0 ** (-8.0 * np.arange(1, AH + 1) / AH)).astype(f)
    return {"ident": np.eye(P, dtype=f), "pairones": np.kron(np.eye(2), np.ones((HD, HD))).astype(f),
            "ones": np.ones((P, P), f), "gmask": gm.reshape(P, 2, 2 * C), "reset": reset.reshape(P, 2, TP),
            "slope": np.tile(slopes, (P, 1)), "negdist": nd}


def tiles(w):
    k, m = w.shape
    return np.ascontiguousarray(w.reshape(k // P, P, m // P, P).transpose(2, 1, 0, 3))


def kernel(**inputs):
    import concourse.bacc as bacc
    from concourse.bass_utils import run_bass_kernel_spmd

    v = {k: np.asarray(x) for k, x in inputs.items()}
    arrays = shape_constants()
    named = {"mu_prev": v["shift_mu_prev"], "mu_next": v["shift_mu_next"], "w0": v["decay_w0"], "a0": v["iclr_a0"],
             "k_k": v["k_k"], "k_a": v["k_a"], "r_k": v["r_k"], "lnx_g": v["lnx_g"], "lnx_b": v["lnx_b"],
             "ln1": v["ln1_g"], "ln2": v["ln2_g"], "lnf": v["lnf_g"], "cw0": v["ffn_conv_w"][0, 0],
             "cw1": v["ffn_conv_w"][0, 1], "cw2": v["ffn_conv_w"][0, 2], "cb": v["ffn_conv_b"]}
    arrays["par"] = np.ascontiguousarray(np.concatenate([named[n].reshape(-1, P) for n in COLS]).T)
    arrays["sink"] = np.ascontiguousarray(np.broadcast_to(v["attn_sink"][0], (P, AH)))
    arrays["xT"] = np.ascontiguousarray(v["x"][0].reshape(T, KD, P).transpose(2, 1, 0))
    w_in = tiles(v["w_in"][0])
    order = [12, 13] + [4 * i + j for j in range(NPAIR) for i in range(3)] + list(range(14, 20))
    arrays["w_in"] = np.ascontiguousarray(w_in[order])
    lora = np.zeros((NPAIR, P, 2 * P), np.float32)
    w2 = v["decay_w2"][0].reshape(2, HD, NPAIR, P)
    lora[:, 0:HD, 0:P], lora[:, 0:HD, P:] = w2[0].transpose(1, 0, 2), w2[1].transpose(1, 0, 2)
    lora[:, HD:, 0:P] = v["iclr_a2"][0].reshape(HD, NPAIR, P).transpose(1, 0, 2)
    arrays["lora_w"] = lora
    arrays["gate_w"] = np.ascontiguousarray(v["gate_g2"][0])
    arrays["w_out"] = tiles(v["w_out"][0])
    arrays["w_gu"] = np.ascontiguousarray(np.stack([tiles(v["ffn_w_gate"][0]), tiles(v["ffn_w_up"][0])], axis=2))
    arrays["w_down"] = tiles(v["ffn_w_down"][0])

    nc = bacc.Bacc("TRN2", target_bir_lowering=False, num_devices=1)
    args = {n: nc.dram_tensor(f"in_{n}", shape, F32, kind="ExternalInput").ap() for n, shape in INPUTS.items()}
    args["out"] = nc.dram_tensor("out_y", (P, KD, T), F32, kind="ExternalOutput").ap()
    hymba_block(nc, args)
    r = run_bass_kernel_spmd(nc, [{f"in_{n}": arrays[n] for n in INPUTS}], core_ids=[0])
    y = r.results[0]["out_y"]
    return np.ascontiguousarray(np.asarray(y).transpose(2, 1, 0).reshape(1, T, D))
```

```python
import math
from contextlib import ExitStack

import numpy as np

import concourse.bass as bass
from concourse import mybir

F32 = mybir.dt.float32
F32R = mybir.dt.float32r
ALU = mybir.AluOpType
ACT = mybir.ActivationFunctionType
AX = mybir.AxisListType

P = 128
T = 1024
D = 1024
HD = 64
KD = D // P
RW = 512
NPAIR = RW // P
NT = T // P
C = 32
NC = T // C
CP = C + 1
TP = NC * CP
F = 2816
KF = F // P
AH = 8
GH = 4
BAND = 3 * P
DECAY = math.exp(-0.5)
KRV = (1, 0, 2)
NORM_EPS = 1e-6
LNX_EPS = 64e-5
L2_EPS = 1e-12
FREE = 1
GROUPS = ((0, 8), (8, 8), (16, 6))
GK = 8
YT = 5
HALF = 512

COLS = {}
_n = 0
for _name, _w in (("mu_prev", 14), ("mu_next", 14), ("w0", 8), ("a0", 4), ("k_k", 4), ("k_a", 4), ("r_k", 4),
                  ("lnx_g", 4), ("lnx_b", 4), ("ln1", 8), ("ln2", 8), ("lnf", 8),
                  ("cw0", 22), ("cw1", 22), ("cw2", 22), ("cb", 22)):
    COLS[_name] = _n
    _n += _w
NPAR = _n


def hymba_block(nc, a):
    with ExitStack() as ctx:
        def sb(name, shape):
            return ctx.enter_context(nc.sbuf_tensor(name, shape, F32))

        def sem(name):
            return ctx.enter_context(nc.semaphore(name))

        def dram(name, shape):
            return nc.dram_tensor(name, shape, F32, kind="Internal").ap()

        AR_d = dram("AR_d", (2, NPAIR, P, NC * 2 * C))
        G_d = dram("G_d", (2, NPAIR, P, NC * 2 * C))
        BK_d = dram("BK_d", (2, NPAIR, P, NC * HD))
        TI_d = dram("TI_d", (2, NPAIR, 2, C, NC * C))
        v_d = dram("v_d", (T, RW))
        y_d = dram("y_d", (2, T, RW))
        q_d = dram("q_d", (4, P, T))
        kk_d = dram("kk_d", (2, P, T + 2 * P))
        va_d = dram("va_d", (T + 2 * P, P))

        par = sb("par", [P, NPAR])
        c0_eps = sb("c0_eps", [P, 16])
        c0 = c0_eps[:, 0:14]
        eps = c0_eps[:, 14:16]
        oka = sb("oka", [P, NPAIR])
        ident = sb("ident", [P, P])
        pairones = sb("pairones", [P, P])
        ones = sb("ones", [P, P])
        gmask = sb("gmask", [P, 2, 2 * C])
        sink = sb("sink", [P, AH])
        slope = sb("slope", [P, AH])
        PC = sb("PC", [P, 2, NPAIR, NC])
        xT = sb("xT", [P, KD, T])
        WPART = KD * P
        H_AT = 2 * GK * T + 6 * WPART
        SG_AT = H_AT + 2 * KD * T
        WORK = SG_AT - KD * T
        region_at = (nc.sbuf_base + 31) // 32 * 32
        hT = sb("hT", [P, KD, T])
        oT = hT
        work = sb("work", [P, WORK])
        sgT = sb("sgT", [P, T])
        bonusT = sb("bonusT", [P, NPAIR, T])

        def part(name, at, shape):
            return nc.alloc_sbuf_tensor_at(name, shape, F32R, offset=region_at + 4 * at)

        g_hi, g_lo = part("g_hi", 0, [P, GK, T]), part("g_lo", GK * T, [P, GK, T])
        w_hi = [part(f"w_hi{i}", 2 * GK * T + i * WPART, [P, KD, P]) for i in range(2)]
        w_lo = [part(f"w_lo{i}", 2 * GK * T + (2 + i) * WPART, [P, KD, P]) for i in range(2)]
        RAW_AT = 2 * GK * T + 4 * WPART - KD * T
        w_raw = [work[:, RAW_AT + i * WPART:RAW_AT + (i + 1) * WPART].rearrange("p (k n) -> p k n", n=P)
                 for i in range(2)]
        h_hi, h_lo = part("h_hi", H_AT, [P, KD, T]), part("h_lo", H_AT + KD * T, [P, KD, T])
        ga = [sgT[:, :], bonusT[:, 0, :]]

        class Carve:
            def __init__(self, at=0):
                self.at = at

            def __call__(self, *shape):
                n = int(np.prod(shape))
                v = work[:, self.at:self.at + n]
                self.at += n
                assert self.at <= WORK, self.at
                if len(shape) == 1:
                    return v
                names = "abcd"[:len(shape)]
                return v.rearrange(f"p ({' '.join(names)}) -> p {' '.join(names)}",
                                   **{x: s for x, s in zip(names[1:], shape[1:])})

        banks = ctx.enter_context(nc.psum_tensor("banks", [P, 8, HALF], F32))
        flat = banks[:, :, :].rearrange("p b n -> p (b n)")
        ps = [flat[:, 2 * s * HALF:2 * (s + 1) * HALF] for s in range(4)]

        def col(name, m, n=1):
            return par[:, bass.ds(m + COLS[name], n)]

        rs, acc = bonusT[:, 0, :], bonusT[:, 1, :]
        sqb = [bonusT[:, 2, :], bonusT[:, 3, :]]

        w = Carve()
        W3 = [w(KD, P) for _ in range(3)]
        lora = w(T)
        lw = w(2 * P)
        rT, kT, vT = w(T), w(T), w(T)
        kkT, bT, aT, tpT, sqT = w(T), w(T), w(T), w(T), w(T)
        L = [w(TP) for _ in range(2)]
        E_AT = w.at
        E = [w(TP) for _ in range(2)]
        Ei = [w(TP) for _ in range(2)]
        reset = w(2, TP)
        AR, BK = w(NC, 2, C), w(NC, 2, C)
        G, BKt = w(NC, 2 * C), w(NC // 2, P)
        vts = w(NT, P)
        assert w.at <= WORK

        xflat = xT[:, :, :].rearrange("p k t -> p (k t)")
        M, TI = ([xflat[:, (2 * i + z) * 2 * C * C:(2 * i + z + 1) * 2 * C * C].rearrange("p (e a b) -> p e a b", e=2, a=C)
                  for z in range(2)] for i in range(2))
        prod = work[:, E_AT:E_AT + 2 * C * C].rearrange("p (e a b) -> p e a b", e=2, a=C)

        w = Carve(E_AT + 2 * TP)
        qst = [w(T) for _ in range(2)]
        zero = w(P)
        vast = w(NT, P)

        w = Carve()
        ARs = [w(2, NPAIR, 2 * 2 * C) for _ in range(2)]
        Gs = [w(2, NPAIR, 2 * 2 * C) for _ in range(2)]
        BKs = [w(2, NPAIR, 2 * HD) for _ in range(2)]
        TIs = [w(2, NPAIR, 2 * C) for _ in range(2)]
        UV = [w(2, 2, NPAIR, HD) for _ in range(2)]
        S = w(2, NPAIR, HD)
        St = w(2, NPAIR, HD)
        Xs = w(2, NPAIR * HD)
        Ys = [w(2, NPAIR * HD) for _ in range(2)]
        qs, ks, vs, nd = w(4, P), w(2, BAND), w(3, P), w(BAND)
        Lg = w(GH, BAND)
        Pr = w(GH, BAND)
        PT = w(3, 2, 2, P)
        mx, nm, es, rsum, rinv = w(GH), w(GH), w(GH), w(GH), w(GH)

        w = Carve(w.at)
        yin = [w(2, RW) for _ in range(2)]
        ysum, ycen, ysq = w(RW), w(RW), w(RW)
        stat = w(4, AH)
        yn = oT[:, 0:NPAIR, :].rearrange("p j (n c) -> p j n c", c=P)
        w = Carve(2 * GK * T + 2 * WPART - KD * T)
        gw = w(RW)
        ot1 = w(T)

        names = """consts_loaded x_loaded consts_made
            p_mm p_scaled p_shift1 p_shifted lora_tanh gate_sig lw_full
            dz0_mm dz1_mm ic_mm sig0 sig1 a_ready kk_ready kk_sq ss_mm nrm_ready nrm_max nrm_rec nk_ready b_ready
            ka_fac kp_ready bon_in bon_mm bon_out vt_mm vts_ready v_stored
            L0_ready L1_ready E0_ready E1_ready
            ab_ready k_prod gram_mm G_half G_ready bkt_mm bkt_ready AR_stored G_stored BK_stored
            pad_zero
            qkv_mm qkv_evicted q_stored q_stored2 z_stored c0_part vat_mm vat_evicted zero_made
            TI_init sol_prod sol_row TI_stored TI1_stored x_again
            X0_mm X1_mm X0_out X1_out U0_mm U1_mm U00 U01 U10 U11 Y0_mm Y1_mm S0_mm S1_mm Y0_out Y1_out
            S0_add S1_add S0_new S1_new
            sc_mm sc_out mx_red mx_sink nm_ready p_exp s_exp sum_all inv_ready p_norm pt_mm pt_out o_mm o_out
            y_summed y_mean y_cent y_sq y_var y_sd y_inv y_normed yt_mm gt_mm y_aff y_bon y_gated gw_loaded
            out_stored""".split()
        s = {n: sem(n) for n in names}
        M_loaded = [sem(f"M_loaded{z}") for z in range(2)]
        w_full = [sem(f"w_full{i}") for i in range(3)]
        scan_full = [sem(f"scan_full{i}") for i in range(2)]
        qk_full, val_full = sem("qk_full"), sem("val_full")
        y_full = [sem(f"y_full{i}") for i in range(2)]
        passed = sem("passed")
        yin_used = [sem(f"yin_used{i}") for i in range(2)]
        ys_stored = [sem(f"ys_stored{i}") for i in range(2)]
        sz = [{k: s[v] for k, v in dict(X_mm=f"X{z}_mm", X_out=f"X{z}_out", U_mm=f"U{z}_mm", U_e0=f"U{z}0",
                                        U_e1=f"U{z}1", Y_mm=f"Y{z}_mm", S_mm=f"S{z}_mm", Y_out=f"Y{z}_out",
                                        S_add=f"S{z}_add", S_new=f"S{z}_new").items()} for z in range(2)]

        ns = {k: sem(f"norm_{k}") for k in ("squared", "summed", "ms_mm", "root", "rstd", "scaled")}

        def slot_sems(tag, keys):
            return {k: [sem(f"{tag}_{k}{i}") for i in range(2)] for k in keys}

        wt = slot_sems("wt", ("full", "hi", "lo", "used"))
        added = [sem(f"added{i}") for i in range(2)]
        gu_done = [sem(f"gu_done{i}") for i in range(2)]
        g_split = [sem(f"g_split{i}") for i in range(2)]
        fs = {k: sem(f"ffn_{k}") for k in ("scaled", "c1", "c2", "gelu", "g_hi")}
        sp_s = {k: sem(k) for k in ("att_hi", "att_lo", "h_hi", "h_lo")}

        NCONST = 8
        start_at_one = [s[n] for n in """p_mm ic_mm bkt_ready G_ready pt_out o_out gram_mm v_stored BK_stored
            AR_stored G_stored pt_mm o_mm bkt_mm p_exp s_exp y_normed""".split()]
        start_at_one += ys_stored + added + gu_done + yin_used + wt["lo"] + wt["used"] + g_split
        start_at_one += [sz[z][n] for z in range(2) for n in ("Y_out", "S_add")]
        block = ctx.enter_context(nc.Block())

        def first_unit(f0):
            return KD // 2 + f0 + (KD // 2) * [g[0] for g in GROUPS].index(f0)


        def chunked(x, z, excl):
            v = x.rearrange("p (c t) -> p c t", t=CP)
            first = (0 if excl else 1) if z == 0 else (1 if excl else 0)
            return v[:, :, first:first + C]

        @block.sync
        def _(sp):
            for x in start_at_one:
                sp.sem_inc(x, FREE)
            for dst, src in ((par[:, :], a["par"]), (ident[:, :], a["ident"]), (pairones[:, :], a["pairones"]),
                             (gmask[:, :, :], a["gmask"]), (reset, a["reset"]), (sink[:, :], a["sink"]),
                             (slope[:, :], a["slope"]), (ones[:, :], a["ones"])):
                sp.dma_start(dst, src).then_inc(s["consts_loaded"], 16)
            for k in range(0, KD, 2):
                sp.dma_start(xT[:, k, :], a["xT"][:, k, :]).then_inc(s["x_loaded"], 16)
            for i in range(2):
                sp.dma_start(W3[i], a["w_in"][i]).then_inc(w_full[i], 16)
            sp.dma_start(W3[2], a["w_in"][4]).then_inc(w_full[2], 16)
            for i in range(2):
                sp.wait_ge(s["p_mm"], i + 1 + FREE)
                sp.dma_start(W3[i], a["w_in"][2 + i]).then_inc(w_full[i], 16)
            def load_gram(j, z):
                sp.wait_ge(s["G_stored"], 32 * j + 16 * (z + 1) + FREE)
                for e in range(2):
                    src = G_d[z][bass.ds(j, 1), 64 * e:64 * e + C].rearrange("o s (c x) -> (o c) s x", x=2 * C)[:, :, 0:C]
                    sp.dma_start(M[z][C * j:C * (j + 1), e, :, :], src).then_inc(M_loaded[z], 16)

            for j in range(NPAIR):
                pair = bass.ds(j, 1)
                sp.wait_ge(s["ic_mm"], j + FREE)
                sp.dma_start(lw, a["lora_w"][pair].rearrange("o p n -> (o p) n")).then_inc(s["lw_full"], 16)
                for i in range(3):
                    sp.wait_ge(s["p_mm"], 3 * j + 3 + i + FREE)
                    sp.dma_start(W3[i], a["w_in"][bass.ds(3 * j + (5 + i), 1)].rearrange("o p k n -> (o p) k n"))\
                      .then_inc(w_full[i], 16)
                for z in range(2):
                    sp.wait_ge(s["ab_ready"], 2 * j + z + 1)
                    sp.dma_start(AR_d[z][pair].rearrange("o p n -> (o p) n"), AR.rearrange("p c a t -> p (c a t)"))\
                      .then_inc(s["AR_stored"], 16)
                    if z == 1:
                        load_gram(j, 0)
                    sp.wait_ge(s["G_ready"], 2 * j + z + 1 + FREE)
                    sp.dma_start(G_d[z][pair].rearrange("o p n -> (o p) n"), G.rearrange("p c t -> p (c t)"))\
                      .then_inc(s["G_stored"], 16)
                    sp.wait_ge(s["bkt_ready"], 2 * j + z + 1 + FREE)
                    for odd in range(2):
                        for e in range(2):
                            dst = BK_d[z][pair, 64 * e:64 * e + 64].rearrange("o p (c q n) -> (o p) c q n", q=2, n=HD)
                            sp.dma_start(dst[:, :, odd, :], BKt[64 * odd:64 * odd + 64, :, HD * e:HD * e + HD])\
                              .then_inc(s["BK_stored"], 16)
                    if z == 0:
                        sp.wait_ge(s["vts_ready"], j + 1)
                        for e in range(2):
                            sp.dma_start(v_d.rearrange("(b p) n -> p b n", p=P)[:, :, bass.ds((e * NPAIR + j) * HD, HD)],
                                         vts[:, :, HD * e:HD * e + HD]).then_inc(s["v_stored"], 16)
                load_gram(j, 1)
            for i in range(3, 6):
                sp.wait_ge(s["qkv_mm"], i - 2)
                sp.dma_start(W3[i % 3], a["w_in"][14 + i]).then_inc(w_full[i % 3], 16)
            sp.wait_ge(s["qkv_mm"], 6)
            sp.wait_ge(s["BK_stored"], 16 * 8 * NPAIR + FREE)
            sp.wait_ge(s["AR_stored"], 16 * 2 * NPAIR + FREE)
            sp.wait_ge(s["v_stored"], 32 * NPAIR + FREE)
            v_rows = v_d.rearrange("(c t) (e n) -> e t c n", t=C, e=2)

            def load_scan(i, slot, given=True, inverses=True):
                for z in range(2):
                    c = (4 * i + 2 * slot) if z == 0 else (i * -4 + (NC - 2 - 2 * slot))
                    for dst, src, n in ((ARs, AR_d, 2 * C), (Gs, G_d, 2 * C), (BKs, BK_d, HD)) if given else ():
                        sp.dma_start(dst[slot][:, z], src[z].rearrange("j p n -> p j n")[:, :, bass.ds(c * n, 2 * n)])\
                          .then_inc(scan_full[slot], 16)
                    for e in range(2):
                        if inverses:
                            sp.dma_start(TIs[slot][64 * e:64 * e + C, z],
                                         TI_d[z, :, e].rearrange("j s n -> s j n")[:, :, bass.ds(c * C, 2 * C)])\
                              .then_inc(scan_full[slot], 16)
                        if given:
                            sp.dma_start(UV[slot][64 * e + C:64 * e + 2 * C, z].rearrange("p c j i -> p c (j i)"),
                                         v_rows[e][:, bass.ds(c, 2), :]).then_inc(scan_full[slot], 16)

            def load_qk(n):
                for dst, src in ((qs, q_d.rearrange("j p t -> p j t")[:, :, bass.ds(n * P, P)]),
                                 (ks, kk_d.rearrange("g p t -> p g t")[:, :, bass.ds(n * P, BAND)]),
                                 (nd, a["negdist"][bass.ds(n, 1)].rearrange("o p n -> (o p) n"))):
                    sp.dma_start(dst, src).then_inc(qk_full, 16)

            def load_values(n):
                sp.dma_start(vs, va_d.rearrange("(b p) n -> p b n", p=P)[:, bass.ds(n, 3), :]).then_inc(val_full, 16)

            load_scan(0, 0, inverses=False)
            load_scan(0, 1, inverses=False)
            sp.wait_ge(s["q_stored"], 16 * 10)
            sp.wait_ge(s["q_stored2"], 32)
            sp.wait_ge(s["z_stored"], 16 * 6)
            load_qk(0)
            load_values(0)
            sp.wait_ge(s["sol_row"], 2 * (C - 1))
            for j in range(NPAIR):
                for e in range(2):
                    sp.dma_start(TI_d[1, j, e].rearrange("s (c t) -> c s t", t=C), TI[1][C * j:C * (j + 1), e])\
                        .then_inc(s["TI1_stored"], 16)
            sp.wait_ge(s["TI_stored"], 16 * 2 * NPAIR)
            sp.wait_ge(s["TI1_stored"], 16 * 2 * NPAIR)
            load_scan(0, 0, given=False)
            load_scan(0, 1, given=False)
            y_rows = y_d.rearrange("z (c t) (j e i) -> z c e t j i", t=C, j=NPAIR, e=2)

            def store_y(i, q):
                for z in range(2):
                    c = 4 * i + q if z == 0 else i * -4 + (NC - 1 - q)
                    sp.wait_ge(sz[z]["Y_out"], 4 * i + q + 1 + FREE)
                    for e in range(2):
                        sp.dma_start(y_rows[z, bass.ds(c, 1), e].rearrange("o t j i -> (o t) j i"),
                                     Ys[q % 2][64 * e + C:64 * e + 2 * C, z].rearrange("p (j i) -> p j i", j=NPAIR))\
                          .then_inc(ys_stored[q % 2], 16)

            def load_y(r, tiles_):
                for slot, n in enumerate(tiles_):
                    sp.wait_ge(ys_stored[slot], 128 * r + 128 * YT + FREE)
                sp.sem_inc(passed, 1)
                for slot, n in enumerate(tiles_):
                    sp.wait_ge(yin_used[slot], r + FREE)
                    sp.sem_inc(passed, 1)
                    sp.dma_start(yin[slot], y_d[:, bass.ds(n * P, P)].rearrange("z p n -> p z n"))\
                      .then_inc(y_full[slot], 16)

            for first, last in ((0, YT - 1), (YT - 1, NC // 4 - 1)):
                with sp.Fori(first, last) as i:
                    for slot in range(2):
                        store_y(i, 2 * slot)
                        if slot == 1:
                            sp.wait_ge(s["sc_out"], 8 * i + 8)
                            load_qk(i + 1)
                        store_y(i, 2 * slot + 1)
                        for z in range(2):
                            sp.wait_ge(sz[z]["Y_mm"], 4 * i + 2 * slot + 2)
                            sp.wait_ge(sz[z]["S_mm"], 4 * i + 2 * slot + 2)
                        if slot == 1:
                            sp.wait_ge(s["o_mm"], 2 * i + 2 + FREE)
                            load_values(i + 1)
                        load_scan(i + 1, slot)
                    if first:
                        load_y(i - (YT - 1), (i * -1 + (NC // 4 - 1), i))
            for q in range(4):
                store_y(NC // 4 - 1, q)
            for b in range(2):
                sp.wait_ge(ys_stored[b], 64 * NC // 2 + FREE)
            sp.wait_ge(s["o_out"], 2 * NT + FREE)
            load_y(NC // 4 - YT, (0, NT - 1))
            sp.dma_start(gw, a["gate_w"]).then_inc(s["gw_loaded"], 16)
            def load_weights(slot, n, src, kn=KD):
                sp.wait_ge(wt["lo"][slot], n + FREE)
                sp.dma_start(w_raw[slot][:, 0:kn], src).then_inc(wt["full"][slot], 16)

            with sp.Fori(0, KD // 2) as i:
                for slot in range(2):
                    load_weights(slot, i, a["w_out"][bass.ds(2 * i + slot, 1)].rearrange("o p k n -> (o p) k n"))
            for f0, fn in GROUPS:
                with sp.Fori(0, fn) as f:
                    for slot in range(2):
                        load_weights(slot, f + first_unit(f0), a["w_gu"][bass.ds(f + f0, 1), :, slot]
                                     .rearrange("o p k n -> (o p) k n"))
                with sp.Fori(0, KD // 2) as i:
                    for slot in range(2):
                        load_weights(slot, i + first_unit(f0) + fn, a["w_down"][bass.ds(2 * i + slot, 1), :, f0:f0 + fn]
                                     .rearrange("o p k n -> (o p) k n"), fn)
            for k in range(KD):
                sp.wait_ge(ns["scaled"], 2 * KD + k + 1)
                sp.dma_start(a["out"][:, k, :], hT[:, k, :]).then_inc(s["out_stored"], 16)
            sp.wait_ge(s["out_stored"], 16 * KD)

        @block.tensor
        def _(pe):
            def dense(out, wt, src, kn, done):
                for k in range(kn):
                    for h in range(2):
                        mm = pe.matmul(out[:, h * HALF:(h + 1) * HALF], wt[:, k, :],
                                       src[:, k, h * HALF:(h + 1) * HALF], start=(k == 0), stop=(k == kn - 1))
                mm.then_inc(done, 1)

            def split_dense(out, slot, hi, lo, kn, after=()):
                for k in range(kn):
                    for k_at, sem_, n in after:
                        if k == k_at:
                            pe.wait_ge(sem_, n)
                    for p_, (wp, xp) in enumerate(((w_hi, hi), (w_hi, lo), (w_lo, hi))):
                        for h in range(2):
                            mm = pe.matmul(out[:, h * HALF:(h + 1) * HALF], wp[slot][:, k, :],
                                           xp[:, k, h * HALF:(h + 1) * HALF], start=(k == 0 and p_ == 0),
                                           stop=(k == kn - 1 and p_ == 2))
                mm.then_inc(wt["used"][slot], 1)

            def whole(out, wt, src, done, rows=slice(0, P)):
                for h in range(2):
                    mm = pe.matmul(out[:, h * HALF:(h + 1) * HALF], wt, src[rows, h * HALF:(h + 1) * HALF],
                                   start=True, stop=True)
                mm.then_inc(done, 1)

            def settled():
                pe.sem_inc(passed, 1)

            def norm(n, ac):
                pe.wait_ge(ns["summed"], (n + 1) * (KD - 1))
                whole(ps[0], ones[:, :], ac, ns["ms_mm"])

            pe.wait_ge(s["consts_loaded"], 16 * NCONST)
            norm(0, acc)
            pe.wait_ge(ns["root"], 1)
            pe.wait_ge(ns["scaled"], KD)
            for i in range(2):
                pe.wait_ge(w_full[i], 16)
                dense(ps[i], W3[i], hT, KD, s["p_mm"])
            pe.wait_ge(s["p_shifted"], 2)
            pe.wait_ge(s["lora_tanh"], 1)
            with pe.Fori(0, NPAIR) as j:
                pe.wait_ge(s["G_ready"], 2 * j + FREE)
                pe.wait_ge(w_full[0], 16 * j + 32)
                dense(ps[2], W3[0], hT, KD, s["p_mm"])
                pe.wait_ge(s["lw_full"], 16 * j + 16)
                pe.wait_ge(s["bkt_ready"], 2 * j + FREE)
                whole(ps[3], lw[0:64, 0:P], lora, s["dz0_mm"], slice(0, 64))
                whole(ps[0], lw[0:64, P:2 * P], lora, s["dz1_mm"], slice(0, 64))
                whole(ps[1], lw[64:128, 0:P], lora, s["ic_mm"], slice(64, P))
                pe.wait_ge(s["sig0"], j + 1)
                pe.wait_ge(w_full[1], 16 * j + 32)
                dense(ps[3], W3[1], hT, KD, s["p_mm"])
                pe.wait_ge(s["kk_sq"], j + 1)
                pe.wait_ge(s["a_ready"], j + 1)
                whole(ps[1], pairones[:, :], sqT, s["ss_mm"])
                pe.wait_ge(s["sig1"], j + 1)
                pe.wait_ge(w_full[2], 16 * j + 16)
                dense(ps[0], W3[2], hT, KD, s["p_mm"])
                pe.wait_ge(s["bon_in"], j + 1)
                pe.wait_ge(s["p_shifted"], 3 * j + 4)
                whole(ps[3], pairones[:, :], tpT, s["bon_mm"])
                for z in range(2):
                    pe.wait_ge(s["ab_ready"], 2 * j + z + 1)
                    pe.wait_ge(s["k_prod"], 2 * j + z + 1)
                    if z == 0:
                        pe.wait_ge(s["nrm_ready"], j + 1)
                        pe.wait_ge(s["p_shifted"], 3 * j + 3)
                    else:
                        pe.wait_ge(s["G_ready"], 2 * j + 1 + FREE)
                        pe.wait_ge(s["vts_ready"], j + 1)
                    settled()
                    for c in range(NC):
                        for e in range(2):
                            h = slice(64 * e, 64 * e + 64)
                            out = ps[1 + c // 16][h, (c % 16) * 64:(c % 16) * 64 + 64]
                            mm = pe.matmul(out, BK[h, c].rearrange("p a b -> p (a b)"),
                                           AR[h, c].rearrange("p a b -> p (a b)"), start=True, stop=True)
                    mm.then_inc(s["gram_mm"], 1)
                    if z == 0:
                        pe.wait_ge(s["bon_out"], j + 1)
                        pe.wait_ge(s["p_shifted"], 3 * j + 5)
                    else:
                        pe.wait_ge(s["bkt_ready"], 2 * j + 1 + FREE)
                    for c in range(NC // 2):
                        out = ps[(3, 0)[c // 8]][:, (c % 8) * P:(c % 8 + 1) * P]
                        mm = pe.transpose(out, BK[:, 2 * c:2 * c + 2].rearrange("p c a b -> p (c a b)"), ident[:, :])
                    mm.then_inc(s["bkt_mm"], 1)
                    if z == 0:
                        pe.wait_ge(s["G_half"], 2 * j + 1)
                        for n in range(NT):
                            mm = pe.transpose(ps[1][:, n * P:(n + 1) * P], vT[:, n * P:(n + 1) * P], ident[:, :])
                        mm.then_inc(s["vt_mm"], 1)
            for i in range(6):
                if i == 0:
                    pe.wait_ge(s["bkt_ready"], 2 * NPAIR + FREE)
                    pe.wait_ge(s["G_ready"], 2 * NPAIR + FREE)
                if i >= 4:
                    pe.wait_ge(s["qkv_evicted"], i - 3)
                pe.wait_ge(w_full[i % 3], 16 * (NPAIR + 1 + i // 3 + (1 if i % 3 < 2 else 0)))
                dense(ps[i % 4], W3[i % 3], hT, KD, s["qkv_mm"])
            pe.wait_ge(s["qkv_evicted"], 6)
            for n in range(NT):
                mm = pe.transpose(ps[2][:, n * P:(n + 1) * P], qst[1][:, n * P:(n + 1) * P], ident[:, :])
            mm.then_inc(s["vat_mm"], 1)
            pe.wait_ge(s["vat_evicted"], 1)
            pe.wait_ge(s["sol_row"], 2 * (C - 1))
            XY = [banks[:, z, 0:NPAIR * HD] for z in range(2)]
            US = [banks[:, 2 + z, :] for z in range(2)]
            def scores(i, g, heads):
                blk = 2 * i + g
                for h in heads:
                    e, hh = h % 2, h // 2
                    if h < 2:
                        pe.wait_ge(s["pt_out"], 3 * blk + FREE)
                    else:
                        pe.wait_ge(s["sc_out"], 4 * blk + h - 1)
                    pe.matmul(banks[:, 4 + h % 2, 0:BAND], qs[64 * e:64 * e + 64, 2 * g + hh, :],
                              ks[64 * e:64 * e + 64, g, :], start=True, stop=True).then_inc(s["sc_mm"], 1)

            def probabilities(i, g):
                pe.wait_ge(s["p_norm"], 2 * i + g + 1)
                for kb in range(3):
                    for h in range(GH):
                        e, hh = h % 2, h // 2
                        mm = pe.transpose(banks[:, 4 + kb, (2 * e + hh) * P:(2 * e + hh + 1) * P],
                                          Pr[:, h, kb * P:(kb + 1) * P], ident[:, :])
                    mm.then_inc(s["pt_mm"], 1)

            def values(i, g):
                blk = 2 * i + g
                pe.wait_ge(val_full, 16 * i + 16)
                pe.wait_ge(s["pt_out"], 3 * blk + 3 + FREE)
                pe.wait_ge(s["o_out"], blk + FREE)
                for e in range(2):
                    for kb in range(3):
                        mm = pe.matmul(banks[64 * e:64 * e + 64, 7, 0:2 * P], vs[:, kb, HD * g:HD * g + HD],
                                       PT[:, kb, e].rearrange("p a b -> p (a b)"), start=(kb == 0), stop=(kb == 2))
                mm.then_inc(s["o_mm"], 1)

            with pe.Fori(0, NC // 4) as i:
                for q in range(4):
                    slot, cc, g = q // 2, q % 2, q // 2
                    n = 4 * i + q
                    if cc == 0:
                        pe.wait_ge(scan_full[slot], 16 * 14 * i + 16 * 14)
                    for z in range(2):
                        c2 = cc if z == 0 else 1 - cc
                        pe.wait_ge(sz[z]["Y_out"], n + FREE)
                        for part in range(2):
                            if part == 1:
                                pe.wait_ge(sz[z]["S_new"], n + 1)
                                settled()
                            for j in range(NPAIR):
                                for e in range(2):
                                    h = slice(64 * e, 64 * e + 64)
                                    hk = slice(64 * e + C, 64 * e + 2 * C)
                                    out = XY[z][h, j * HD:(j + 1) * HD]
                                    if part == 0:
                                        mm = pe.matmul(out, Gs[slot][hk, z, j, c2 * 64:c2 * 64 + 64],
                                                       UV[slot][hk, z, c2, j, :], start=(j == 0), stop=False,
                                                       skip_group_check=True)
                                    else:
                                        mm = pe.matmul(out, ARs[slot][h, z, j, c2 * 64:c2 * 64 + 64],
                                                       S[h, z, j, :], start=False, stop=(j == NPAIR - 1),
                                                       skip_group_check=True)
                        mm.then_inc(sz[z]["X_mm"], 1)
                    if cc == 0:
                        pe.wait_ge(qk_full, 48 * i + 48)
                        scores(i, g, (0, 1))
                    else:
                        probabilities(i, g)
                    for z in range(2):
                        c2 = cc if z == 0 else 1 - cc
                        pe.wait_ge(sz[z]["X_out"], n + 1)
                        pe.wait_ge(sz[z]["S_add"], n + FREE)
                        settled()
                        for j in range(NPAIR):
                            for e in range(2):
                                hu = slice(64 * e, 64 * e + C)
                                mm = pe.matmul(US[z][hu, j * HD:(j + 1) * HD], TIs[slot][hu, z, j, c2 * C:c2 * C + C],
                                               Xs[hu, z, j * HD:(j + 1) * HD], start=True, stop=True)
                        mm.then_inc(sz[z]["U_mm"], 1)
                    if cc == 0:
                        scores(i, g, (2, 3))
                    else:
                        values(i, g)
                    for z in range(2):
                        c2 = cc if z == 0 else 1 - cc
                        pe.wait_ge(sz[z]["U_e0"], n + 1)
                        pe.wait_ge(sz[z]["U_e1"], n + 1)
                        settled()
                        for j in range(NPAIR):
                            for e in range(2):
                                h = slice(64 * e, 64 * e + 64)
                                mm = pe.matmul(US[z][h, 256 + j * HD:256 + (j + 1) * HD],
                                               BKs[slot][h, z, j, c2 * HD:c2 * HD + HD], UV[slot][h, z, c2, j, :],
                                               start=True, stop=True)
                        mm.then_inc(sz[z]["S_mm"], 1)
                        for j in range(NPAIR):
                            for e in range(2):
                                hu = slice(64 * e, 64 * e + C)
                                mm = pe.matmul(XY[z][64 * e + C:64 * e + 2 * C, j * HD:(j + 1) * HD],
                                               Gs[slot][hu, z, j, c2 * 64 + C:c2 * 64 + 2 * C],
                                               UV[slot][hu, z, c2, j, :], start=False, stop=True,
                                               skip_group_check=True)
                        mm.then_inc(sz[z]["Y_mm"], 1)
            pe.wait_ge(s["y_normed"], NT + FREE)
            pe.wait_ge(s["gw_loaded"], 16)
            pe.wait_ge(s["o_out"], 2 * NT + FREE)
            for z in range(2):
                pe.wait_ge(sz[z]["Y_out"], NC + FREE)
                pe.wait_ge(sz[z]["S_add"], NC + FREE)
            for j in range(NPAIR):
                if j >= 2:
                    pe.wait_ge(s["y_gated"], j - 1)
                a0, a1 = ps[2 * (j % 2)], ps[2 * (j % 2) + 1]
                for n in range(NT):
                    mm = pe.transpose(a0[:, n * P:(n + 1) * P], yn[:, j, n, :], ident[:, :])
                mm.then_inc(s["yt_mm"], 1)
                whole(a1, gw[:, j * P:(j + 1) * P], sgT, s["gt_mm"])
            pe.wait_ge(s["y_gated"], NPAIR)
            pe.wait_ge(sp_s["att_lo"], KD - NPAIR)
            with pe.Fori(0, KD // 2) as i:
                for slot in range(2):
                    pe.wait_ge(wt["lo"][slot], i + 1 + FREE)
                    pe.wait_ge(added[slot], i + FREE)
                    split_dense(ps[slot], slot, h_hi, h_lo, KD, [(k, sp_s["h_lo"], k + 1) for k in range(NPAIR)])
            for slot in range(2):
                pe.wait_ge(added[slot], KD // 2 + FREE)
            norm(1, acc)
            pe.wait_ge(ns["root"], 2)
            for gi, (f0, fn) in enumerate(GROUPS):
                for slot in range(2):
                    pe.wait_ge(added[slot], KD // 2 * (gi + 1) + FREE)
                with pe.Fori(0, fn // 2) as i:
                    for b in range(2):
                        n = 2 * i + (b + first_unit(f0))
                        pe.wait_ge(gu_done[b], i + f0 // 2 + FREE)
                        for slot in range(2):
                            pe.wait_ge(wt["lo"][slot], n + 1 + FREE)
                            split_dense(ps[2 * b + slot], slot, h_hi, h_lo, KD,
                                        [(k, sp_s["h_lo"], NPAIR + k + 1) for k in range(KD)] if slot == 0 else ())
                pe.wait_ge(gu_done[0], (f0 + fn) // 2 + FREE)
                with pe.Fori(0, KD // 2) as i:
                    for slot in range(2):
                        pe.wait_ge(wt["lo"][slot], i + (first_unit(f0) + fn) + 1 + FREE)
                        pe.wait_ge(added[slot], i + KD // 2 * (gi + 1) + FREE)
                        split_dense(ps[slot], slot, g_hi, g_lo, fn,
                                    ((0, g_split[0], (f0 + fn) // 2 + FREE), (fn - 1, g_split[1], (f0 + fn) // 2 + FREE)))
            for slot in range(2):
                pe.wait_ge(added[slot], KD // 2 * (len(GROUPS) + 1) + FREE)
            norm(2, acc)

        @block.scalar
        def _(act):
            for k in range(1, KD, 2):
                act.dma_start(xT[:, k, :], a["xT"][:, k, :]).then_inc(s["x_loaded"], 16)

            def square(n, k):
                if k >= 3:
                    act.wait_ge(ns["summed"], n * (KD - 1) + k - 2)
                act.activation(acc if k == 0 else sqb[k % 2], xT[:, k, :], ACT.Square).then_inc(ns["squared"], 1)

            def norm_root(n):
                act.wait_ge(ns["ms_mm"], n + 1)
                act.activation(rs, ps[0], ACT.Sqrt, bias=eps[:, 0:1], scale=1.0 / D).then_inc(ns["root"], 1)

            act.wait_ge(s["x_loaded"], 16 * KD)
            act.wait_ge(s["consts_made"], 4)
            for k in range(KD):
                square(0, k)
            norm_root(0)
            for i, dst in enumerate((lora, sgT[:, :])):
                act.wait_ge(s["p_mm"], i + 1 + FREE)
                act.activation(dst, ps[i], ACT.Copy, scale=c0[:, 12 + i:13 + i]).then_inc(s["p_scaled"], 1)
            act.wait_ge(s["p_shifted"], 1)
            act.activation(lora[0:64, :], lora[0:64, :], ACT.Tanh).then_inc(s["lora_tanh"], 1)
            act.wait_ge(s["p_shifted"], 2)
            act.activation(sgT[:, :], sgT[:, :], ACT.Sigmoid).then_inc(s["gate_sig"], 1)
            with act.Fori(0, NPAIR) as j:
                act.wait_ge(s["gram_mm"], 2 * j + FREE)
                act.wait_ge(s["G_ready"], 2 * j + FREE)
                def own_share(i, dst, slot):
                    act.wait_ge(s["p_mm"], 3 * j + 3 + i + FREE)
                    act.activation(dst, ps[slot], ACT.Copy, scale=c0[:, bass.ds(j + 4 * KRV[i], 1)])\
                       .then_inc(s["p_scaled"], 1)

                own_share(0, kT, 2)
                act.wait_ge(s["pad_zero"], 2)
                for z, slot in ((0, 3), (1, 0)):
                    act.wait_ge(s[f"dz{z}_mm"], j + 1)
                    act.activation(chunked(L[z], z, False), ps[slot].rearrange("p (c t) -> p c t", t=C), ACT.Sigmoid,
                                   bias=col("w0", j + 4 * z)).then_inc(s[f"sig{z}"], 1)
                act.wait_ge(s["ic_mm"], j + 1 + FREE)
                act.activation(aT, ps[1], ACT.Sigmoid, bias=col("a0", j)).then_inc(s["a_ready"], 1)
                act.wait_ge(s["kk_ready"], j + 1)
                act.activation(sqT, kkT, ACT.Square).then_inc(s["kk_sq"], 1)
                for z in range(2):
                    act.wait_ge(s[f"L{z}_ready"], j + 1)
                    act.activation(E[z], L[z], ACT.Exp, scale=-DECAY).then_inc(s[f"E{z}_ready"], 1)
                    act.activation(Ei[z], L[z], ACT.Exp, scale=DECAY).then_inc(s[f"E{z}_ready"], 1)
                own_share(1, rT, 3)
                act.wait_ge(s["ss_mm"], j + 1)
                act.activation(sqT, ps[1], ACT.Sqrt).then_inc(s["nrm_ready"], 1)
                own_share(2, vT, 0)
                for z in range(2):
                    act.wait_ge(s["bkt_mm"], 2 * j + z + 1 + FREE)
                    act.wait_ge(s["BK_stored"], 128 * j + 64 * z + FREE)
                    act.activation(BKt[:, 0:8].rearrange("p a b -> p (a b)"), ps[3], ACT.Copy)
                    act.activation(BKt[:, 8:16].rearrange("p a b -> p (a b)"), ps[0], ACT.Copy)\
                       .then_inc(s["bkt_ready"], 1)
                    if z == 0:
                        act.wait_ge(s["vt_mm"], j + 1)
                        act.wait_ge(s["v_stored"], 32 * j + FREE)
                        act.activation(vts.rearrange("p a b -> p (a b)"), ps[1], ACT.Copy).then_inc(s["vts_ready"], 1)
            act.wait_ge(s["BK_stored"], 16 * 8 * NPAIR + FREE)
            act.wait_ge(s["AR_stored"], 16 * 2 * NPAIR + FREE)
            act.wait_ge(s["G_stored"], 16 * 2 * NPAIR + FREE)
            act.wait_ge(s["v_stored"], 32 * NPAIR + FREE)
            for i in range(6):
                act.wait_ge(s["qkv_mm"], i + 1)
                if i >= 2:
                    act.wait_ge(s[("q_stored", "q_stored2")[i % 2]], 16 * (i // 2))
                act.activation(qst[i % 2], ps[i % 4], ACT.Copy, scale=(HD ** -0.5 if i < 4 else 1.0))\
                   .then_inc(s["qkv_evicted"], 1)
                act.wait_ge(s["qkv_evicted"], i + 1)
                if i < 4:
                    act.dma_start(q_d[i], qst[i % 2]).then_inc(s[("q_stored", "q_stored2")[i % 2]], 16)
                elif i == 4:
                    for g in range(2):
                        for e in range(2):
                            act.dma_start(kk_d[g, 64 * e:64 * e + 64, P:P + T], qst[0][64 * g:64 * g + 64, :])\
                               .then_inc(s["q_stored"], 16)
            act.wait_ge(s["vat_mm"], 1)
            act.activation(vast.rearrange("p a b -> p (a b)"), ps[2], ACT.Copy).then_inc(s["vat_evicted"], 1)
            act.wait_ge(s["vat_evicted"], 1)
            for n in range(4):
                act.dma_start(va_d[(1 + 2 * n) * P:(3 + 2 * n) * P].rearrange("(b p) n -> p b n", p=P),
                              vast[:, 2 * n:2 * n + 2]).then_inc(s["q_stored"], 16)
            act.wait_ge(s["q_stored"], 16 * 10)
            act.wait_ge(s["q_stored2"], 32)
            act.wait_ge(s["sol_row"], 2 * (C - 1))
            def y_square(m):
                act.wait_ge(s["y_cent"], m + 1)
                act.activation(ysq, ycen, ACT.Square).then_inc(s["y_sq"], 1)

            def y_root(m):
                act.wait_ge(s["y_var"], m + 1)
                act.activation(stat[:, 2], stat[:, 1], ACT.Sqrt, bias=eps[:, 1:2], scale=1.0 / HD).then_inc(s["y_sd"], 1)

            for first, last in ((0, YT), (YT, NC // 4)):
                with act.Fori(first, last) as i:
                    for q in range(4):
                        slot, cc, g = q // 2, q % 2, q // 2
                        n = 4 * i + q
                        blk = 2 * i + g
                        act.wait_ge(sz[1]["X_mm"], n + 1)
                        act.activation(Xs[:, 1], banks[:, 1, 0:256], ACT.Copy).then_inc(sz[1]["X_out"], 1)
                        if cc == 1:
                            act.wait_ge(s["o_mm"], blk + FREE)
                            for kb in range(3):
                                act.wait_ge(s["pt_mm"], 3 * blk + kb + 1 + FREE)
                                act.activation(PT[:, kb].rearrange("p a b c -> p (a b c)"), banks[:, 4 + kb, :], ACT.Copy)\
                                   .then_inc(s["pt_out"], 1)
                        for z in range(2):
                            c2 = cc if z == 0 else 1 - cc
                            act.wait_ge(sz[z]["U_mm"], n + 1)
                            act.activation(UV[slot][64:64 + C, z, c2].rearrange("p a b -> p (a b)"),
                                           banks[64:64 + C, 2 + z, 0:256], ACT.Copy).then_inc(sz[z]["U_e1"], 1)
                        if first and cc == 1:
                            y_root(2 * i + (slot - 2 * YT))
                        if cc == 1:
                            act.wait_ge(s["o_mm"], blk + 1 + FREE)
                            act.activation(oT[:, NPAIR + 2 * g:NPAIR + 2 * g + 2, bass.ds(i * P, P)],
                                           banks[:, 7, 0:2 * P].rearrange("p (a b) -> p a b", a=2), ACT.Copy)\
                               .then_inc(s["o_out"], 1)
                        for z in range(2):
                            act.wait_ge(sz[z]["Y_mm"], n + 1)
                            if z == 0:
                                act.wait_ge(ys_stored[q % 2], 64 * (2 * i + q // 2) + FREE)
                            act.activation(Ys[q % 2][:, z], banks[:, z, 0:256], ACT.Copy).then_inc(sz[z]["Y_out"], 1)
                        if cc == 0:
                            act.wait_ge(s["nm_ready"], blk + 1)
                            act.wait_ge(s["pt_mm"], 3 * blk + FREE)
                            for h in range(GH):
                                act.activation(Pr[:, h, :], Lg[:, h, :], ACT.Exp, bias=nm[:, h:h + 1],
                                               accum_out=rsum[:, h:h + 1]).then_inc(s["p_exp"], 1)
                            act.wait_ge(s["mx_sink"], 2 * blk + 2)
                            act.activation(es, mx, ACT.Exp).then_inc(s["s_exp"], 1)
                        if first and cc == 0:
                            y_square(2 * i + (slot - 2 * YT))
            for m in (NT - 2, NT - 1):
                y_square(m)
                y_root(m)
            def weights_hi(slot, n):
                act.wait_ge(wt["full"][slot], 16 * n + 16)
                act.wait_ge(wt["used"][slot], n + FREE)
                act.activation(w_hi[slot][:, :, :], w_raw[slot], ACT.Copy).then_inc(wt["hi"][slot], 1)

            act.wait_ge(s["y_normed"], NT + FREE)
            for k in range(NPAIR, KD):
                act.activation(h_hi[:, k, :], oT[:, k, :], ACT.Copy).then_inc(sp_s["att_hi"], 1)
            for slot in range(2):
                weights_hi(slot, 0)
            for j in range(NPAIR):
                act.wait_ge(s["y_gated"], j + 1)
                act.activation(h_hi[:, j, :], oT[:, j, :], ACT.Copy).then_inc(sp_s["h_hi"], 1)
            for k in range(KD):
                weights_hi(k % 2, k // 2 + 1)
                act.wait_ge(added[k % 2], k // 2 + 1 + FREE)
                square(1, k)
            norm_root(1)
            for k in range(KD):
                act.wait_ge(ns["scaled"], KD + k + 1)
                act.activation(h_hi[:, k, :], hT[:, k, :], ACT.Copy).then_inc(sp_s["h_hi"], 1)
            act.wait_ge(ns["scaled"], 2 * KD)
            for gi, (f0, fn) in enumerate(GROUPS):
                with act.Fori(0, fn // 2) as i:
                    for b in range(2):
                        f = 2 * i + (f0 + b)
                        n = 2 * i + (b + first_unit(f0))
                        act.wait_ge(wt["used"][0], n + 1 + FREE)
                        act.wait_ge(g_split[b], i + f0 // 2 + FREE)
                        act.activation(ga[b], ps[2 * b], ACT.Identity, bias=col("cb", f), scale=col("cw1", f))\
                           .then_inc(fs["scaled"], 1)
                        weights_hi(0, n + 1)
                        act.wait_ge(fs["c2"], f + 1)
                        act.activation(ga[b], ga[b], ACT.Gelu).then_inc(fs["gelu"], 1)
                        weights_hi(1, n + 1)
                        act.wait_ge(gu_done[b], i + (f0 // 2 + 1) + FREE)
                        act.activation(g_hi[:, bass.ds(2 * i + b, 1), :].rearrange("p o t -> p (o t)"), ga[b], ACT.Copy)\
                           .then_inc(fs["g_hi"], 1)
                if gi < len(GROUPS) - 1:
                    with act.Fori(0, KD // 2) as i:
                        for slot in range(2):
                            weights_hi(slot, i + (first_unit(f0) + fn + 1))
                else:
                    for k in range(KD):
                        if k < KD - 2:
                            weights_hi(k % 2, first_unit(f0) + fn + 1 + k // 2)
                        act.wait_ge(added[k % 2], KD // 2 * len(GROUPS) + k // 2 + 1 + FREE)
                        square(2, k)
            norm_root(2)

        @block.gpsimd
        def _(pool):
            for z in range(2):
                v = L[z].rearrange("p (c t) -> p c t", t=CP)
                pool.wait_ge(ns["scaled"], KD)
                pool.memset(v[:, :, 0:1] if z == 0 else v[:, :, C:C + 1], 0.0).then_inc(s["pad_zero"], 1)

            for z in range(2):
                pool.memset(TI[z], 0.0).then_inc(s["TI_init"], 1)
            pool.wait_ge(s["TI_init"], 2)
            for z in range(2):
                diag = TI[z].rearrange("p e s t -> p e (s t)")[:, :, 0:C * C:C + 1]
                pool.memset(diag, 1.0).then_inc(s["TI_init"], 1)

            with pool.Fori(0, NPAIR) as j:
                for z in range(2):
                    pool.wait_ge(s["kp_ready"], j + 1)
                    pool.wait_ge(s[f"E{z}_ready"], 2 * j + 2)
                    pool.wait_ge(s["bkt_mm"], 2 * j + z + FREE)
                    pool.tensor_tensor(BK[:, :, 1, :], kT.rearrange("p (c t) -> p c t", t=C), chunked(Ei[z], z, False),
                                       ALU.mult).then_inc(s["k_prod"], 1)
            pool.wait_ge(s["BK_stored"], 16 * 8 * NPAIR + FREE)
            pool.wait_ge(s["v_stored"], 32 * NPAIR + FREE)
            pool.wait_ge(s["G_stored"], 16 * 2 * NPAIR + FREE)
            pool.memset(zero, 0.0).then_inc(s["zero_made"], 1)
            pool.wait_ge(s["zero_made"], 1)
            for at in (0, P + T):
                for g in range(2):
                    pool.dma_start(kk_d[g, :, at:at + P], zero).then_inc(s["z_stored"], 16)
                pool.dma_start(va_d[at:at + P, :], zero).then_inc(s["z_stored"], 16)
            pool.wait_ge(s["sol_row"], C - 1)
            for j in range(NPAIR):
                for e in range(2):
                    pool.dma_start(TI_d[0, j, e].rearrange("s (c t) -> c s t", t=C), TI[0][C * j:C * (j + 1), e])\
                        .then_inc(s["TI_stored"], 16)
            pool.wait_ge(s["sol_row"], 2 * (C - 1))
            pool.wait_ge(s["TI_stored"], 16 * 2 * NPAIR)
            pool.wait_ge(s["TI1_stored"], 16 * 2 * NPAIR)
            for k in range(KD):
                pool.dma_start(xT[:, k, :], a["xT"][:, k, :]).then_inc(s["x_again"], 16)

            for k in range(NPAIR, KD):
                pool.wait_ge(sp_s["att_hi"], k - NPAIR + 1)
                pool.tensor_tensor(h_lo[:, k, :], oT[:, k, :], h_hi[:, k, :].bitcast(F32), ALU.subtract)\
                    .then_inc(sp_s["att_lo"], 1)

        @block.vector
        def _(dve):
            tt, ts, stt = dve.tensor_tensor, dve.tensor_scalar, dve.scalar_tensor_tensor

            def low_part(out, x, hi, hi_ready, count, done):
                dve.wait_ge(hi_ready, count)
                tt(out, x, hi.bitcast(F32), ALU.subtract).then_inc(done, 1)

            def weights_lo(slot, n):
                low_part(w_lo[slot][:, :, :], w_raw[slot], w_hi[slot][:, :, :], wt["hi"][slot], n + 1, wt["lo"][slot])

            def add_square(n, k):
                dve.wait_ge(ns["squared"], n * KD + k + 1)
                if k >= 2:
                    dve.wait_ge(ns["summed"], n * (KD - 1) + k - 1)
                tt(acc, acc, sqb[k % 2], ALU.add).then_inc(ns["summed"], 1)

            def normalised(n, gain):
                dve.wait_ge(ns["root"], n + 1)
                dve.reciprocal(rs, rs).then_inc(ns["rstd"], 1)
                dve.wait_ge(ns["rstd"], n + 1)
                for k in range(KD):
                    stt(hT[:, k, :], xT[:, k, :], col(gain, k), rs, ALU.mult, ALU.mult).then_inc(ns["scaled"], 1)
                    if n == 1 and k:
                        low_part(h_lo[:, k - 1, :], hT[:, k - 1, :], h_hi[:, k - 1, :], sp_s["h_hi"], NPAIR + k,
                                 sp_s["h_lo"])
                if n == 1:
                    low_part(h_lo[:, KD - 1, :], hT[:, KD - 1, :], h_hi[:, KD - 1, :], sp_s["h_hi"], NPAIR + KD,
                             sp_s["h_lo"])

            dve.memset(eps[:, 0:1], NORM_EPS).then_inc(s["consts_made"], 1)
            dve.memset(eps[:, 1:2], LNX_EPS).then_inc(s["consts_made"], 1)
            dve.wait_ge(s["consts_loaded"], 16 * NCONST)
            mp, mn = par[:, COLS["mu_prev"]:COLS["mu_prev"] + 14], par[:, COLS["mu_next"]:COLS["mu_next"] + 14]
            ts(c0[:, :], mp, -1.0, 1.0, ALU.mult, ALU.add).then_inc(s["c0_part"], 1)
            dve.wait_ge(s["c0_part"], 1)
            tt(c0[:, :], c0[:, :], mn, ALU.subtract).then_inc(s["consts_made"], 1)
            ka = par[:, COLS["k_a"]:COLS["k_a"] + NPAIR]
            ts(oka[:, :], ka, -1.0, 1.0, ALU.mult, ALU.add).then_inc(s["consts_made"], 1)
            for k in range(1, KD):
                add_square(0, k)
            normalised(0, "ln1")

            for i, dst in enumerate((lora, sgT[:, :])):
                dve.wait_ge(s["p_scaled"], i + 1)
                stt(dst[:, 1:T], ps[i][:, 0:T - 1], col("mu_prev", 12 + i), dst[:, 1:T], ALU.mult, ALU.add)\
                    .then_inc(s["p_shift1"], 1)
                dve.wait_ge(s["p_shift1"], i + 1)
                stt(dst[:, 0:T - 1], ps[i][:, 1:T], col("mu_next", 12 + i), dst[:, 0:T - 1], ALU.mult, ALU.add)\
                    .then_inc(s["p_shifted"], 1)

            with dve.Fori(0, NPAIR) as j:
                def shift(i, dst, slot):
                    m = j + 4 * KRV[i]
                    dve.wait_ge(s["p_scaled"], 3 * j + 3 + i)
                    stt(dst[:, 1:T], ps[slot][:, 0:T - 1], col("mu_prev", m), dst[:, 1:T], ALU.mult, ALU.add)\
                        .then_inc(s["p_shift1"], 1)
                    dve.wait_ge(s["p_shift1"], 3 * j + 3 + i)
                    stt(dst[:, 0:T - 1], ps[slot][:, 1:T], col("mu_next", m), dst[:, 0:T - 1], ALU.mult, ALU.add)\
                        .then_inc(s["p_shifted"], 1)

                shift(0, kT, 2)
                dve.wait_ge(s["p_shifted"], 3 * j + 3)
                ts(kkT, kT, col("k_k", j), None, ALU.mult).then_inc(s["kk_ready"], 1)
                for z in range(2):
                    dve.wait_ge(s[f"sig{z}"], j + 1)
                    order = slice(None) if z == 0 else slice(None, None, -1)
                    dve.tensor_tensor_scan(L[z][:, order], reset[:, z, order], L[z][:, order], 0.0, ALU.mult, ALU.add)\
                        .then_inc(s[f"L{z}_ready"], 1)
                dve.wait_ge(s["a_ready"], j + 1)
                dve.wait_ge(s["kk_ready"], j + 1)
                ts(tpT, aT, col("k_a", j), oka[:, bass.ds(j, 1)], ALU.mult, ALU.add).then_inc(s["ka_fac"], 1)
                dve.wait_ge(s["ka_fac"], j + 1)
                tt(kT, kT, tpT, ALU.mult).then_inc(s["kp_ready"], 1)
                shift(1, rT, 3)
                dve.wait_ge(s["kp_ready"], j + 1)
                dve.wait_ge(s["p_shifted"], 3 * j + 4)
                stt(tpT, rT, col("r_k", j), kT, ALU.mult, ALU.mult).then_inc(s["bon_in"], 1)
                dve.wait_ge(s["nrm_ready"], j + 1)
                ts(sqT, sqT, L2_EPS, None, ALU.max).then_inc(s["nrm_max"], 1)
                dve.wait_ge(s["nrm_max"], j + 1)
                dve.reciprocal(sqT, sqT).then_inc(s["nrm_rec"], 1)
                dve.wait_ge(s["nrm_rec"], j + 1)
                stt(kkT, kkT, -1.0, sqT, ALU.mult, ALU.mult).then_inc(s["nk_ready"], 1)
                dve.wait_ge(s["nk_ready"], j + 1)
                stt(bT, kkT, -1.0, aT, ALU.mult, ALU.mult).then_inc(s["b_ready"], 1)
                dve.wait_ge(s["b_ready"], j + 1)
                by_chunk = lambda x: x.rearrange("p (c t) -> p c t", t=C)
                for z in range(2):
                    dve.wait_ge(s[f"E{z}_ready"], 2 * j + 2)
                    last = E[z].rearrange("p (c t) -> p c t", t=CP)[:, :, (C if z == 0 else 0)]
                    dve.tensor_copy(PC[:, z, bass.ds(j, 1), :].rearrange("p o c -> p (o c)"), last)
                    dve.wait_ge(s["AR_stored"], 32 * j + 16 * z + FREE)
                    tt(AR[:, :, 0, :], by_chunk(kkT), chunked(E[z], z, True), ALU.mult)
                    tt(AR[:, :, 1, :], by_chunk(rT), chunked(E[z], z, False), ALU.mult)
                    dve.wait_ge(s["bkt_mm"], 2 * j + z + FREE)
                    tt(BK[:, :, 0, :], by_chunk(bT), chunked(Ei[z], z, False), ALU.mult).then_inc(s["ab_ready"], 1)
                    if z == 0:
                        shift(2, vT, 0)
                        dve.wait_ge(s["p_shifted"], 3 * j + 5)
                        dve.wait_ge(s["bon_mm"], j + 1)
                        tt(bonusT[:, bass.ds(j, 1), :].rearrange("p o t -> p (o t)"), ps[3], vT, ALU.mult)\
                            .then_inc(s["bon_out"], 1)
                    dve.wait_ge(s["gram_mm"], 2 * j + z + 1 + FREE)
                    dve.wait_ge(s["G_stored"], 32 * j + 16 * z + FREE)
                    for b in range(2):
                        tt(G[:, 16 * b:16 * b + 16, :], ps[1 + b].rearrange("p (c t) -> p c t", t=2 * C),
                           gmask[:, z, :].unsqueeze(1).broadcast_to([P, 16, 2 * C]), ALU.mult)\
                            .then_inc(s["G_half"] if b == 0 else s["G_ready"], 1)

            dve.wait_ge(s["TI_init"], 4)
            step = 0
            for z in range(2):
                dve.wait_ge(M_loaded[z], 16 * 2 * NPAIR)
                for n in range(1, C):
                    row = C - 1 - n if z == 0 else n
                    lo = row + 1 if z == 0 else 0
                    m = M[z][:, :, row, lo:lo + n].unsqueeze(2).broadcast_to([P, 2, n, n])
                    known = TI[z][:, :, lo:lo + n, lo:lo + n].rearrange("p e s t -> p e t s")
                    out = prod[:, :, 0:n, 0:n]
                    if step:
                        dve.wait_ge(s["sol_row"], step)
                    tt(out, m, known, ALU.mult).then_inc(s["sol_prod"], 1)
                    step += 1
                    dve.wait_ge(s["sol_prod"], step)
                    dve.tensor_reduce(TI[z][:, :, row, lo:lo + n], out, AX.X, ALU.add).then_inc(s["sol_row"], 1)

            dve.wait_ge(s["BK_stored"], 16 * 8 * NPAIR + FREE)
            dve.wait_ge(s["AR_stored"], 16 * 2 * NPAIR + FREE)
            dve.wait_ge(s["G_stored"], 16 * 2 * NPAIR + FREE)
            dve.wait_ge(s["v_stored"], 32 * NPAIR + FREE)
            dve.wait_ge(s["vat_evicted"], 1)
            dve.wait_ge(s["q_stored"], 16 * 10)
            dve.wait_ge(s["z_stored"], 16 * 6)
            dve.wait_ge(s["q_stored2"], 32)
            for z in range(2):
                dve.memset(S[:, z], 0.0).then_inc(sz[z]["S_new"], 1)
            def logits(i, g, heads):
                blk = 2 * i + g
                for h in heads:
                    dve.wait_ge(s["sc_mm"], 4 * blk + h + 1)
                    stt(Lg[:, h, :], nd, slope[:, GH * g + h:GH * g + h + 1], banks[:, 4 + h % 2, 0:BAND],
                        ALU.mult, ALU.add).then_inc(s["sc_out"], 1)

            def maxima(i, g):
                blk = 2 * i + g
                dve.wait_ge(s["sc_out"], 4 * blk + 4)
                dve.tensor_reduce(nm, Lg, AX.X, ALU.max).then_inc(s["mx_red"], 1)
                dve.wait_ge(s["mx_red"], blk + 1)
                dve.wait_ge(s["s_exp"], blk + FREE)
                tt(mx, nm, sink[:, GH * g:GH * g + GH], ALU.max).then_inc(s["mx_sink"], 1)
                dve.wait_ge(s["mx_sink"], 2 * blk + 1)
                ts(nm, mx, -1.0, None, ALU.mult).then_inc(s["nm_ready"], 1)
                dve.wait_ge(s["nm_ready"], blk + 1)
                tt(mx, sink[:, GH * g:GH * g + GH], mx, ALU.subtract).then_inc(s["mx_sink"], 1)

            def normalise(i, g):
                blk = 2 * i + g
                dve.wait_ge(s["p_exp"], 4 * blk + 4 + FREE)
                dve.wait_ge(s["s_exp"], blk + 1 + FREE)
                tt(rsum, rsum, es, ALU.add).then_inc(s["sum_all"], 1)
                dve.wait_ge(s["sum_all"], blk + 1)
                dve.reciprocal(rinv, rsum).then_inc(s["inv_ready"], 1)
                dve.wait_ge(s["inv_ready"], blk + 1)
                tt(Pr, Pr, rinv.unsqueeze(2).broadcast_to([P, GH, BAND]), ALU.mult).then_inc(s["p_norm"], 1)

            heads = lambda x: x.rearrange("p (h n) -> p h n", n=HD)

            def y_centre(m, r, slot):
                dve.wait_ge(y_full[slot], 16 * r)
                tt(ysum, yin[slot][:, 0], yin[slot][:, 1], ALU.add).then_inc(yin_used[slot], 1)
                dve.wait_ge(yin_used[slot], r + FREE)
                dve.tensor_reduce(stat[:, 0], heads(ysum), AX.X, ALU.add).then_inc(s["y_summed"], 1)
                dve.wait_ge(s["y_summed"], m + 1)
                ts(stat[:, 0], stat[:, 0], 1.0 / HD, None, ALU.mult).then_inc(s["y_mean"], 1)
                dve.wait_ge(s["y_mean"], m + 1)
                dve.wait_ge(s["y_normed"], m + FREE)
                tt(heads(ycen), heads(ysum), stat[:, 0].unsqueeze(2).broadcast_to([P, AH, HD]), ALU.subtract)\
                    .then_inc(s["y_cent"], 1)

            def y_variance(m):
                dve.wait_ge(s["y_sq"], m + 1)
                dve.tensor_reduce(stat[:, 1], heads(ysq), AX.X, ALU.add).then_inc(s["y_var"], 1)

            def y_normalise(m, tile):
                dve.wait_ge(s["y_sd"], m + 1)
                dve.reciprocal(stat[:, 3], stat[:, 2]).then_inc(s["y_inv"], 1)
                dve.wait_ge(s["y_inv"], m + 1)
                by_head = lambda x: x.rearrange("p (j e) c -> p j e c", e=2)
                tt(yn[:, :, bass.ds(tile, 1), :].rearrange("p j o (e c) -> p j (o e) c", e=2), by_head(heads(ycen)),
                   by_head(stat[:, 3].unsqueeze(2).broadcast_to([P, AH, HD])), ALU.mult).then_inc(s["y_normed"], 1)

            for first, last in ((0, YT), (YT, NC // 4)):
                with dve.Fori(first, last) as i:
                    for q in range(4):
                        slot, cc, g = q // 2, q % 2, q // 2
                        n = 4 * i + q
                        dve.wait_ge(sz[0]["X_mm"], n + 1)
                        dve.tensor_copy(Xs[:, 0], banks[:, 0, 0:256]).then_inc(sz[0]["X_out"], 1)
                        if cc == 0:
                            dve.wait_ge(s["p_exp"], 8 * i + 4 * g + FREE)
                            logits(i, g, (0, 1))
                        else:
                            normalise(i, g)
                        if first and cc == 1:
                            y_variance(2 * i + (slot - 2 * YT))
                        for z in range(2):
                            c2 = cc if z == 0 else 1 - cc
                            dve.wait_ge(sz[z]["U_mm"], n + 1)
                            dve.tensor_copy(UV[slot][0:C, z, c2].rearrange("p a b -> p (a b)"),
                                            banks[0:C, 2 + z, 0:256]).then_inc(sz[z]["U_e0"], 1)
                        if cc == 0:
                            logits(i, g, (2, 3))
                            maxima(i, g)
                        for z in range(2):
                            c = n if z == 0 else (i * -4 + (NC - 1 - q))
                            dve.wait_ge(sz[z]["S_mm"], n + 1)
                            tt(St[:, z], S[:, z], banks[:, 2 + z, 256:512].rearrange("p (j i) -> p j i", j=NPAIR), ALU.add)\
                                .then_inc(sz[z]["S_add"], 1)
                            dve.wait_ge(sz[z]["S_add"], n + 1 + FREE)
                            tt(S[:, z], St[:, z], PC[:, z, :, bass.ds(c, 1)].broadcast_to([P, NPAIR, HD]), ALU.mult)\
                                .then_inc(sz[z]["S_new"], 1)
                        if first and cc == 0:
                            y_centre(2 * i + (slot - 2 * YT), i + (1 - YT), slot)
                        elif first:
                            y_normalise(2 * i + (slot - 2 * YT), i + -1 if slot else i * -1 + NC // 4)

            for slot, tile in enumerate((0, NT - 1)):
                m = NT - 2 + slot
                y_centre(m, NT // 2, slot)
                y_variance(m)
                y_normalise(m, tile)
            dve.wait_ge(s["o_out"], 2 * NT + FREE)
            for j in range(NPAIR):
                dve.wait_ge(s["yt_mm"], j + 1)
                ts(ot1, ps[2 * (j % 2)], col("lnx_g", j), col("lnx_b", j), ALU.mult, ALU.add).then_inc(s["y_aff"], 1)
                dve.wait_ge(s["y_aff"], j + 1)
                tt(ot1, ot1, bonusT[:, j, :], ALU.add).then_inc(s["y_bon"], 1)
                dve.wait_ge(s["y_bon"], j + 1)
                dve.wait_ge(s["gt_mm"], j + 1)
                tt(oT[:, j, :], ot1, ps[2 * (j % 2) + 1], ALU.mult).then_inc(s["y_gated"], 1)
                dve.wait_ge(s["y_gated"], j + 1)
                if j:
                    low_part(h_lo[:, j - 1, :], oT[:, j - 1, :], h_hi[:, j - 1, :], sp_s["h_hi"], j, sp_s["h_lo"])
            low_part(h_lo[:, NPAIR - 1, :], oT[:, NPAIR - 1, :], h_hi[:, NPAIR - 1, :], sp_s["h_hi"], NPAIR, sp_s["h_lo"])

            def add_product(n0, i, slot):
                x = xT[:, bass.ds(2 * i + slot, 1), :].rearrange("p o t -> p (o t)")
                dve.wait_ge(wt["used"][slot], i + (n0 + 1) + FREE)
                tt(x, x, ps[slot], ALU.add).then_inc(added[slot], 1)

            def add_and_square(n, n0, split):
                for k in range(KD):
                    add_product(n0, k // 2, k % 2)
                    if k < split:
                        weights_lo(k % 2, n0 + k // 2 + 1)
                    if k >= 2:
                        add_square(n, k - 1)
                add_square(n, KD - 1)

            for slot in range(2):
                weights_lo(slot, 0)
            dve.wait_ge(s["x_again"], 16 * KD)
            add_and_square(1, 0, KD)
            normalised(1, "ln2")
            for gi, (f0, fn) in enumerate(GROUPS):
                with dve.Fori(0, fn // 2) as i:
                    for b in range(2):
                        g = ga[b]
                        f = 2 * i + (f0 + b)
                        n = 2 * i + (b + first_unit(f0))
                        dve.wait_ge(fs["scaled"], f + 1)
                        stt(g[:, 1:T], ps[2 * b][:, 0:T - 1], col("cw0", f), g[:, 1:T], ALU.mult, ALU.add)\
                            .then_inc(fs["c1"], 1)
                        dve.wait_ge(fs["c1"], f + 1)
                        stt(g[:, 0:T - 1], ps[2 * b][:, 1:T], col("cw2", f), g[:, 0:T - 1], ALU.mult, ALU.add)\
                            .then_inc(fs["c2"], 1)
                        weights_lo(0, n + 1)
                        dve.wait_ge(wt["used"][1], n + 1 + FREE)
                        dve.wait_ge(fs["gelu"], f + 1)
                        tt(g, g, ps[2 * b + 1], ALU.mult).then_inc(gu_done[b], 1)
                        weights_lo(1, n + 1)
                        low_part(g_lo[:, bass.ds(2 * i + b, 1), :].rearrange("p o t -> p (o t)"), g,
                                 g_hi[:, bass.ds(2 * i + b, 1), :].rearrange("p o t -> p (o t)"), fs["g_hi"], f + 1,
                                 g_split[b])
                if gi < len(GROUPS) - 1:
                    with dve.Fori(0, KD // 2) as i:
                        for slot in range(2):
                            add_product(first_unit(f0) + fn, i, slot)
                            weights_lo(slot, i + (first_unit(f0) + fn + 1))
                else:
                    add_and_square(2, first_unit(f0) + fn, KD - 2)
            normalised(2, "lnf")


INPUTS = {"par": (P, NPAR), "ident": (P, P), "pairones": (P, P), "ones": (P, P), "gmask": (P, 2, 2 * C),
          "reset": (P, 2, TP), "sink": (P, AH), "slope": (P, AH), "negdist": (NT, P, BAND), "xT": (P, KD, T),
          "w_in": (20, P, KD, P), "lora_w": (NPAIR, P, 2 * P), "gate_w": (P, RW), "w_out": (KD, P, KD, P),
          "w_gu": (KF, P, 2, KD, P), "w_down": (KD, P, KF, P)}


def shape_constants():
    f = np.float32
    t = np.arange(C)
    gm = np.zeros((2, 2, C, 2, 2, C), f)
    sv, tv = t[:, None], t[None, :]
    for z, (strict, loose) in enumerate(((sv < tv, sv <= tv), (sv > tv, sv >= tv))):
        gm[:, :, :, z, 0] = strict
        gm[:, :, :, z, 1] = loose
    reset = np.ones((P, 2, NC, CP), f)
    reset[:, 0, :, 0] = 0
    reset[:, 1, :, C] = 0
    q, k = np.arange(P)[:, None], np.arange(BAND)[None, :] - P
    dist = np.abs(k - q)
    nd = np.empty((NT, P, BAND), f)
    for n in range(NT):
        ok = (dist <= P) & (n * P + k >= 0) & (n * P + k < T)
        nd[n] = np.where(ok, -dist, -1e33)
    slopes = (2.0 ** (-8.0 * np.arange(1, AH + 1) / AH)).astype(f)
    return {"ident": np.eye(P, dtype=f), "pairones": np.kron(np.eye(2), np.ones((HD, HD))).astype(f),
            "ones": np.ones((P, P), f), "gmask": gm.reshape(P, 2, 2 * C), "reset": reset.reshape(P, 2, TP),
            "slope": np.tile(slopes, (P, 1)), "negdist": nd}


def tiles(w):
    k, m = w.shape
    return np.ascontiguousarray(w.reshape(k // P, P, m // P, P).transpose(2, 1, 0, 3))


def kernel(**inputs):
    import concourse.bacc as bacc
    from concourse.bass_utils import run_bass_kernel_spmd

    v = {k: np.asarray(x) for k, x in inputs.items()}
    arrays = shape_constants()
    named = {"mu_prev": v["shift_mu_prev"], "mu_next": v["shift_mu_next"], "w0": v["decay_w0"], "a0": v["iclr_a0"],
             "k_k": v["k_k"], "k_a": v["k_a"], "r_k": v["r_k"], "lnx_g": v["lnx_g"], "lnx_b": v["lnx_b"],
             "ln1": v["ln1_g"], "ln2": v["ln2_g"], "lnf": v["lnf_g"], "cw0": v["ffn_conv_w"][0, 0],
             "cw1": v["ffn_conv_w"][0, 1], "cw2": v["ffn_conv_w"][0, 2], "cb": v["ffn_conv_b"]}
    arrays["par"] = np.ascontiguousarray(np.concatenate([named[n].reshape(-1, P) for n in COLS]).T)
    arrays["sink"] = np.ascontiguousarray(np.broadcast_to(v["attn_sink"][0], (P, AH)))
    arrays["xT"] = np.ascontiguousarray(v["x"][0].reshape(T, KD, P).transpose(2, 1, 0))
    w_in = tiles(v["w_in"][0])
    order = [12, 13] + [4 * i + j for j in range(NPAIR) for i in KRV] + list(range(14, 20))
    arrays["w_in"] = np.ascontiguousarray(w_in[order])
    lora = np.zeros((NPAIR, P, 2 * P), np.float32)
    w2 = v["decay_w2"][0].reshape(2, HD, NPAIR, P)
    lora[:, 0:HD, 0:P], lora[:, 0:HD, P:] = w2[0].transpose(1, 0, 2), w2[1].transpose(1, 0, 2)
    lora[:, HD:, 0:P] = v["iclr_a2"][0].reshape(HD, NPAIR, P).transpose(1, 0, 2)
    arrays["lora_w"] = lora
    arrays["gate_w"] = np.ascontiguousarray(v["gate_g2"][0])
    arrays["w_out"] = tiles(v["w_out"][0])
    arrays["w_gu"] = np.ascontiguousarray(np.stack([tiles(v["ffn_w_gate"][0]), tiles(v["ffn_w_up"][0])], axis=2))
    arrays["w_down"] = tiles(v["ffn_w_down"][0])

    nc = bacc.Bacc("TRN2", target_bir_lowering=False, num_devices=1)
    args = {n: nc.dram_tensor(f"in_{n}", shape, F32, kind="ExternalInput").ap() for n, shape in INPUTS.items()}
    args["out"] = nc.dram_tensor("out_y", (P, KD, T), F32, kind="ExternalOutput").ap()
    hymba_block(nc, args)
    r = run_bass_kernel_spmd(nc, [{f"in_{n}": arrays[n] for n in INPUTS}], core_ids=[0])
    y = r.results[0]["out_y"]
    return np.ascontiguousarray(np.asarray(y).transpose(2, 1, 0).reshape(1, T, D))
```
